# Optimizing a Trainium2 kernel written in Bass

```python
import math
import jax, jax.numpy as jnp
from jax import lax
import numpy as np

D_MODEL = 1024
BATCH = 1
SEQ = 1024
DEPTH = 1
DEC_BATCH = 1
DEC_SEQ = 32
PAST_LEN = 2048

CHUNK = 64
Q_BLOCK = 128
EPS = 1e-6
SB_HEADS = 8
SB_DIM = 64
SB_W = SB_HEADS * SB_DIM
MLA_HEADS = 8
MLA_NOPE = 64
MLA_ROPE = 32
MLA_V = 64
Q_RANK = 384
KV_RANK = 256
ROPE_THETA = 10000.0
MLA_W = MLA_HEADS * MLA_V
MIX_W = SB_W + MLA_W
SPLITS = (SB_W, 2 * SB_W, 3 * SB_W, 3 * SB_W + Q_RANK, 3 * SB_W + Q_RANK + KV_RANK)
IN_COLS = 3 * SB_W + Q_RANK + KV_RANK + MLA_ROPE
N_GROUPS = 4
EXP_PER_GROUP = 8
N_EXPERTS = N_GROUPS * EXP_PER_GROUP
TOP_K = 2
D_EXPERT = 256

kernel_name = 'streaming_hybrid_sb_mla_hmoe'

def rmsnorm(x, g):
    xf = x.astype(jnp.float32)
    y = xf * lax.rsqrt(jnp.mean(xf * xf, axis=-1, keepdims=True) + EPS)
    return (y * g.astype(jnp.float32)).astype(x.dtype)

def modulate(h, shift, scale):
    return h * (1 + scale[:, None, :]) + shift[:, None, :]

def rope_tables(pos):
    inv = ROPE_THETA ** (-jnp.arange(0, MLA_ROPE, 2, dtype=jnp.float32) / MLA_ROPE)
    ang = pos.astype(jnp.float32)[:, None] * inv[None, :]
    return jnp.cos(ang), jnp.sin(ang)

def rope(x, cos, sin):
    x1, x2 = jnp.split(x, 2, axis=-1)
    cos = cos.astype(x.dtype)
    sin = sin.astype(x.dtype)
    return jnp.concatenate([x1 * cos - x2 * sin, x1 * sin + x2 * cos], axis=-1)

def sb_attend(q, k, v, q_pos, k_pos):
    z = jnp.einsum('bqhd,bkhd->bhqk', q, k, preferred_element_type=jnp.float32) / math.sqrt(SB_DIM)
    allowed = k_pos[None, :] < q_pos[:, None]
    log_beta = jax.nn.log_sigmoid(z)
    log_1m = jnp.where(allowed, jax.nn.log_sigmoid(-z), 0.0)
    suffix = lax.cumsum(log_1m, axis=z.ndim - 1, reverse=True) - log_1m
    w = jnp.where(allowed, jnp.exp(log_beta + suffix), 0.0)
    return jnp.einsum('bhqk,bkhd->bqhd', w.astype(v.dtype), v)

def mla_attend(q, k, v, q_pos, k_pos):
    z = jnp.einsum('bqhd,bkhd->bhqk', q, k, preferred_element_type=jnp.float32) / math.sqrt(MLA_NOPE + MLA_ROPE)
    allowed = (k_pos // CHUNK)[None, :] <= (q_pos // CHUNK)[:, None]
    p = jax.nn.softmax(jnp.where(allowed, z, -1e30), axis=-1)
    return jnp.einsum('bhqk,bkhd->bqhd', p.astype(v.dtype), v)

def query_blocks(fn, q_sb, q_mla, pos):
    B, S = q_sb.shape[:2]
    if S <= Q_BLOCK:
        return fn(q_sb, q_mla, pos)
    nb = S // Q_BLOCK
    def split(a):
        return a.reshape(B, nb, Q_BLOCK, *a.shape[2:]).swapaxes(0, 1)
    out = lax.map(lambda args: fn(*args), (split(q_sb), split(q_mla), pos.reshape(nb, Q_BLOCK)))
    return out.swapaxes(0, 1).reshape(B, S, out.shape[-1])

def hier_moe(h, w_rg, b_rg, w_re, b_re, w_gate, w_up, w_down):
    def per_seq(hs):
        g_logits = jnp.dot(hs, w_rg, preferred_element_type=jnp.float32) + b_rg.astype(jnp.float32)
        g_prob = jax.nn.softmax(g_logits, axis=-1)
        g_sel = jnp.argmax(g_logits, axis=-1)
        p_g = jnp.take_along_axis(g_prob, g_sel[:, None], axis=-1)
        e_logits = jnp.dot(hs, w_re, preferred_element_type=jnp.float32) + b_re.astype(jnp.float32)
        e_logits = e_logits.reshape(hs.shape[0], N_GROUPS, EXP_PER_GROUP)
        e_in = jnp.take_along_axis(e_logits, g_sel[:, None, None], axis=1)[:, 0]
        top_v, top_i = lax.top_k(e_in, TOP_K)
        w2 = jax.nn.softmax(top_v, axis=-1) * p_g
        idx = g_sel[:, None] * EXP_PER_GROUP + top_i
        gates = jnp.einsum('ske,sk->se', jax.nn.one_hot(idx, N_EXPERTS, dtype=jnp.float32), w2)
        a = jnp.einsum('sd,edf->sef', hs, w_gate)
        b = jnp.einsum('sd,edf->sef', hs, w_up)
        act = jax.nn.silu(a) * b * gates[:, :, None].astype(a.dtype)
        return jnp.einsum('sef,efd->sd', act, w_down)
    return lax.map(per_seq, h)

def trunk_layer(x, c, pos, past, w):
    (w_ada, b_ada, g_mix, w_in, g_sb_q, g_sb_k, g_qa, w_qb, g_kva, w_kvb,
     g_mq_nope, g_mk_nope, g_mq_pe, g_mk_pe, w_out, g_ffn,
     w_rg, b_rg, w_re, b_re, w_gate, w_up, w_down) = w
    B, S, _ = x.shape
    mod = jnp.dot(jax.nn.silu(c), w_ada) + b_ada
    sh_a, sc_a, gt_a, sh_m, sc_m, gt_m = jnp.split(mod, 6, axis=-1)

    h = modulate(rmsnorm(x, g_mix), sh_a, sc_a)
    u = jnp.dot(h, w_in)
    q_sb, k_sb, v_sb, q_lat, kv_lat, kpe_raw = jnp.split(u, SPLITS, axis=-1)
    cos, sin = rope_tables(pos)
    q_sb = rmsnorm(q_sb.reshape(B, S, SB_HEADS, SB_DIM), g_sb_q)
    k_sb_new = rmsnorm(k_sb.reshape(B, S, SB_HEADS, SB_DIM), g_sb_k)
    v_sb_new = v_sb.reshape(B, S, SB_HEADS, SB_DIM)
    qm = jnp.dot(rmsnorm(q_lat, g_qa), w_qb).reshape(B, S, MLA_HEADS, MLA_NOPE + MLA_ROPE)
    q_nope = rmsnorm(qm[..., :MLA_NOPE], g_mq_nope)
    q_pe = rope(rmsnorm(qm[..., MLA_NOPE:], g_mq_pe), cos[:, None, :], sin[:, None, :])
    q_mla = jnp.concatenate([q_nope, q_pe], axis=-1)
    ckv_new = rmsnorm(kv_lat, g_kva)
    kpe_new = rope(rmsnorm(kpe_raw, g_mk_pe), cos, sin)

    if past is None:
        k_sb_all, v_sb_all, ckv_all, kpe_all = k_sb_new, v_sb_new, ckv_new, kpe_new
        k_pos = pos
    else:
        pk, pv, pc, pp = past
        k_sb_all = jnp.concatenate([pk, k_sb_new], axis=1)
        v_sb_all = jnp.concatenate([pv, v_sb_new], axis=1)
        ckv_all = jnp.concatenate([pc, ckv_new], axis=1)
        kpe_all = jnp.concatenate([pp, kpe_new], axis=1)
        k_pos = jnp.arange(pk.shape[1] + S, dtype=jnp.int32)
    T = ckv_all.shape[1]
    kv = jnp.dot(ckv_all, w_kvb).reshape(B, T, MLA_HEADS, MLA_NOPE + MLA_V)
    k_nope = rmsnorm(kv[..., :MLA_NOPE], g_mk_nope)
    v_mla = kv[..., MLA_NOPE:]
    k_mla = jnp.concatenate([k_nope, jnp.broadcast_to(kpe_all[:, :, None, :], (B, T, MLA_HEADS, MLA_ROPE))], axis=-1)

    def attend(qs_sb, qs_mla, qp):
        o_sb = sb_attend(qs_sb, k_sb_all, v_sb_all, qp, k_pos)
        o_mla = mla_attend(qs_mla, k_mla, v_mla, qp, k_pos)
        tq = qs_sb.shape[1]
        return jnp.concatenate([o_sb.reshape(B, tq, SB_W), o_mla.reshape(B, tq, MLA_W)], axis=-1)

    o = query_blocks(attend, q_sb, q_mla, pos)
    x = x + gt_a[:, None, :] * jnp.dot(o, w_out)

    h2 = modulate(rmsnorm(x, g_ffn), sh_m, sc_m)
    x = x + gt_m[:, None, :] * hier_moe(h2, w_rg, b_rg, w_re, b_re, w_gate, w_up, w_down)
    return x, (k_sb_new, v_sb_new, ckv_new, kpe_new)

def setup_inputs(seed: int = 0) -> dict:
    key = jax.random.key(seed)
    ks = iter(jax.random.split(key, 48))
    f32 = jnp.float32

    def nrm(shape, scale=1.0):
        return jax.random.normal(next(ks), shape, f32) * scale

    def gain(n):
        return 1.0 + nrm((DEPTH, n), 0.05)

    D = D_MODEL
    return {
        'x_prompt': nrm((BATCH, SEQ, D)),
        'x_sample': nrm((DEC_BATCH, DEC_SEQ, D)),
        'cache_sb_k': nrm((DEPTH, DEC_BATCH, PAST_LEN, SB_HEADS, SB_DIM)),
        'cache_sb_v': nrm((DEPTH, DEC_BATCH, PAST_LEN, SB_HEADS, SB_DIM)),
        'cache_mla_ckv': nrm((DEPTH, DEC_BATCH, PAST_LEN, KV_RANK)),
        'cache_mla_kpe': nrm((DEPTH, DEC_BATCH, PAST_LEN, MLA_ROPE)),
        'c_prompt': nrm((BATCH, D)),
        'c_sample': nrm((DEC_BATCH, D)),
        'w_ada': nrm((DEPTH, D, 6 * D), 0.5 * D ** -0.5),
        'b_ada': nrm((DEPTH, 6 * D), 0.02),
        'g_mix': gain(D),
        'w_in': nrm((DEPTH, D, IN_COLS), D ** -0.5),
        'g_sb_q': gain(SB_DIM),
        'g_sb_k': gain(SB_DIM),
        'g_qa': gain(Q_RANK),
        'w_qb': nrm((DEPTH, Q_RANK, MLA_HEADS * (MLA_NOPE + MLA_ROPE)), Q_RANK ** -0.5),
        'g_kva': gain(KV_RANK),
        'w_kvb': nrm((DEPTH, KV_RANK, MLA_HEADS * (MLA_NOPE + MLA_V)), KV_RANK ** -0.5),
        'g_mq_nope': gain(MLA_NOPE),
        'g_mk_nope': gain(MLA_NOPE),
        'g_mq_pe': gain(MLA_ROPE),
        'g_mk_pe': gain(MLA_ROPE),
        'w_out': nrm((DEPTH, MIX_W, D), MIX_W ** -0.5),
        'g_ffn': gain(D),
        'w_rg': nrm((DEPTH, D, N_GROUPS), D ** -0.5),
        'b_rg': nrm((DEPTH, N_GROUPS), 0.01),
        'w_re': nrm((DEPTH, D, N_EXPERTS), D ** -0.5),
        'b_re': nrm((DEPTH, N_EXPERTS), 0.01),
        'w_gate': nrm((DEPTH, N_EXPERTS, D, D_EXPERT), D ** -0.5),
        'w_up': nrm((DEPTH, N_EXPERTS, D, D_EXPERT), D ** -0.5),
        'w_down': nrm((DEPTH, N_EXPERTS, D_EXPERT, D), D_EXPERT ** -0.5),
    }

def reference(x_prompt, x_sample, cache_sb_k, cache_sb_v, cache_mla_ckv, cache_mla_kpe,
              c_prompt, c_sample, w_ada, b_ada, g_mix, w_in, g_sb_q, g_sb_k, g_qa, w_qb,
              g_kva, w_kvb, g_mq_nope, g_mk_nope, g_mq_pe, g_mk_pe, w_out, g_ffn,
              w_rg, b_rg, w_re, b_re, w_gate, w_up, w_down):
    weights = (w_ada, b_ada, g_mix, w_in, g_sb_q, g_sb_k, g_qa, w_qb, g_kva, w_kvb,
               g_mq_nope, g_mk_nope, g_mq_pe, g_mk_pe, w_out, g_ffn,
               w_rg, b_rg, w_re, b_re, w_gate, w_up, w_down)
    pos_p = jnp.arange(x_prompt.shape[1], dtype=jnp.int32)
    pos_s = cache_sb_k.shape[2] + jnp.arange(x_sample.shape[1], dtype=jnp.int32)
    yp, ys = x_prompt, x_sample
    st_p, st_s = [], []
    for l in range(DEPTH):
        wl = tuple(wt[l] for wt in weights)
        yp, sp = trunk_layer(yp, c_prompt, pos_p, None, wl)
        ys, ss = trunk_layer(ys, c_sample, pos_s,
                             (cache_sb_k[l], cache_sb_v[l], cache_mla_ckv[l], cache_mla_kpe[l]), wl)
        st_p.append(sp)
        st_s.append(ss)
    sb_k_prompt = jnp.stack([s[0] for s in st_p])
    sb_v_prompt = jnp.stack([s[1] for s in st_p])
    ckv_prompt = jnp.stack([s[2] for s in st_p])
    kpe_prompt = jnp.stack([s[3] for s in st_p])
    sb_k_sample = jnp.stack([s[0] for s in st_s])
    sb_v_sample = jnp.stack([s[1] for s in st_s])
    ckv_sample = jnp.stack([s[2] for s in st_s])
    kpe_sample = jnp.stack([s[3] for s in st_s])
    return (yp, ys, sb_k_prompt, sb_v_prompt, ckv_prompt, kpe_prompt,
            sb_k_sample, sb_v_sample, ckv_sample, kpe_sample)


_drawn_inputs = setup_inputs


def setup_inputs(seed=0):
    import zlib

    import numpy as np

    out = dict(_drawn_inputs(seed))
    spreads = {}
    factors = {'cache_sb_k': 5.928,
     'cache_mla_ckv': 5.691,
     'cache_mla_kpe': 8.0,
     'g_sb_q': 8.0,
     'g_qa': 8.0,
     'w_qb': 2.675,
     'g_mq_nope': 8.0,
     'g_mk_nope': 8.0,
     'g_mq_pe': 8.0,
     'g_ffn': 3.109,
     'b_rg': 8.0,
     'b_re': 8.0}
    for name, (base, spread) in spreads.items():
        noise = np.random.default_rng([zlib.crc32(name.encode()), seed]).standard_normal(out[name].shape)
        drawn = base * np.exp(spread * noise) if base else spread * noise
        out[name] = __import__('jax').numpy.asarray(drawn.astype(out[name].dtype))
    for name, factor in factors.items():
        out[name] = (out[name] * factor).astype(out[name].dtype)
    return out
```

```python
from contextlib import ExitStack

import numpy as np

import concourse.bass as bass
from concourse import mybir

F32 = mybir.dt.float32
BF16 = mybir.dt.bfloat16
U32 = mybir.dt.uint32
I32 = mybir.dt.int32
ALU = mybir.AluOpType
ACT = mybir.ActivationFunctionType
AX = mybir.AxisListType

P = 128
D = 1024
KD = D // P
SEQ, DEC, PAST = 1024, 32, 2048
PT = SEQ // P
NT = PT + 1
TOK = SEQ + DEC
SBH, SBD = 8, 64
MH, NOPE, ROPE, MV = 8, 64, 32, 64
MK = NOPE + ROPE
QR, KR = 384, 256
SBW = SBH * SBD
INC = 3 * SBW + QR + KR + ROPE
EPS = 1e-6
NEG = -1e30
NG, EPG, NE, DE = 4, 8, 32, 256
SB_SCALE = SBD ** -0.5
MLA_SCALE = MK ** -0.5
PTILES = PAST // P
SKEYS = PAST + DEC
REGION = 9 * P
PAD = TOK

ROWS = {}
_at = 0
for _n, _w in (("g_sb_q", SBD), ("g_sb_k", SBD), ("g_mq_nope", NOPE), ("g_mk_nope", NOPE), ("g_mq_pe", ROPE),
               ("g_mk_pe", ROPE), ("g_kva", KR), ("g_qa", QR), ("b_rg", NG), ("b_re", NE)):
    ROWS[_n] = (_at, _at + _w)
    _at += _w
ROWW = _at
VEC = {"b_ada": (0, 48), "g_mix": (48, 56), "g_ffn": (56, 64), "c_prompt": (64, 72), "c_sample": (72, 80)}


class Steps:

    def __init__(self, engine, sem):
        self.engine, self.sem, self.base, self.n, self.total = engine, sem, 0, 0, 0

    def __call__(self, ins):
        ins.then_inc(self.sem, 1)
        self.n += 1
        self.engine.wait_ge(self.sem, self.base + self.n)

    def enter(self, turn, per):
        self.base, self.n, self.per = self.total + turn * per, 0, per

    def leave(self, turns):
        assert self.n == self.per, (self.n, self.per)
        self.total += turns * self.per
        self.base, self.n = self.total, 0

    def straight(self):
        self.total += self.n
        self.base, self.n = self.total, 0


class Memory:

    def __init__(self, nc, stack):
        self.nc, self.stack = nc, stack

    def sb(self, name, shape, dt=F32):
        t = self.stack.enter_context(self.nc.sbuf_tensor(name, shape, dt))
        return t

    def ps(self, name, shape, dt=F32):
        return self.stack.enter_context(self.nc.psum_tensor(name, shape, dt))

    def sems(self, names):
        made = [self.nc.alloc_semaphore(n) for n in names.split()]
        USED.extend(made)
        return made


USED = []


def retire_semaphores(nc):
    nc.clear_and_free_semaphores(list(USED))
    USED.clear()
    nc.all_engine_barrier()


def phase_a(nc, io, g):
    with ExitStack() as stack:
        m = Memory(nc, stack)
        WCOLS, WBUFS = 512, 2
        CHUNKS = 6 * D // WCOLS
        CT = WCOLS // P
        vrows = m.sb("vrows", [80, P])
        grow = m.sb("grow", [1, 1024])
        ones1 = m.sb("ones1", [1, P])
        vecT = m.sb("vecT", [P, 80])
        sig = m.sb("sig", [P, 16])
        silu_c = m.sb("silu_c", [P, KD, 2])
        wa = g.values[:, 0:WBUFS * KD * WCOLS].rearrange("p (b k n) -> p b k n", b=WBUFS, n=WCOLS)
        ps_vec = m.ps("ps_vec", [P, 512])
        ps_row = m.ps("ps_row", [P, 1024])
        ps_mod = [m.ps(f"ps_mod{b}", [P, 512]) for b in range(WBUFS)]
        (vec_in, row_in, const_ready, vec_t, vec_done, sig_done, silu_done, row_mm, row_done, mod_mm, mod_done,
         dve_step, w_loaded0, w_loaded1, pool_step) = m.sems(
            "vec_in row_in const_ready vec_t vec_done sig_done silu_done row_mm row_done mod_mm mod_done "
            "dve_step w_loaded0 w_loaded1 pool_step")
        w_loaded = [w_loaded0, w_loaded1]
        block = stack.enter_context(nc.Block())
        w_ada = io["w_ada"].rearrange("(k p) n -> p k n", p=P)

        @block.sync
        def _(sp):
            for name, (a, b) in VEC.items():
                sp.dma_start(vrows[a:b, :], io[name].rearrange("(j p) -> j p", p=P)).then_inc(vec_in, 16)
            for name, (a, b) in ROWS.items():
                sp.dma_start(grow[0:1, a:b], io[name].rearrange("(o n) -> o n", o=1)).then_inc(row_in, 16)
            for b in range(WBUFS):
                sp.dma_start(wa[:, b], w_ada[:, :, b * WCOLS:(b + 1) * WCOLS]).then_inc(w_loaded[b], 16)
            with sp.Fori(1, CHUNKS // WBUFS) as j:
                for b in range(WBUFS):
                    sp.wait_ge(mod_mm, j * WBUFS + (b - WBUFS + 1))
                    sp.dma_start(wa[:, b], w_ada[:, :, bass.ds((j * WBUFS + b) * WCOLS, WCOLS)]
                                 ).then_inc(w_loaded[b], 16)
            sp.dma_start(g.w_in[:], io["w_in"].rearrange("(k p) n -> p k n", p=P)).then_inc(g.w_in_loaded, 16)
            sp.dma_start(g.w_qb[:], io["w_qb"].rearrange("(k p) n -> p k n", p=P)).then_inc(g.w_small_loaded, 16)
            sp.dma_start(g.w_kvb[:], io["w_kvb"].rearrange("(k p) n -> p k n", p=P)).then_inc(g.w_small_loaded, 16)
            sp.dma_start(g.rope[:], io["rope"]).then_inc(g.w_small_loaded, 16)

        @block.gpsimd
        def _(pool):
            step = Steps(pool, pool_step)
            step(nc.gpsimd.memset(g.ident[:], 0.0))
            step(nc.gpsimd.memset(ones1[:], 1.0))
            step(nc.gpsimd.memset(g.mask_sb[:], 0.0))
            step(nc.gpsimd.memset(g.mask_mla[:], 0.0))
            step(nc.gpsimd.memset(g.mask_mla[0:64, 64:P], NEG))
            step(nc.gpsimd.memset(g.tri[:], 1.0))
            step(nc.gpsimd.memset(g.ones[:], 1.0))
            step(nc.gpsimd.memset(g.eps[:], EPS))
            step(nc.gpsimd.affine_select(out=g.ident[:], in_=g.ident[:], compare_op=ALU.not_equal, fill=1.0,
                                         base=0, pattern=[[-1, P]], channel_multiplier=1))
            step(nc.gpsimd.affine_select(out=g.mask_sb[:], in_=g.mask_sb[:], compare_op=ALU.is_gt, fill=NEG,
                                         base=0, pattern=[[-1, P]], channel_multiplier=1))
            step(nc.gpsimd.affine_select(out=g.tri[:], in_=g.tri[:], compare_op=ALU.is_gt, fill=0.0,
                                         base=0, pattern=[[1, P]], channel_multiplier=-1))
            nc.gpsimd.tensor_copy(g.identb[:], g.ident[:]).then_inc(const_ready, 1)

        @block.scalar
        def _(act):
            act.wait_ge(vec_done, 1)
            a = VEC["c_prompt"][0]
            nc.scalar.activation(sig[:], vecT[:, a:a + 16], ACT.Sigmoid).then_inc(sig_done, 1)

        @block.tensor
        def _(pe):
            pe.wait_ge(const_ready, 1)
            pe.wait_ge(vec_in, 16 * len(VEC))
            nc.tensor.transpose(ps_vec[:, 0:80], vrows[:], g.ident[0:80, 0:80]).then_inc(vec_t, 1)
            pe.wait_ge(row_in, 16 * len(ROWS))
            nc.tensor.matmul(ps_row[:, 0:512], lhsT=ones1[:], rhs=grow[0:1, 0:512], start=True, stop=True)
            nc.tensor.matmul(ps_row[:, 512:ROWW], lhsT=ones1[:], rhs=grow[0:1, 512:ROWW], start=True,
                             stop=True).then_inc(row_mm, 1)
            pe.wait_ge(silu_done, 1)

            def chunk(j, b, first):
                pe.wait_ge(w_loaded[b], 16 * j + 16)
                if not first:
                    pe.wait_ge(mod_done, j * WBUFS + (b - WBUFS + 1))
                for t in range(CT):
                    for k in range(KD):
                        last = nc.tensor.matmul(ps_mod[b][:, 2 * t:2 * t + 2], lhsT=wa[:, b, k, t * P:(t + 1) * P],
                                                rhs=silu_c[:, k, :], start=k == 0, stop=k == KD - 1)
                last.then_inc(mod_mm, 1)

            for b in range(WBUFS):
                chunk(0, b, True)
            with pe.Fori(1, CHUNKS // WBUFS) as j:
                for b in range(WBUFS):
                    chunk(j, b, False)

        @block.vector
        def _(dve):
            step = Steps(dve, dve_step)
            dve.wait_ge(vec_t, 1)
            nc.vector.tensor_copy(vecT[:], ps_vec[:, 0:80]).then_inc(vec_done, 1)
            dve.wait_ge(row_mm, 1)
            nc.vector.tensor_copy(g.rows[:], ps_row[:, 0:ROWW]).then_inc(row_done, 1)
            dve.wait_ge(sig_done, 1)
            a = VEC["c_prompt"][0]
            dve.wait_ge(vec_done, 1)
            nc.vector.tensor_tensor(silu_c[:].rearrange("p k b -> p b k"),
                                    vecT[:, a:a + 16].rearrange("p (b k) -> p b k", b=2),
                                    sig[:].rearrange("p (b k) -> p b k", b=2), ALU.mult).then_inc(silu_done, 1)

            def chunk(j, b):
                at = (j * WBUFS + b) * CT
                dve.wait_ge(mod_mm, j * WBUFS + (b + 1))
                nc.vector.tensor_tensor(g.modT[:, bass.ds(at, CT), :],
                                        ps_mod[b][:, 0:2 * CT].rearrange("p (t b) -> p t b", b=2),
                                        vecT[:, bass.ds(at, CT)].unsqueeze(2).broadcast_to([P, CT, 2]),
                                        ALU.add).then_inc(mod_done, 1)

            with dve.Fori(0, CHUNKS // WBUFS) as j:
                for b in range(WBUFS):
                    chunk(j, b)
            dve.wait_ge(mod_done, CHUNKS)
            for out, name, chunk_at in ((g.scale_a, "g_mix", 1), (g.scale_m, "g_ffn", 4)):
                a, b = VEC[name]
                step(nc.vector.tensor_scalar(out[:], g.modT[:, 8 * chunk_at:8 * chunk_at + 8, :], 1.0, None,
                                             ALU.add))
                step(nc.vector.tensor_tensor(out[:], out[:], vecT[:, a:b].unsqueeze(2).broadcast_to([P, KD, 2]),
                                             ALU.mult))


def phase_b(nc, io, g):
    with ExitStack() as stack:
        m = Memory(nc, stack)
        x = m.sb("b_x", [P, D])
        hT = m.sb("b_hT", [P, KD, P])
        sq = m.sb("b_sq", [P, D])
        qk = m.sb("b_qk", [P, 2 * SBH, SBD])
        qlat = m.sb("b_qlat", [P, QR])
        qlatT = m.sb("b_qlatT", [P, QR // P, P])
        ckvT = m.sb("b_ckvT", [P, KR // P, P])
        kpe = m.sb("b_kpe", [P, 2 * ROPE])
        qf = m.sb("b_qf", [P, MH, MK])
        kf = m.sb("b_kf", [P, MH, MK])
        qsT = m.sb("b_qsT", [P, 4, P])
        ksT = m.sb("b_ksT", [P, 4, P])
        qmT = m.sb("b_qmT", [MK, MH, P])
        rot = m.sb("b_rot", [P, MH, ROPE])
        st = m.sb("b_st", [P, 8])
        sth = m.sb("b_sth", [P, 48])
        ckv = g.ckv_new
        U = [m.ps(f"b_U{n}", [P, 512]) for n in range(2)]
        U2 = m.ps("b_U2", [P, 512])
        UL = m.ps("b_UL", [P, 2, 512])
        TA, TB, X = (m.ps(n, [P, 512]) for n in ("b_TA", "b_TB", "b_X"))
        (x_in, xstat, xrms, xrec, xn_done, ht_mm, ht_done, lat_mm, lat_sq, lat_rms, lat_norm, kpe_done,
         latT_mm, latTa_done, latTb_done, q_mm, k_mm, v_mm, qk_evac, qk_sq, v_evac, qk_red, qk_rms, qk_norm,
         qmla_mm, kv_mm, qm_evac, kv_evac, mla_red, mla_rms, mla_norm, r0, r1, r2, r3, r4, r5, e0, e1, e2, e3,
         e4, e5, st_ckv, st_kpe, st_k, st_v, st_qs, st_ks, st_qm, dve_step) = m.sems(
            "x_in xstat xrms xrec xn_done ht_mm ht_done lat_mm lat_sq lat_rms lat_norm kpe_done latT_mm "
            "latTa_done latTb_done q_mm k_mm v_mm qk_evac qk_sq v_evac qk_red qk_rms qk_norm qmla_mm kv_mm "
            "qm_evac kv_evac mla_red mla_rms mla_norm r0 r1 r2 r3 r4 r5 e0 e1 e2 e3 e4 e5 st_ckv st_kpe st_k "
            "st_v st_qs st_ks st_qm b_dve_step")
        block = stack.enter_context(nc.Block())
        row = {n: g.rows[:, a:b] for n, (a, b) in ROWS.items()}

        def last(i):
            return isinstance(i, int) and i == PT

        def width(i):
            return DEC if last(i) else P

        def tiles(engine, body, steps=None):
            body(0)
            if steps:
                per = steps.n
                steps.straight()
            with engine.Fori(1, PT - 1) as i:
                if steps:
                    steps.enter(i - 1, per)
                body(i)
            if steps:
                steps.leave(PT - 2)
            body(PT - 1)
            body(PT)

        @block.sync
        def _(sp):
            sp.dma_start(x[:], io["x_prompt"][0:P, :]).then_inc(x_in, 16)

            def queries_out(i):
                T = width(i)
                sp.wait_ge(e0, i + 1)
                sp.dma_start(g.qs_dram[:, :, bass.ds(i * P, T)].rearrange("a p t -> p a t"),
                             qsT[:, :, 0:T]).then_inc(st_qs, 16)
                sp.wait_ge(e1, i + 1)
                sp.dma_start(g.ks_dram[:, :, bass.ds(i * P, T)].rearrange("a p t -> p a t"),
                             ksT[:, :, 0:T]).then_inc(st_ks, 16)
                sp.wait_ge(e3, i + 1)
                sp.wait_ge(e2, i + 1)
                sp.dma_start(g.qm_dram[:, :, bass.ds(i * P, T)].rearrange("h p t -> p h t"),
                             qmT[:, :, 0:T]).then_inc(st_qm, 16)

            def out(name, i):
                return io[name + "_s"] if last(i) else io[name + "_p"][bass.ds(i * P, P), :]

            def body(i):
                T = width(i)
                if not last(i):
                    sp.wait_ge(ht_mm, i + 1)
                    if last(i + 1):
                        sp.dma_start(x[0:DEC, :], io["x_sample"]).then_inc(x_in, 16)
                    else:
                        sp.dma_start(x[:], io["x_prompt"][bass.ds((i + 1) * P, P), :]).then_inc(x_in, 16)
                sp.wait_ge(kpe_done, i + 1)
                sp.dma_start(out("o_ckv", i), ckv[0:T, :]).then_inc(st_ckv, 16)
                sp.dma_start(out("o_kpe", i), kpe[0:T, ROPE:2 * ROPE]).then_inc(st_kpe, 16)
                if not (isinstance(i, int) and i == 0):
                    queries_out(i - 1)
                sp.wait_ge(qk_norm, i + 1)
                sp.dma_start(out("o_k", i), qk[0:T, SBH:, :].rearrange("p h d -> p (h d)")).then_inc(st_k, 16)
                sp.wait_ge(v_evac, i + 1)
                sp.dma_start(out("o_v", i), g.v_sb[0:T, i, :]).then_inc(st_v, 16)

            tiles(sp, body)
            queries_out(PT)
            for s in (st_ckv, st_kpe, st_v, st_k, st_qs, st_ks, st_qm):
                sp.wait_ge(s, 16 * NT)

        @block.tensor
        def _(pe):
            pe.wait_ge(g.w_in_loaded, 16)
            pe.wait_ge(g.w_small_loaded, 48)

            def transposes(dst, src, w, n, T, sem, wait):
                for s, v in wait:
                    pe.wait_ge(s, v)
                for j in range(n):
                    end = nc.tensor.transpose(dst[0:w, j * P:j * P + T], src(j), g.ident[0:T, 0:T])
                end.then_inc(sem, 1)

            def hT_of(i):
                T = width(i)
                pe.wait_ge(xn_done, i + 1)
                for k in range(KD):
                    end = nc.tensor.transpose(U[k // 4][:, (k % 4) * P:(k % 4) * P + T],
                                               x[0:T, k * P:(k + 1) * P], g.ident[0:T, 0:T])
                end.then_inc(ht_mm, 1)

            def project(dst, c0, c1, T, sem, val=None):
                for k in range(KD):
                    end = nc.tensor.matmul(dst[0:T, 0:c1 - c0], lhsT=hT[:, k, 0:T], rhs=g.w_in[:, k, c0:c1],
                                            start=k == 0, stop=k == KD - 1)
                if sem is not None:
                    end.then_inc(sem, 1)

            def pairs(first_head):
                return lambda j: qk[:, first_head + 2 * j:first_head + 2 * j + 2, :].rearrange("p h d -> p (h d)")

            def back(i, part):
                T = width(i)
                if part == 0:
                    pe.wait_ge(qk_norm, i + 1)
                    transposes(TA, lambda j: pairs(0)(j)[0:T], P, 4, T, r0, [(latTa_done, i + 1)])
                    transposes(TB, lambda j: pairs(SBH)(j)[0:T], P, 4, T, r1, [(kv_evac, i + 1)])
                    pe.wait_ge(mla_norm, i + 1)
                    transposes(X, lambda j: qf[0:T, j, :], MK, 4, T, r2, [(kv_evac, i + 1)])
                elif part == 1:
                    transposes(TA, lambda j: qf[0:T, 4 + j, :], MK, 4, T, r3, [(e0, i + 1)])
                    transposes(TB, lambda j: kf[0:T, j, :], MK, 4, T, r4, [(e1, i + 1)])
                    transposes(X, lambda j: kf[0:T, 4 + j, :], MK, 4, T, r5, [(e2, i + 1)])

            def body(i):
                T, first = width(i), isinstance(i, int) and i == 0
                pe.wait_ge(ht_done, i + 1)
                if not first:
                    pe.wait_ge(qm_evac, i)
                project(UL[:, 0, :], 3 * SBW, 3 * SBW + QR, T, None)
                project(UL[:, 1, :], 3 * SBW + QR, INC, T, lat_mm)
                if not first:
                    back(i - 1, 0)
                project(U[0], 0, SBW, T, q_mm)
                if not first:
                    back(i - 1, 1)
                project(U[1], SBW, 2 * SBW, T, k_mm)
                pe.wait_ge(lat_norm, i + 1)
                if not first:
                    pe.wait_ge(e3, i)
                    pe.wait_ge(e4, i)
                for j in range(QR // P):
                    nc.tensor.transpose(TA[:, j * P:j * P + T], qlat[0:T, j * P:(j + 1) * P], g.ident[0:T, 0:T])
                for j in range(KR // P):
                    end = nc.tensor.transpose(TB[:, j * P:j * P + T], ckv[0:T, j * P:(j + 1) * P],
                                               g.ident[0:T, 0:T])
                end.then_inc(latT_mm, 1)
                if not first:
                    pe.wait_ge(v_evac, i)
                project(U2, 2 * SBW, 3 * SBW, T, v_mm)
                if not last(i):
                    pe.wait_ge(qk_evac, i + 1)
                    hT_of(i + 1)
                pe.wait_ge(latTa_done, i + 1)
                pe.wait_ge(latTb_done, i + 1)
                pe.wait_ge(kpe_done, i + 1)
                for c in range(2):
                    for k in range(QR // P):
                        end = nc.tensor.matmul(UL[0:T, c, 0:QR], lhsT=qlatT[:, k, 0:T],
                                                rhs=g.w_qb[:, k, c * QR:(c + 1) * QR], start=k == 0,
                                                stop=k == QR // P - 1)
                end.then_inc(qmla_mm, 1)
                if not first:
                    pe.wait_ge(e5, i)
                for c, dst in enumerate((X, TB)):
                    for k in range(KR // P):
                        end = nc.tensor.matmul(dst[0:T, :], lhsT=ckvT[:, k, 0:T],
                                                rhs=g.w_kvb[:, k, c * 512:(c + 1) * 512], start=k == 0,
                                                stop=k == KR // P - 1)
                end.then_inc(kv_mm, 1)

            hT_of(0)
            tiles(pe, body)
            back(PT, 0)
            back(PT, 1)

        @block.scalar
        def _(act):
            def x_stats(i):
                T = width(i)
                act.wait_ge(x_in, 16 * i + 16)
                nc.scalar.activation(sq[0:T, :], x[0:T, :], ACT.Square, scale=D ** -0.5,
                                     accum_out=st[0:T, 0:1]).then_inc(xstat, 1)
                act.wait_ge(xstat, i + 1)
                nc.scalar.activation(st[0:T, 1:2], st[0:T, 0:1], ACT.Sqrt, bias=g.eps[0:T]).then_inc(xrms, 1)

            def back(i):
                T = width(i)
                cols = bass.ds(i * P, T)
                act.wait_ge(r1, i + 1)
                if not (isinstance(i, int) and i == 0):
                    act.wait_ge(st_ks, 16 * i)
                nc.scalar.activation(ksT[:, :, 0:T], TB[:, :].rearrange("p (j t) -> p j t", t=P)[:, :, 0:T],
                                     ACT.Copy).then_inc(e1, 1)
                act.wait_ge(r2, i + 1)
                if not (isinstance(i, int) and i == 0):
                    act.wait_ge(st_qm, 16 * i)
                nc.scalar.activation(qmT[:, 0:4, 0:T], X[0:MK, :].rearrange("p (j t) -> p j t", t=P)[:, :, 0:T],
                                     ACT.Copy).then_inc(e2, 1)
                act.wait_ge(r4, i + 1)
                nc.scalar.activation(g.kT_m[:, 0:4, cols],
                                     TB[0:MK, :].rearrange("p (j t) -> p j t", t=P)[:, :, 0:T],
                                     ACT.Copy).then_inc(e4, 1)
                act.wait_ge(r5, i + 1)
                nc.scalar.activation(g.kT_m[:, 4:8, cols],
                                     X[0:MK, :].rearrange("p (j t) -> p j t", t=P)[:, :, 0:T],
                                     ACT.Copy).then_inc(e5, 1)

            def body(i):
                T, first = width(i), isinstance(i, int) and i == 0
                act.wait_ge(lat_mm, i + 1)
                nc.scalar.activation(sq[0:T, 0:QR], UL[0:T, 0, 0:QR], ACT.Square, scale=QR ** -0.5,
                                     accum_out=st[0:T, 2:3])
                nc.scalar.activation(sq[0:T, QR:QR + KR], UL[0:T, 1, 0:KR], ACT.Square, scale=KR ** -0.5,
                                     accum_out=st[0:T, 3:4])
                nc.scalar.activation(sq[0:T, QR + KR:QR + KR + ROPE], UL[0:T, 1, KR:KR + ROPE], ACT.Square,
                                     scale=ROPE ** -0.5, accum_out=st[0:T, 4:5]).then_inc(lat_sq, 1)
                act.wait_ge(lat_sq, i + 1)
                nc.scalar.activation(st[0:T, 5:8], st[0:T, 2:5], ACT.Sqrt, bias=g.eps[0:T]).then_inc(lat_rms, 1)
                if not first:
                    back(i - 1)
                if not first:
                    act.wait_ge(st_k, 16 * i)
                act.wait_ge(q_mm, i + 1)
                nc.scalar.activation(qk[0:T, 0:SBH, :], U[0][0:T, :].rearrange("p (h d) -> p h d", d=SBD), ACT.Copy)
                act.wait_ge(k_mm, i + 1)
                nc.scalar.activation(qk[0:T, SBH:, :], U[1][0:T, :].rearrange("p (h d) -> p h d", d=SBD),
                                     ACT.Copy).then_inc(qk_evac, 1)
                act.wait_ge(qk_evac, i + 1)
                nc.scalar.activation(sq[0:T, :], qk[0:T, :, :].rearrange("p h d -> p (h d)"), ACT.Square,
                                     scale=SBD ** -0.5).then_inc(qk_sq, 1)
                act.wait_ge(latT_mm, i + 1)
                nc.scalar.activation(ckvT[:, :, 0:T], TB[:, 0:KR].rearrange("p (j t) -> p j t", t=P)[:, :, 0:T],
                                     ACT.Copy).then_inc(latTb_done, 1)
                act.wait_ge(qk_red, i + 1)
                nc.scalar.activation(sth[0:T, 16:32], sth[0:T, 0:16], ACT.Sqrt, bias=g.eps[0:T]
                                     ).then_inc(qk_rms, 1)
                if not last(i):
                    x_stats(i + 1)
                act.wait_ge(v_mm, i + 1)
                nc.scalar.activation(g.v_sb[0:T, i, :], U2[0:T, :], ACT.Copy).then_inc(v_evac, 1)
                act.wait_ge(qmla_mm, i + 1)
                nc.scalar.activation(qf[0:T, :, :].rearrange("p h d -> p (h d)").rearrange("p (c n) -> p c n", c=2),
                                     UL[0:T, :, 0:QR], ACT.Copy).then_inc(qm_evac, 1)
                act.wait_ge(kv_mm, i + 1)
                for c, src in enumerate((X, TB)):
                    heads = src[0:T, :].rearrange("p (h n) -> p h n", n=NOPE + MV)
                    nc.scalar.activation(kf[0:T, 4 * c:4 * c + 4, 0:NOPE], heads[:, :, 0:NOPE], ACT.Copy)
                    end = nc.scalar.activation(
                        g.v_m[0:T, i, c * 256:(c + 1) * 256].rearrange("p (h n) -> p h n", n=MV),
                        heads[:, :, NOPE:], ACT.Copy)
                end.then_inc(kv_evac, 1)
                act.wait_ge(mla_red, i + 1)
                nc.scalar.activation(sth[0:T, 24:48], sth[0:T, 0:24], ACT.Sqrt, bias=g.eps[0:T]
                                     ).then_inc(mla_rms, 1)

            x_stats(0)
            tiles(act, body)
            back(PT)

        @block.vector
        def _(dve):
            step = Steps(dve, dve_step)
            rope_c = lambda i, T: g.rope[0:T, i, 0:ROPE]
            rope_s = lambda i, T: g.rope[0:T, i, ROPE:2 * ROPE]

            def xn_of(i):
                T = width(i)
                dve.wait_ge(xrms, i + 1)
                nc.vector.reciprocal(st[0:T, 0:1], st[0:T, 1:2]).then_inc(xrec, 1)
                dve.wait_ge(xrec, i + 1)
                nc.vector.tensor_scalar(x[0:T, :], x[0:T, :], st[0:T, 0:1], None, ALU.mult).then_inc(xn_done, 1)

            def hT_of(i):
                T, b = width(i), 1 if last(i) else 0
                dve.wait_ge(ht_mm, i + 1)
                for k in range(KD):
                    end = nc.vector.tensor_scalar(hT[:, k, 0:T], U[k // 4][:, (k % 4) * P:(k % 4) * P + T],
                                                   g.scale_a[:, k, b:b + 1], g.modT[:, k, b:b + 1],
                                                   ALU.mult, ALU.add)
                end.then_inc(ht_done, 1)

            def back(i, part):
                T = width(i)
                if part == 0:
                    dve.wait_ge(r0, i + 1)
                    if not (isinstance(i, int) and i == 0):
                        dve.wait_ge(st_qs, 16 * i)
                    nc.vector.tensor_copy(qsT[:, :, 0:T], TA[:, :].rearrange("p (j t) -> p j t", t=P)[:, :, 0:T]
                                          ).then_inc(e0, 1)
                else:
                    dve.wait_ge(r3, i + 1)
                    if not (isinstance(i, int) and i == 0):
                        dve.wait_ge(st_qm, 16 * i)
                    nc.vector.tensor_copy(qmT[:, 4:8, 0:T],
                                          TA[0:MK, :].rearrange("p (j t) -> p j t", t=P)[:, :, 0:T]
                                          ).then_inc(e3, 1)

            def spread(ap, heads, width, T):
                return ap.unsqueeze(2).broadcast_to([T, heads, width])

            def body(i):
                T, first = width(i), isinstance(i, int) and i == 0
                dve.wait_ge(lat_rms, i + 1)
                step(nc.vector.reciprocal(st[0:T, 5:8], st[0:T, 5:8]))
                if not first:
                    dve.wait_ge(st_ckv, 16 * i)
                    dve.wait_ge(st_kpe, 16 * i)
                nc.vector.scalar_tensor_tensor(qlat[0:T, :], UL[0:T, 0, 0:QR], st[0:T, 5:6], row["g_qa"][0:T],
                                               ALU.mult, ALU.mult)
                nc.vector.scalar_tensor_tensor(ckv[0:T, :], UL[0:T, 1, 0:KR], st[0:T, 6:7], row["g_kva"][0:T],
                                               ALU.mult, ALU.mult).then_inc(lat_norm, 1)
                step(nc.vector.scalar_tensor_tensor(kpe[0:T, 0:ROPE], UL[0:T, 1, KR:KR + ROPE], st[0:T, 7:8],
                                                    row["g_mk_pe"][0:T], ALU.mult, ALU.mult))
                swapped = kpe[0:T, 0:ROPE].rearrange("p (a b) -> p a b", a=2)[:, ::-1, :]
                nc.vector.tensor_tensor(rot[0:T, 0, :].rearrange("p (a b) -> p a b", a=2), swapped,
                                        rope_s(i, T).rearrange("p (a b) -> p a b", a=2), ALU.mult)
                step(nc.vector.tensor_tensor(rot[0:T, 1, :], kpe[0:T, 0:ROPE], rope_c(i, T), ALU.mult))
                nc.vector.tensor_tensor(kpe[0:T, ROPE:2 * ROPE], rot[0:T, 0, :], rot[0:T, 1, :], ALU.add
                                        ).then_inc(kpe_done, 1)
                if not first:
                    back(i - 1, 0)
                    back(i - 1, 1)
                dve.wait_ge(latT_mm, i + 1)
                nc.vector.tensor_copy(qlatT[:, :, 0:T], TA[:, 0:QR].rearrange("p (j t) -> p j t", t=P)[:, :, 0:T]
                                      ).then_inc(latTa_done, 1)
                dve.wait_ge(qk_sq, i + 1)
                nc.vector.tensor_reduce(sth[0:T, 0:16], sq[0:T, :].rearrange("p (h d) -> p h d", d=SBD), AX.X,
                                        ALU.add).then_inc(qk_red, 1)
                dve.wait_ge(qk_rms, i + 1)
                step(nc.vector.reciprocal(sth[0:T, 16:32], sth[0:T, 16:32]))
                step(nc.vector.tensor_tensor(qk[0:T], qk[0:T], spread(sth[0:T, 16:32], 16, SBD, T), ALU.mult))
                for a, name in ((0, "g_sb_q"), (SBH, "g_sb_k")):
                    end = nc.vector.tensor_tensor(
                        qk[0:T, a:a + SBH, :], qk[0:T, a:a + SBH, :],
                        row[name][0:T].unsqueeze(1).broadcast_to([T, SBH, SBD]), ALU.mult)
                end.then_inc(qk_norm, 1)
                if not last(i):
                    xn_of(i + 1)
                    hT_of(i + 1)
                dve.wait_ge(qm_evac, i + 1)
                step(nc.vector.tensor_tensor(sq[0:T, 0:768], qf[0:T].rearrange("p h d -> p (h d)"),
                                             qf[0:T].rearrange("p h d -> p (h d)"), ALU.mult))
                sqh = sq[0:T, 0:768].rearrange("p (h d) -> p h d", d=MK)
                nc.vector.tensor_reduce(sth[0:T, 0:8], sqh[:, :, 0:NOPE], AX.X, ALU.add)
                step(nc.vector.tensor_reduce(sth[0:T, 16:24], sqh[:, :, NOPE:], AX.X, ALU.add))
                dve.wait_ge(kv_evac, i + 1)
                kn = sq[0:T, 0:512].rearrange("p (h d) -> p h d", d=NOPE)
                step(nc.vector.tensor_tensor(kn, kf[0:T, :, 0:NOPE], kf[0:T, :, 0:NOPE], ALU.mult))
                step(nc.vector.tensor_reduce(sth[0:T, 8:16], kn, AX.X, ALU.add))
                nc.vector.tensor_scalar(sth[0:T, 0:16], sth[0:T, 0:16], 1.0 / NOPE, None, ALU.mult)
                nc.vector.tensor_scalar(sth[0:T, 16:24], sth[0:T, 16:24], 1.0 / ROPE, None, ALU.mult
                                        ).then_inc(mla_red, 1)
                dve.wait_ge(mla_rms, i + 1)
                step(nc.vector.reciprocal(sth[0:T, 24:48], sth[0:T, 24:48]))
                nc.vector.tensor_tensor(qf[0:T, :, 0:NOPE], qf[0:T, :, 0:NOPE],
                                        spread(sth[0:T, 24:32], MH, NOPE, T), ALU.mult)
                nc.vector.tensor_tensor(kf[0:T, :, 0:NOPE], kf[0:T, :, 0:NOPE],
                                        spread(sth[0:T, 32:40], MH, NOPE, T), ALU.mult)
                step(nc.vector.tensor_tensor(qf[0:T, :, NOPE:], qf[0:T, :, NOPE:],
                                             spread(sth[0:T, 40:48], MH, ROPE, T), ALU.mult))
                gain = lambda name, w: row[name][0:T].unsqueeze(1).broadcast_to([T, MH, w])
                nc.vector.tensor_tensor(qf[0:T, :, 0:NOPE], qf[0:T, :, 0:NOPE], gain("g_mq_nope", NOPE), ALU.mult)
                nc.vector.tensor_tensor(kf[0:T, :, 0:NOPE], kf[0:T, :, 0:NOPE], gain("g_mk_nope", NOPE), ALU.mult)
                nc.vector.tensor_copy(kf[0:T, :, NOPE:],
                                      kpe[0:T, ROPE:2 * ROPE].unsqueeze(1).broadcast_to([T, MH, ROPE]))
                step(nc.vector.tensor_tensor(qf[0:T, :, NOPE:], qf[0:T, :, NOPE:], gain("g_mq_pe", ROPE), ALU.mult))
                half = ROPE // 2
                for a, b in ((0, half), (half, 0)):
                    end = nc.vector.tensor_tensor(
                        rot[0:T, :, a:a + half], qf[0:T, :, NOPE + b:NOPE + b + half],
                        rope_s(i, T)[:, a:a + half].unsqueeze(1).broadcast_to([T, MH, half]), ALU.mult)
                step(end)
                step(nc.vector.tensor_tensor(qf[0:T, :, NOPE:], qf[0:T, :, NOPE:],
                                             rope_c(i, T).unsqueeze(1).broadcast_to([T, MH, ROPE]), ALU.mult))
                nc.vector.tensor_tensor(qf[0:T, :, NOPE:], qf[0:T, :, NOPE:], rot[0:T], ALU.add
                                        ).then_inc(mla_norm, 1)

            dve.wait_ge(g.w_small_loaded, 48)
            xn_of(0)
            hT_of(0)
            tiles(dve, body, step)
            back(PT, 0)
            back(PT, 1)


def phase_cd(nc, io, g):
    with ExitStack() as stack:
        m = Memory(nc, stack)
        ROWG = P // DEC
        z = m.sb("c_z", [P, 4, SKEYS])
        v_s = m.sb("c_v", [P, PTILES, SBW])
        ckv_s = m.sb("c_ckv", [P, PTILES, KR])
        work = m.sb("c_work", [P, 4864])
        kc = work[:, 0:1024].rearrange("p (b n) -> p b n", b=2)
        cc = work[:, 1024:1536].rearrange("p (b n) -> p b n", b=2)
        kT4 = work[:, 1536:2560].rearrange("p (b j n) -> p b j n", b=2, j=4)
        kf = work[:, 2560:3328].rearrange("p (h n) -> p h n", h=MH)
        kTm = work[0:MK, 3328:4352].rearrange("p (h n) -> p h n", h=MH)
        sq = work[:, 4352:4864].rearrange("p (h n) -> p h n", h=MH)
        stick = work[:, 0:SKEYS + 1]
        beta = work[:, 2084:2084 + SKEYS]
        pc = m.sb("c_pc", [P, 2, ROPE])
        ccT = m.sb("c_ccT", [P, KR // P, P])
        ms = m.sb("c_ms", [P, 2 * MH])
        qbd = m.sb("c_qbd", [P, 4, 2 * DEC])
        qm = m.sb("c_qm", [MK, MH, DEC])
        ksn = m.sb("c_ksn", [P, 4, DEC])
        wT = m.sb("c_wT", [P, PTILES + 1, P])
        pcn = m.sb("c_pcn", [P, KR])
        pcT = m.sb("c_pcT", [P, KR // P, P])
        sm = m.sb("c_sm", [P, 8])
        o_s = m.sb("c_o", [DEC, D])
        A, B, C, DB, E, F = (m.ps(n, [P, 512]) for n in ("c_A", "c_B", "c_C", "c_D", "c_E", "c_F"))
        (kc0, kc1, cc0, cc1, pc0, pc1, q_in, v_in, ckv_in, z0, t1a, t1b, a_done, b_done, kn_mm, c_done, ms_done,
         rms_done, kn_done, t2, d_done, e_done, z_mm, z_done, masked, dve_step, pool_step, prob, tr, evA, evB,
         pv, o_done, pcn_done, pcT_mm, pcT_done, om, s_done, mx_done, st_o) = m.sems(
            "c_kc0 c_kc1 c_cc0 c_cc1 c_pc0 c_pc1 c_q_in c_v_in c_ckv_in c_zero c_t1a c_t1b c_a c_b c_kn_mm "
            "c_c c_ms c_rms c_kn c_t2 c_d c_e c_z_mm c_z_done c_masked c_dve_step c_pool_step c_prob c_tr c_evA "
            "c_evB c_pv c_o_done c_pcn_done c_pcT_mm c_pcT_done c_om c_s_done c_mx c_st_o")
        kc_in, cc_in, pc_in = (kc0, kc1), (cc0, cc1), (pc0, pc1)
        block = stack.enter_context(nc.Block())
        gain = g.rows[:, slice(*ROWS["g_mk_nope"])]
        w_nope = g.w_kvb[:].rearrange("p k (h n) -> p k h n", n=NOPE + MV)

        def tiles(engine, body, steps=None):
            body(0, 0, 0)
            body(1, 1, 0)
            if steps:
                per = steps.n
                steps.straight()
            with engine.Fori(1, PTILES // 2) as j:
                if steps:
                    steps.enter(j - 1, per)
                body(2 * j, 0, j)
                body(2 * j + 1, 1, j)
            if steps:
                steps.leave(PTILES // 2 - 1)

        def later(t, than=0):
            return not isinstance(t, int) or t > than

        GROUPS = (0, 2, 1, 3)
        BATCHES = [(b * 4, min(4, PTILES + 1 - b * 4)) for b in range((PTILES + 4) // 4)]

        def keys_of(t):
            return P if t < PTILES else DEC

        @block.sync
        def _(sp):
            sp.wait_ge(z0, 1)
            new = slice(SEQ, TOK)
            sp.dma_start(qbd[0:64, :, 0:DEC], g.qs_dram[:, 0:64, new].rearrange("a p t -> p a t")).then_inc(q_in, 16)
            sp.dma_start(qbd[64:P, :, DEC:], g.qs_dram[:, 64:P, new].rearrange("a p t -> p a t")).then_inc(q_in, 16)
            sp.dma_start(qm[:], g.qm_dram[:, :, new].rearrange("h p t -> p h t")).then_inc(q_in, 16)
            sp.dma_start(ksn[:], g.ks_dram[:, :, new].rearrange("a p t -> p a t")).then_inc(q_in, 16)

            def body(t, b, n):
                rows = bass.ds(t * P, P)
                if later(t, 1):
                    sp.wait_ge(t1a, t - 1)
                sp.dma_start(kc[:, b], io["cache_sb_k"][rows, :]).then_inc(kc_in[b], 16)
                if later(t, 1):
                    sp.wait_ge(t1b, t - 1)
                sp.dma_start(cc[:, b], io["cache_mla_ckv"][rows, :]).then_inc(cc_in[b], 16)
                if later(t, 1):
                    sp.wait_ge(kn_done, t - 1)
                sp.dma_start(pc[:, b], io["cache_mla_kpe"][rows, :]).then_inc(pc_in[b], 16)

            tiles(sp, body)
            sp.wait_ge(o_done, 4)
            sp.dma_start(g.o_dram[SEQ:TOK, :], o_s[:]).then_inc(st_o, 16)
            sp.wait_ge(st_o, 16)

        @block.gpsimd
        def _(pool):
            nc.gpsimd.memset(qbd[:], 0.0).then_inc(z0, 1)
            pool.wait_ge(z_done, PTILES + 1)
            nc.gpsimd.memset(stick[:, SKEYS:], 1.0).then_inc(pool_step, 1)
            pool.wait_ge(pool_step, 1)
            for a in range(ROWG):
                if a:
                    pool.wait_ge(masked, a)
                part = z[a * DEC:(a + 1) * DEC, 0:2, PAST:]
                nc.gpsimd.affine_select(out=part, in_=part, compare_op=ALU.is_gt, fill=NEG, base=0,
                                        pattern=[[0, 2], [-1, DEC]], channel_multiplier=1).then_inc(masked, 1)

        @block.tensor
        def _(pe):
            def finish_transposes(t):
                pe.wait_ge(kn_done, t + 1)
                if later(t):
                    pe.wait_ge(d_done, t)
                    pe.wait_ge(e_done, t)
                for c, dst in enumerate((DB, E)):
                    for j in range(4):
                        end = nc.tensor.transpose(dst[0:MK, j * P:(j + 1) * P], kf[:, 4 * c + j, :], g.ident[:])
                end.then_inc(t2, 1)

            def scores(t, keys_sb, keys_m, n):
                if later(t):
                    pe.wait_ge(z_done, t)
                out = F[:, :].rearrange("p (a k) -> p a k", k=P)
                for j in range(4):
                    r = (j % 2) * 2 * DEC
                    nc.tensor.matmul(out[r:r + 2 * DEC, j // 2, 0:n], lhsT=qbd[:, j, :], rhs=keys_sb(j),
                                     start=True, stop=True)
                for h in range(MH):
                    r = (h % ROWG) * DEC
                    end = nc.tensor.matmul(out[r:r + DEC, 2 + h // ROWG, 0:n], lhsT=qm[:, h, :], rhs=keys_m(h),
                                           start=True, stop=True, tile_position=(0, r))
                end.then_inc(z_mm, 1)

            def tile_scores(t, b):
                pe.wait_ge(a_done, t + 1)
                pe.wait_ge(d_done, t + 1)
                pe.wait_ge(e_done, t + 1)
                scores(t, lambda j: kT4[:, b, j, :], lambda h: kTm[:, h, :], P)

            def body(t, b, n):
                pe.wait_ge(kc_in[b], 16 * n + 16)
                if later(t):
                    pe.wait_ge(a_done, t)
                    pe.wait_ge(b_done, t)
                for j in range(4):
                    end = nc.tensor.transpose(A[:, j * P:(j + 1) * P], kc[:, b, j * P:(j + 1) * P], g.ident[:])
                end.then_inc(t1a, 1)
                pe.wait_ge(cc_in[b], 16 * n + 16)
                for j in range(KR // P):
                    end = nc.tensor.transpose(B[:, j * P:(j + 1) * P], cc[:, b, j * P:(j + 1) * P], g.ident[:])
                end.then_inc(t1b, 1)
                if later(t):
                    finish_transposes(t - 1)
                    pe.wait_ge(c_done, t)
                pe.wait_ge(b_done, t + 1)
                for k in range(KR // P):
                    end = nc.tensor.matmul(C[:, :], lhsT=ccT[:, k, :], rhs=w_nope[:, k, :, 0:NOPE],
                                           start=k == 0, stop=k == KR // P - 1)
                end.then_inc(kn_mm, 1)
                if later(t):
                    tile_scores(t - 1, 1 - b)

            pe.wait_ge(q_in, 64)
            tiles(pe, body)
            finish_transposes(PTILES - 1)
            tile_scores(PTILES - 1, 1)
            scores(PTILES, lambda j: ksn[:, j, :], lambda h: g.kT_m[:, h, SEQ:TOK], DEC)

            pe.wait_ge(v_in, 16)
            pe.wait_ge(ckv_in, 16)
            for n, a in enumerate(GROUPS):
                src = stick if a >= 2 else beta
                pe.wait_ge(prob, n + 1)
                for i, (t0, cnt) in enumerate(BATCHES):
                    dst = (A, B)[i % 2]
                    if i % 2 == 0:
                        pe.wait_ge(evA, 3 * n + i // 2) if 3 * n + i // 2 else None
                    else:
                        pe.wait_ge(evB, 2 * n + i // 2) if 2 * n + i // 2 else None
                    for j in range(cnt):
                        k = keys_of(t0 + j)
                        end = nc.tensor.transpose(dst[0:k, j * P:(j + 1) * P],
                                                  src[:, (t0 + j) * P:(t0 + j) * P + k], g.ident[:])
                    end.then_inc(tr, 1)
                pe.wait_ge(evA, 3 * n + 3)
                pe.wait_ge(evB, 2 * n + 2)
                if n:
                    pe.wait_ge(o_done, n)
                for t in range(PTILES + 1):
                    k = keys_of(t)
                    if a < 2:
                        v = v_s[:, t, a * 256:(a + 1) * 256] if t < PTILES else \
                            g.v_sb[0:k, PT, a * 256:(a + 1) * 256]
                    else:
                        v = ckv_s[:, t, :] if t < PTILES else g.ckv_new[0:k, :]
                    end = nc.tensor.matmul(C[:, 0:256], lhsT=wT[0:k, t, :], rhs=v, start=t == 0, stop=t == PTILES)
                end.then_inc(pv, 1)
                if a >= 2:
                    pe.wait_ge(pcn_done, a - 1)
                    for j in range(KR // P):
                        end = nc.tensor.transpose(E[:, j * P:(j + 1) * P], pcn[:, j * P:(j + 1) * P], g.ident[:])
                    end.then_inc(pcT_mm, 1)
                    pe.wait_ge(pcT_done, a - 1)
                    for j in range(ROWG):
                        h = (a - 2) * ROWG + j
                        for k in range(KR // P):
                            end = nc.tensor.matmul(F[0:DEC, j * MV:(j + 1) * MV],
                                                   lhsT=pcT[:, k, j * DEC:(j + 1) * DEC],
                                                   rhs=w_nope[:, k, h, NOPE:], start=k == 0,
                                                   stop=k == KR // P - 1)
                    end.then_inc(om, 1)

        @block.scalar
        def _(act):
            act.dma_start(v_s[:], io["cache_sb_v"].rearrange("(t p) n -> p t n", p=P)).then_inc(v_in, 16)
            act.dma_start(ckv_s[:], io["cache_mla_ckv"].rearrange("(t p) n -> p t n", p=P)).then_inc(ckv_in, 16)

            def evac_keys(t):
                act.wait_ge(t2, t + 1)
                if later(t):
                    act.wait_ge(z_mm, t)
                nc.scalar.activation(kTm[:, 4:8, :], E[0:MK, :].rearrange("p (j t) -> p j t", t=P), ACT.Copy
                                     ).then_inc(e_done, 1)

            def evac_scores(t, n):
                act.wait_ge(z_mm, t + 1)
                nc.scalar.activation(z[:, :, bass.ds(t * P, n)],
                                     F[:, :].rearrange("p (a k) -> p a k", k=P)[:, :, 0:n], ACT.Copy
                                     ).then_inc(z_done, 1)

            def body(t, b, n):
                act.wait_ge(t1b, t + 1)
                if later(t):
                    act.wait_ge(kn_mm, t)
                nc.scalar.activation(ccT[:], B[:, 0:KR].rearrange("p (j t) -> p j t", t=P), ACT.Copy
                                     ).then_inc(b_done, 1)
                if later(t):
                    evac_keys(t - 1)
                act.wait_ge(kn_mm, t + 1)
                nc.scalar.activation(kf[:, :, 0:NOPE], C[:, :].rearrange("p (h n) -> p h n", n=NOPE), ACT.Copy
                                     ).then_inc(c_done, 1)
                act.wait_ge(ms_done, t + 1)
                nc.scalar.activation(ms[:, MH:], ms[:, 0:MH], ACT.Sqrt, bias=g.eps[:], scale=1.0 / NOPE
                                     ).then_inc(rms_done, 1)
                if later(t):
                    evac_scores(t - 1, P)

            tiles(act, body)
            evac_keys(PTILES - 1)
            evac_scores(PTILES - 1, P)
            evac_scores(PTILES, DEC)

            act.wait_ge(masked, ROWG)
            act.wait_ge(pool_step, 1)
            act.wait_ge(z_done, PTILES + 1)
            for n, a in enumerate(GROUPS):
                if a < 2:
                    if n:
                        act.wait_ge(pv, n)
                    nc.scalar.activation(stick[:, 0:SKEYS], z[:, a, :], ACT.Sigmoid, scale=-SB_SCALE
                                         ).then_inc(s_done, 1)
                    nc.scalar.activation(beta[:], z[:, a, :], ACT.Sigmoid, scale=SB_SCALE).then_inc(s_done, 1)
                else:
                    act.wait_ge(mx_done, a - 1)
                    act.wait_ge(prob, n)
                    nc.scalar.activation(stick[:, 0:SKEYS], z[:, a, :], ACT.Exp, bias=sm[:, a:a + 1],
                                         scale=MLA_SCALE, accum_out=sm[:, 2 + a:3 + a]).then_inc(prob, 1)
                for i in (1, 3):
                    t0, cnt = BATCHES[i]
                    act.wait_ge(tr, 5 * n + i + 1)
                    if n:
                        act.wait_ge(pv, n)
                    nc.scalar.activation(wT[:, t0:t0 + cnt, :], B[:, 0:cnt * P].rearrange("p (j t) -> p j t", t=P),
                                         ACT.Copy).then_inc(evB, 1)
                if a >= 2:
                    act.wait_ge(pcT_mm, a - 1)
                    nc.scalar.activation(pcT[:], E[:, 0:KR].rearrange("p (j t) -> p j t", t=P), ACT.Copy
                                         ).then_inc(pcT_done, 1)

        @block.vector
        def _(dve):
            step = Steps(dve, dve_step)

            def evac_keys(t):
                dve.wait_ge(t2, t + 1)
                if later(t):
                    dve.wait_ge(z_mm, t)
                nc.vector.tensor_copy(kTm[:, 0:4, :], DB[0:MK, :].rearrange("p (j t) -> p j t", t=P)
                                      ).then_inc(d_done, 1)

            def body(t, b, n):
                dve.wait_ge(t1a, t + 1)
                if later(t, 1):
                    dve.wait_ge(z_mm, t - 1)
                nc.vector.tensor_copy(kT4[:, b], A[:, :].rearrange("p (j t) -> p j t", t=P)).then_inc(a_done, 1)
                if later(t):
                    evac_keys(t - 1)
                dve.wait_ge(c_done, t + 1)
                step(nc.vector.tensor_tensor(sq[:], kf[:, :, 0:NOPE], kf[:, :, 0:NOPE], ALU.mult))
                nc.vector.tensor_reduce(ms[:, 0:MH], sq[:], AX.X, ALU.add).then_inc(ms_done, 1)
                dve.wait_ge(pc_in[b], 16 * n + 16)
                nc.vector.tensor_copy(kf[:, :, NOPE:], pc[:, b, :].unsqueeze(1).broadcast_to([P, MH, ROPE]))
                dve.wait_ge(rms_done, t + 1)
                step(nc.vector.reciprocal(ms[:, MH:], ms[:, MH:]))
                step(nc.vector.tensor_tensor(kf[:, :, 0:NOPE], kf[:, :, 0:NOPE],
                                             ms[:, MH:].unsqueeze(2).broadcast_to([P, MH, NOPE]), ALU.mult))
                nc.vector.tensor_tensor(kf[:, :, 0:NOPE], kf[:, :, 0:NOPE],
                                        gain.unsqueeze(1).broadcast_to([P, MH, NOPE]), ALU.mult
                                        ).then_inc(kn_done, 1)

            tiles(dve, body, step)
            evac_keys(PTILES - 1)

            dve.wait_ge(z_done, PTILES + 1)
            for a in (2, 3):
                step(nc.vector.tensor_reduce(sm[:, 6:7], z[:, a, :], AX.X, ALU.max))
                nc.vector.tensor_scalar(sm[:, a:a + 1], sm[:, 6:7], -MLA_SCALE, None, ALU.mult
                                        ).then_inc(mx_done, 1)
                dve.wait_ge(mx_done, a - 1)
            sb = 0
            for n, a in enumerate(GROUPS):
                if a < 2:
                    dve.wait_ge(s_done, 2 * sb + 1)
                    back = stick[:, 0:SKEYS][:, ::-1]
                    step(nc.vector.tensor_tensor_scan(back, back, back, 1.0, ALU.mult, ALU.bypass))
                    dve.wait_ge(s_done, 2 * sb + 2)
                    nc.vector.tensor_tensor(beta[:], beta[:], stick[:, 1:], ALU.mult).then_inc(prob, 1)
                    sb += 1
                for i in (0, 2, 4):
                    t0, cnt = BATCHES[i]
                    dve.wait_ge(tr, 5 * n + i + 1)
                    if n:
                        dve.wait_ge(pv, n)
                    k = keys_of(t0)
                    nc.vector.tensor_copy(wT[0:k, t0:t0 + cnt, :],
                                          A[0:k, 0:cnt * P].rearrange("p (j t) -> p j t", t=P)).then_inc(evA, 1)
                dve.wait_ge(pv, n + 1)
                if a < 2:
                    for j in range(ROWG):
                        h = a * ROWG + j
                        end = nc.vector.tensor_copy(o_s[:, h * SBD:(h + 1) * SBD],
                                                    C[j * DEC:(j + 1) * DEC, j * SBD:(j + 1) * SBD])
                    end.then_inc(o_done, 1)
                else:
                    step(nc.vector.reciprocal(sm[:, 2 + a:3 + a], sm[:, 2 + a:3 + a]))
                    nc.vector.tensor_scalar(pcn[:], C[:, 0:256], sm[:, 2 + a:3 + a], None, ALU.mult
                                            ).then_inc(pcn_done, 1)
                    dve.wait_ge(om, a - 1)
                    nc.vector.tensor_copy(o_s[:, SBW + (a - 2) * 256:SBW + (a - 1) * 256], F[0:DEC, 0:256]
                                          ).then_inc(o_done, 1)


def phase_e(nc, io, g, latent):
    with ExitStack() as stack:
        n_ = "m_" if latent else "s_"
        m = Memory(nc, stack)
        UNITS = 2 * PT
        ORDER = list(range(PT))
        HEADS = SBH
        KROWS = MK if latent else P
        q = m.sb(n_ + "q", [KROWS, 2, SEQ])
        keys = None if latent else m.sb(n_ + "keys", [P, SBH // 2, SEQ])
        stick = m.sb(n_ + "stick", [P, 2, SEQ + 1])
        w = m.sb(n_ + "w", [P, 2, SEQ])
        wT = m.sb(n_ + "wT", [P, 2, PT, P])
        o = m.sb(n_ + "o", [P, 2, PT, SBD])
        sm = m.sb(n_ + "sm", [P, 2, 4])
        Z = [m.ps(f"{n_}Z{b}", [P, SEQ]) for b in range(2)]
        TA, TB = (m.ps(n_ + x, [P, 512]) for x in ("TA", "TB"))
        O = [m.ps(f"{n_}O{b}", [P, 512]) for b in range(2)]
        (zero, q0, q1, keys_in, z_mm, z_read, s_done, b_done, w_done, tr_a, tr_b, evA, evB, tr_end, pv, o_done,
         mx_done, dve_step, st_o0, st_o1) = m.sems(" ".join(n_ + x for x in (
             "zero q0 q1 keys_in z_mm z_read s_done b_done w_done tr_a tr_b evA evB tr_end pv o_done mx_done "
             "dve_step st_o0 st_o1").split()))
        q_in, st_o = (q0, q1), (st_o0, st_o1)
        block = stack.enter_context(nc.Block())
        mask = g.mask_mla if latent else g.mask_sb
        values = g.v_m if latent else g.v_sb
        BIG = [t >= 4 for t in ORDER] * 2

        def big_before(u):
            return sum(BIG[:u])

        def unit(p, u):
            return p * UNITS + u, ORDER[u % PT], u // PT

        def first(p, u, n=1):
            return isinstance(p, int) and p == 0 and u < n

        def units(engine, body, finish, steps=None):
            for u in range(UNITS):
                body(0, u)
            if steps:
                per = steps.n
                steps.straight()
            with engine.Fori(1, HEADS // 2) as p:
                if steps:
                    steps.enter(p - 1, per)
                for u in range(UNITS):
                    body(p, u)
            if steps:
                steps.leave(HEADS // 2 - 1)
            finish(HEADS // 2 - 1, UNITS - 1)

        def before(p, u):
            return (p, u - 1) if u else (p - 1, UNITS - 1)

        @block.sync
        def _(sp):
            def load_q(p, hh):
                if latent:
                    sp.dma_start(q[:, hh, :], g.qm_dram[2 * p + hh, :, 0:SEQ]).then_inc(q_in[hh], 16)
                else:
                    r = slice(hh * SBD, (hh + 1) * SBD)
                    sp.dma_start(q[r, hh, :], g.qs_dram[p, r, 0:SEQ]).then_inc(q_in[hh], 16)

            if not latent:
                sp.wait_ge(zero, 3)
                sp.dma_start(keys[:], g.ks_dram[:, :, 0:SEQ].rearrange("a p t -> p a t")).then_inc(keys_in, 16)
            for hh in range(2):
                load_q(0, hh)

            def store(p, hh):
                sp.wait_ge(o_done, p * UNITS + (hh + 1) * PT)
                col = bass.ds((SBW if latent else 0) + (2 * p + hh) * SBD, SBD)
                sp.dma_start(g.o_dram[0:SEQ, col].rearrange("(t p) c -> p t c", p=P), o[:, hh]
                             ).then_inc(st_o[hh], 16)

            with sp.Fori(0, HEADS // 2 - 1) as p:
                for hh in range(2):
                    sp.wait_ge(z_mm, p * UNITS + (hh + 1) * PT)
                    load_q(p + 1, hh)
                    store(p, hh)
            for hh in range(2):
                store(HEADS // 2 - 1, hh)
            for hh in range(2):
                sp.wait_ge(st_o[hh], 16 * (HEADS // 2))

        @block.gpsimd
        def _(pool):
            if not latent:
                nc.gpsimd.memset(q[SBD:P, 0, :], 0.0).then_inc(zero, 1)
                pool.wait_ge(zero, 1)
                nc.gpsimd.memset(q[0:SBD, 1, :], 0.0).then_inc(zero, 1)
                pool.wait_ge(zero, 2)
                nc.gpsimd.memset(stick[:, :, SEQ:], 1.0).then_inc(zero, 1)

        @block.tensor
        def _(pe):
            def finish(p, u):
                n, t, hh = unit(p, u)
                b = u % 2
                pe.wait_ge(w_done, n + 1)
                if not first(p, u):
                    pe.wait_ge(evA, n)
                for j in range(min(4, t + 1)):
                    src = w[:, b, SEQ - (t + 1) * P + j * P:SEQ - (t + 1) * P + (j + 1) * P]
                    end = nc.tensor.transpose(TA[:, j * P:(j + 1) * P], src, g.ident[:])
                end.then_inc(tr_a, 1)
                if BIG[u]:
                    nb = p * (2 * 4) + big_before(u)
                    if not (isinstance(nb, int) and nb == 0):
                        pe.wait_ge(evB, nb)
                    for j in range(4, t + 1):
                        src = w[:, b, SEQ - (t + 1) * P + j * P:SEQ - (t + 1) * P + (j + 1) * P]
                        end = nc.tensor.transpose(TB[:, (j - 4) * P:(j - 3) * P], src, g.ident[:])
                    end.then_inc(tr_b, 1)
                pe.wait_ge(evA, n + 1)
                if not first(p, u, 2):
                    pe.wait_ge(o_done, n - 1)
                col = (2 * p + hh) * SBD
                for j in range(t + 1):
                    if j == 4:
                        pe.wait_ge(evB, nb + 1)
                    end = nc.tensor.matmul(O[b][:, 0:SBD], lhsT=wT[:, b, j, :], rhs=values[:, j, bass.ds(col, SBD)],
                                           start=j == 0, stop=j == t)
                end.then_inc(pv, 1)

            def body(p, u):
                n, t, hh = unit(p, u)
                if u % PT == 0:
                    pe.wait_ge(q_in[hh], 16 * p + 16)
                if not first(p, u, 2):
                    pe.wait_ge(w_done if latent else z_read, n - 1)
                for c in range(0, (t + 1) * P, 512):
                    c1 = min(c + 512, (t + 1) * P)
                    rhs = g.kT_m[:, 2 * p + hh, c:c1] if latent else keys[:, p, c:c1]
                    nc.tensor.matmul(Z[u % 2][:, c:c1], lhsT=q[:, hh, t * P:(t + 1) * P], rhs=rhs, start=True,
                                     stop=c1 < (t + 1) * P)
                nc.tensor.matmul(Z[u % 2][:, t * P:(t + 1) * P], lhsT=g.identb[:], rhs=mask[:], start=False,
                                 stop=True).then_inc(z_mm, 1)
                if not first(p, u):
                    finish(*before(p, u))

            if not latent:
                pe.wait_ge(keys_in, 16)
                pe.wait_ge(zero, 3)
            units(pe, body, finish)

        @block.scalar
        def _(act):
            def finish(p, u):
                n, t, hh = unit(p, u)
                act.wait_ge(tr_a, n + 1)
                if not first(p, u, 2):
                    act.wait_ge(pv, n - 1)
                cnt = min(4, t + 1)
                nc.scalar.activation(wT[:, u % 2, 0:cnt, :], TA[:, 0:cnt * P].rearrange("p (j t) -> p j t", t=P),
                                     ACT.Copy).then_inc(evA, 1)

            def body(p, u):
                n, t, hh = unit(p, u)
                b = u % 2
                if not first(p, u):
                    finish(*before(p, u))
                W = (t + 1) * P
                act.wait_ge(z_mm, n + 1)
                if latent:
                    act.wait_ge(mx_done, n + 1)
                    if not first(p, u, 2):
                        act.wait_ge(pv, n - 1)
                        act.wait_ge(o_done, n - 1)
                    nc.scalar.activation(w[:, b, SEQ - W:], Z[b][:, 0:W], ACT.Exp, bias=sm[:, b, 1:2],
                                         scale=MLA_SCALE, accum_out=sm[:, b, 2:3]).then_inc(w_done, 1)
                else:
                    if not first(p, u, 2):
                        act.wait_ge(w_done, n - 1)
                    nc.scalar.activation(stick[:, b, SEQ - W:SEQ], Z[b][:, 0:W], ACT.Sigmoid, scale=-SB_SCALE
                                         ).then_inc(s_done, 1)
                    if not first(p, u, 2):
                        act.wait_ge(pv, n - 1)
                    nc.scalar.activation(w[:, b, SEQ - W:], Z[b][:, 0:W], ACT.Sigmoid, scale=SB_SCALE
                                         ).then_inc(z_read, 1)

            units(act, body, finish)

        @block.vector
        def _(dve):
            step = Steps(dve, dve_step)

            def evac_b(p, u):
                n, t, hh = unit(p, u)
                if BIG[u]:
                    nb = p * (2 * 4) + big_before(u)
                    dve.wait_ge(tr_b, nb + 1)
                    if not first(p, u, 2):
                        dve.wait_ge(pv, n - 1)
                    nc.vector.tensor_copy(wT[:, u % 2, 4:t + 1, :],
                                          TB[:, 0:(t - 3) * P].rearrange("p (j t) -> p j t", t=P)).then_inc(evB, 1)

            def out(p, u):
                n, t, hh = unit(p, u)
                b = u % 2
                dve.wait_ge(pv, n + 1)
                if u % PT == 0 and not (isinstance(p, int) and p == 0):
                    dve.wait_ge(st_o[hh], 16 * p)
                if latent:
                    step(nc.vector.reciprocal(sm[:, b, 3:4], sm[:, b, 2:3]))
                    nc.vector.tensor_scalar(o[:, hh, t, :], O[b][:, 0:SBD], sm[:, b, 3:4], None, ALU.mult
                                            ).then_inc(o_done, 1)
                else:
                    nc.vector.tensor_copy(o[:, hh, t, :], O[b][:, 0:SBD]).then_inc(o_done, 1)

            def body(p, u):
                n, t, hh = unit(p, u)
                b, W = u % 2, (t + 1) * P
                if latent:
                    dve.wait_ge(z_mm, n + 1)
                    step(nc.vector.tensor_reduce(sm[:, b, 0:1], Z[b][:, 0:W], AX.X, ALU.max))
                    if not first(p, u, 2):
                        dve.wait_ge(w_done, n - 1)
                    nc.vector.tensor_scalar(sm[:, b, 1:2], sm[:, b, 0:1], -MLA_SCALE, None, ALU.mult
                                            ).then_inc(mx_done, 1)
                if not first(p, u):
                    evac_b(*before(p, u))
                if not latent:
                    dve.wait_ge(s_done, n + 1)
                    back = stick[:, b, SEQ - W:SEQ][:, ::-1]
                    step(nc.vector.tensor_tensor_scan(back, back, back, 1.0, ALU.mult, ALU.bypass))
                    dve.wait_ge(z_read, n + 1)
                    nc.vector.tensor_tensor(w[:, b, SEQ - W:], w[:, b, SEQ - W:], stick[:, b, SEQ - W + 1:],
                                            ALU.mult).then_inc(w_done, 1)
                if not first(p, u):
                    out(*before(p, u))

            def finish(p, u):
                evac_b(p, u)
                out(p, u)

            if not latent:
                dve.wait_ge(zero, 3)
            if latent:
                step(nc.vector.memset(sm[:], 0.0))
            units(dve, body, finish, step)


def phase_f(nc, io, g):
    with ExitStack() as stack:
        m = Memory(nc, stack)
        wo = m.sb("f_wo", [P, KD, D])
        wr = m.sb("f_wr", [P, KD, NG + NE])
        rows = m.sb("f_rows", [P, 3, 2, D])
        o = m.sb("f_o", [P, D])
        oT = m.sb("f_oT", [P, KD, P])
        xr = m.sb("f_xr", [P, D])
        h2 = m.sb("f_h2", [P, D])
        h2T = m.sb("f_h2T", [P, KD, P])
        sq = m.sb("f_sq", [P, D])
        st = m.sb("f_st", [P, 3])
        zero = m.sb("f_zero", [1, D])
        LROWS = NE * REGION // P
        rown = m.sb("f_rown", [P, LROWS], I32)
        padt = m.sb("f_padt", [P, LROWS], I32)
        rowf = m.sb("f_rowf", [P, LROWS])
        pad = m.sb("f_pad", [P, LROWS, 2], U32)
        A = m.ps("f_A", [P, D])
        B = m.ps("f_B", [P, D])
        C = m.ps("f_C", [P, D])
        R = m.ps("f_R", [P, 512])
        (w_in, r_in, o_in, x_in, z0, z_out, row_mm, row_done, oT_mm, oT_done, pr_mm, x2_done, ssq, rms, h2_done,
         h2T_mm, h2T_done, rt_mm, rt_done, st_h2, dve_step, pool_step, pad_done) = m.sems(
            "f_w_in f_r_in f_o_in f_x_in f_z0 f_z_out f_row_mm f_row_done f_oT_mm f_oT_done f_pr_mm f_x2_done "
            "f_ssq f_rms f_h2_done f_h2T_mm f_h2T_done f_rt_mm f_rt_done f_st_h2 f_dve_step f_pool_step f_pad_done")
        block = stack.enter_context(nc.Block())
        bias = g.rows[:, ROWS["b_rg"][0]:ROWS["b_re"][1]]

        def last(i):
            return isinstance(i, int) and i == PT

        def width(i):
            return DEC if last(i) else P

        def tiles(engine, body, steps=None):
            body(0)
            if steps:
                per = steps.n
                steps.straight()
            with engine.Fori(1, PT) as i:
                if steps:
                    steps.enter(i - 1, per)
                body(i)
            if steps:
                steps.leave(PT - 1)
            body(PT)

        def later(i):
            return not (isinstance(i, int) and i == 0)

        SPREADS = [(rows[:, 0, b, :], g.modT[:, 16:24, b]) for b in range(2)] + \
                  [(rows[:, 1, b, :], g.scale_m[:, :, b]) for b in range(2)] + \
                  [(rows[:, 2, b, :], g.modT[:, 24:32, b]) for b in range(2)] + \
                  [(g.gate_m[:, b, :], g.modT[:, 40:48, b]) for b in range(2)]

        @block.sync
        def _(sp):
            sp.dma_start(wo[:], io["w_out"].rearrange("(k p) n -> p k n", p=P)).then_inc(w_in, 16)
            sp.dma_start(wr[:, :, 0:NG], io["w_rg"].rearrange("(k p) n -> p k n", p=P)).then_inc(r_in, 16)
            sp.dma_start(wr[:, :, NG:], io["w_re"].rearrange("(k p) n -> p k n", p=P)).then_inc(r_in, 16)
            sp.wait_ge(z0, 1)
            sp.wait_ge(pad_done, 1)
            sp.dma_start(g.h2_dram[PAD:PAD + 1, :], zero[:]).then_inc(z_out, 16)
            sp.dma_start(g.list_dram.rearrange("(p n) o -> p n o", p=P), pad[:]).then_inc(z_out, 16)

            def store(i):
                sp.wait_ge(h2_done, i + 1)
                sp.dma_start(g.h2_dram[bass.ds(i * P, width(i)), :], h2[0:width(i), :]).then_inc(st_h2, 16)

            def body(i):
                T = width(i)
                if later(i):
                    sp.wait_ge(oT_mm, i)
                sp.dma_start(o[0:T, :], g.o_dram[bass.ds(i * P, T), :]).then_inc(o_in, 16)
                if later(i):
                    sp.wait_ge(x2_done, i)
                x = io["x_sample"] if last(i) else io["x_prompt"][bass.ds(i * P, P), :]
                sp.dma_start(xr[0:T, :], x).then_inc(x_in, 16)
                if later(i):
                    store(i - 1)

            tiles(sp, body)
            store(PT)
            sp.wait_ge(st_h2, 16 * NT)
            sp.wait_ge(z_out, 32)

        @block.gpsimd
        def _(pool):
            nc.gpsimd.iota(rown[:], pattern=[[1, LROWS]], base=0, channel_multiplier=LROWS).then_inc(pool_step, 1)
            pool.wait_ge(pool_step, 1)
            nc.gpsimd.iota(padt[:], pattern=[[0, LROWS]], base=PAD, channel_multiplier=0).then_inc(pool_step, 1)
            pool.wait_ge(pool_step, 2)
            nc.gpsimd.memset(zero[:], 0.0).then_inc(z0, 1)

        @block.tensor
        def _(pe):
            for n, (_, col) in enumerate(SPREADS):
                dst = (A, B, C)[n % 3]
                if n >= 3:
                    pe.wait_ge(row_done, n - 2)
                for k in range(KD):
                    end = nc.tensor.transpose(dst[:, k * P:(k + 1) * P], col[:, k:k + 1].broadcast_to([P, P]),
                                              g.ident[:])
                end.then_inc(row_mm, 1)
            pe.wait_ge(row_done, len(SPREADS))

            def finish(i, part):
                T = width(i)
                if part == 0:
                    pe.wait_ge(h2_done, i + 1)
                    if later(i):
                        pe.wait_ge(h2T_done, i)
                    for k in range(KD):
                        end = nc.tensor.transpose(B[:, k * P:k * P + T], h2[0:T, k * P:(k + 1) * P],
                                                  g.ident[0:T, 0:T])
                    end.then_inc(h2T_mm, 1)
                else:
                    pe.wait_ge(h2T_done, i + 1)
                    if later(i):
                        pe.wait_ge(rt_done, i)
                    for k in range(KD):
                        end = nc.tensor.matmul(R[0:T, 0:NG + NE], lhsT=h2T[:, k, 0:T], rhs=wr[:, k, :],
                                               start=k == 0, stop=k == KD - 1)
                    end.then_inc(rt_mm, 1)

            def body(i):
                T = width(i)
                pe.wait_ge(o_in, 16 * i + 16)
                if later(i):
                    pe.wait_ge(oT_done, i)
                for k in range(KD):
                    end = nc.tensor.transpose(A[:, k * P:k * P + T], o[0:T, k * P:(k + 1) * P], g.ident[0:T, 0:T])
                end.then_inc(oT_mm, 1)
                if later(i):
                    finish(i - 1, 0)
                    pe.wait_ge(x2_done, i)
                pe.wait_ge(oT_done, i + 1)
                for c in range(2):
                    for k in range(KD):
                        end = nc.tensor.matmul(C[0:T, c * 512:(c + 1) * 512], lhsT=oT[:, k, 0:T],
                                               rhs=wo[:, k, c * 512:(c + 1) * 512], start=k == 0, stop=k == KD - 1)
                end.then_inc(pr_mm, 1)
                if later(i):
                    finish(i - 1, 1)

            pe.wait_ge(w_in, 16)
            pe.wait_ge(r_in, 32)
            tiles(pe, body)
            finish(PT, 0)
            finish(PT, 1)

        @block.scalar
        def _(act):
            for n, (dst, _) in enumerate(SPREADS):
                act.wait_ge(row_mm, n + 1)
                nc.scalar.activation(dst, (A, B, C)[n % 3][:], ACT.Copy).then_inc(row_done, 1)

            def finish(i):
                T = width(i)
                act.wait_ge(h2T_mm, i + 1)
                if later(i):
                    act.wait_ge(rt_mm, i)
                nc.scalar.activation(h2T[:, :, 0:T], B[:].rearrange("p (k t) -> p k t", t=P)[:, :, 0:T], ACT.Copy
                                     ).then_inc(h2T_done, 1)

            def body(i):
                T = width(i)
                act.wait_ge(oT_mm, i + 1)
                if later(i):
                    act.wait_ge(pr_mm, i)
                nc.scalar.activation(oT[:, :, 0:T], A[:].rearrange("p (k t) -> p k t", t=P)[:, :, 0:T], ACT.Copy
                                     ).then_inc(oT_done, 1)
                if later(i):
                    finish(i - 1)
                act.wait_ge(x2_done, i + 1)
                nc.scalar.activation(sq[0:T], g.x2[0:T, i, :], ACT.Square, scale=D ** -0.5,
                                     accum_out=st[0:T, 0:1]).then_inc(ssq, 1)
                act.wait_ge(ssq, i + 1)
                nc.scalar.activation(st[0:T, 1:2], st[0:T, 0:1], ACT.Sqrt, bias=g.eps[0:T]).then_inc(rms, 1)

            tiles(act, body)
            finish(PT)

        @block.vector
        def _(dve):
            step = Steps(dve, dve_step)
            step(nc.vector.memset(g.logits[:], 0.0))
            dve.wait_ge(pool_step, 2)
            step(nc.vector.tensor_scalar(rown[:], rown[:], P - 1, None, ALU.bitwise_and))
            step(nc.vector.tensor_scalar(rowf[:], rown[:], float(2 * TOK), None, ALU.add))
            step(nc.vector.tensor_copy(pad[:, :, 0], padt[:]))
            nc.vector.tensor_copy(pad[:, :, 1], rowf[:]).then_inc(pad_done, 1)
            dve.wait_ge(row_done, len(SPREADS))

            def finish(i):
                T = width(i)
                dve.wait_ge(rt_mm, i + 1)
                nc.vector.tensor_tensor(g.logits[0:T, i, :], R[0:T, 0:NG + NE], bias[0:T], ALU.add
                                        ).then_inc(rt_done, 1)

            def body(i):
                T, b = width(i), 1 if last(i) else 0
                dve.wait_ge(pr_mm, i + 1)
                step(nc.vector.tensor_tensor(g.x2[0:T, i, :], C[0:T], rows[0:T, 0, b, :], ALU.mult))
                dve.wait_ge(x_in, 16 * i + 16)
                nc.vector.tensor_tensor(g.x2[0:T, i, :], g.x2[0:T, i, :], xr[0:T], ALU.add).then_inc(x2_done, 1)
                dve.wait_ge(rms, i + 1)
                step(nc.vector.reciprocal(st[0:T, 2:3], st[0:T, 1:2]))
                if later(i):
                    dve.wait_ge(h2T_mm, i)
                    dve.wait_ge(st_h2, 16 * i)
                step(nc.vector.scalar_tensor_tensor(h2[0:T], g.x2[0:T, i, :], st[0:T, 2:3], rows[0:T, 1, b, :],
                                                    ALU.mult, ALU.mult))
                nc.vector.tensor_tensor(h2[0:T], h2[0:T], rows[0:T, 2, b, :], ALU.add).then_inc(h2_done, 1)
                if later(i):
                    finish(i - 1)

            step.straight()
            tiles(dve, body, step)
            finish(PT)


def phase_r(nc, io, g):
    with ExitStack() as stack:
        m = Memory(nc, stack)
        gm = m.sb("r_gm", [P, NT])
        ex = m.sb("r_ex", [P, NT, NG])
        den = m.sb("r_den", [P, NT])
        pg = m.sb("r_pg", [P, NT])
        eq = m.sb("r_eq", [P, NT, EPG])
        sc = m.sb("r_sc", [P, NT])
        og = m.sb("r_og", [P, NT, NG])
        oe = [m.sb(f"r_oe{k}", [P, NT, EPG]) for k in range(2)]
        full = m.sb("r_full", [P, NT, NG, EPG])
        e_in = m.sb("r_e_in", [P, NT, EPG])
        v = [m.sb(f"r_v{k}", [P, NT]) for k in range(2)]
        pick = [m.sb(f"r_pick{k}", [P, NT, NE]) for k in range(2)]
        both = m.sb("r_both", [P, NT, NE])
        cum = m.sb("r_cum", [P, NT + 1, NE])
        rank = m.sb("r_rank", [P, NT, NE])
        tmp = m.sb("r_tmp", [P, NT, NE])
        rk = m.sb("r_rk", [P, NT])
        ei = m.sb("r_ei", [P, NT])
        dd = m.sb("r_dd", [P, NT])
        valid = m.sb("r_valid", [P, NT])
        count = m.sb("r_count", [P, NE])
        cmax = m.sb("r_cmax", [P, 1])
        i32 = m.sb("r_i32", [P, NE], I32)
        dest = m.sb("r_dest", [P, 2, NT], U32)
        idx = m.sb("r_idx", [P, NE])
        rev = m.sb("r_rev", [P, EPG])
        pair = m.sb("r_pair", [P, 2, NT, 2], U32)
        ranks = m.ps("r_ranks", [P, 512])
        counts = m.ps("r_counts", [P, 512])
        dve_step, pool_step, diff, expd, picked, ranked, placed, listed = m.sems(
            "r_dve_step r_pool_step r_diff r_expd r_picked r_ranked r_placed r_listed")
        block = stack.enter_context(nc.Block())

        def over(ap, n):
            return ap.unsqueeze(2).broadcast_to([P, NT, n])

        @block.gpsimd
        def _(pool):
            step = Steps(pool, pool_step)
            step(nc.gpsimd.iota(i32[:], pattern=[[1, NE]], base=0, channel_multiplier=0))
            for k in range(2):
                step(nc.gpsimd.iota(pair[:, k, :, 0], pattern=[[P, NT]], base=0, channel_multiplier=1))
                step(nc.gpsimd.iota(pair[:, k, :, 1], pattern=[[P, NT]], base=k * TOK, channel_multiplier=1))
            step(nc.gpsimd.memset(valid[:], 1.0))
            step(nc.gpsimd.memset(valid[:, PT:], 0.0))
            step(nc.gpsimd.memset(valid[0:DEC, PT:], 1.0))
            pool.wait_ge(placed, 1)
            for k in range(2):
                for i in range(NT):
                    T = P if i < PT else DEC
                    nc.gpsimd.indirect_dma_start(out=g.list_dram[:, :],
                                                 out_offset=bass.IndirectOffsetOnAxis(ap=dest[0:T, k, i:i + 1],
                                                                                      axis=0),
                                                 in_=pair[0:T, k, i, :], in_offset=None).then_inc(listed, 16)
            pool.wait_ge(listed, 2 * 16 * NT)

        @block.tensor
        def _(pe):
            pe.wait_ge(picked, 1)
            flat = lambda ap: ap.rearrange("p i e -> p (i e)")
            nc.tensor.matmul(ranks[:, 0:NT * NE], lhsT=g.tri[:], rhs=flat(both[:]), start=True, stop=False)
            nc.tensor.matmul(ranks[:, 0:NT * NE], lhsT=g.ones[:], rhs=flat(cum[:, 0:NT, :]), start=False, stop=True)
            nc.tensor.matmul(counts[:, 0:NE], lhsT=g.ones[:], rhs=cum[:, NT, :], start=True, stop=True
                             ).then_inc(ranked, 1)

        @block.scalar
        def _(act):
            act.wait_ge(diff, 1)
            nc.scalar.activation(ex[:], ex[:], ACT.Exp).then_inc(expd, 1)
            act.wait_ge(diff, 2)
            nc.scalar.activation(v[1][:], v[1][:], ACT.Exp).then_inc(expd, 1)

        @block.vector
        def _(dve):
            step = Steps(dve, dve_step)
            V = nc.vector
            dve.wait_ge(pool_step, 8)
            step(V.tensor_copy(idx[:], i32[:]))
            step(V.tensor_scalar(rev[:], idx[:, 0:EPG], -1.0, float(EPG), ALU.mult, ALU.add))
            lg = g.logits[:, :, 0:NG]
            le = g.logits[:, :, NG:].rearrange("p i (a e) -> p i a e", e=EPG)

            def first_max(out, values, top, n):
                r = rev[:, 0:n].unsqueeze(1).broadcast_to([P, NT, n])
                step(V.tensor_reduce(top, values, AX.X, ALU.max))
                step(V.tensor_tensor(eq[:, :, 0:n], values, over(top, n), ALU.is_equal))
                step(V.tensor_tensor(eq[:, :, 0:n], eq[:, :, 0:n], r, ALU.mult))
                step(V.tensor_reduce(sc[:], eq[:, :, 0:n], AX.X, ALU.max))
                step(V.tensor_tensor(out, eq[:, :, 0:n], over(sc[:], n), ALU.is_equal))

            first_max(og[:], lg, gm[:], NG)
            V.tensor_tensor(ex[:], lg, over(gm[:], NG), ALU.subtract).then_inc(diff, 1)
            step(V.tensor_tensor(full[:], le, og[:].unsqueeze(3).broadcast_to([P, NT, NG, EPG]), ALU.mult))
            step(V.tensor_reduce(e_in[:], full[:].rearrange("p i a e -> p i e a"), AX.X, ALU.add))
            first_max(oe[0][:], e_in[:], v[0][:], EPG)
            step(V.scalar_tensor_tensor(e_in[:].rearrange("p i e -> p (i e)"),
                                        oe[0][:].rearrange("p i e -> p (i e)"), 3.0 * NEG,
                                        e_in[:].rearrange("p i e -> p (i e)"), ALU.mult, ALU.add))
            first_max(oe[1][:], e_in[:], v[1][:], EPG)
            V.tensor_tensor(v[1][:], v[1][:], v[0][:], ALU.subtract).then_inc(diff, 1)
            dve.wait_ge(expd, 2)
            step(V.tensor_reduce(den[:], ex[:], AX.X, ALU.add))
            step(V.tensor_scalar(pg[:], v[1][:], 1.0, None, ALU.add))
            step(V.tensor_tensor(den[:], den[:], pg[:], ALU.mult))
            step(V.reciprocal(g.weight[:, 0, :], den[:]))
            step(V.tensor_tensor(g.weight[:, 1, :], g.weight[:, 0, :], v[1][:], ALU.mult))
            for k in range(2):
                p4 = pick[k][:].rearrange("p i (a e) -> p i a e", e=EPG)
                step(V.tensor_tensor(oe[k][:], oe[k][:], over(valid[:], EPG), ALU.mult))
                step(V.tensor_tensor(p4, og[:].unsqueeze(3).broadcast_to([P, NT, NG, EPG]),
                                     oe[k][:].unsqueeze(2).broadcast_to([P, NT, NG, EPG]), ALU.mult))
            step(V.memset(cum[:, 0, :], 0.0))
            step(V.tensor_tensor(both[:], pick[0][:], pick[1][:], ALU.add))
            for i in range(NT):
                end = V.tensor_tensor(cum[:, i + 1, :], cum[:, i, :], both[:, i, :], ALU.add)
                if i < NT - 1:
                    step(end)
            end.then_inc(picked, 1)
            dve.wait_ge(ranked, 1)
            step(V.tensor_copy(rank[:], ranks[:, 0:NT * NE].rearrange("p (i e) -> p i e", e=NE)))
            step(V.tensor_copy(count[:], counts[:, 0:NE]))
            step(V.tensor_copy(g.count[:], count[:]))
            step(V.tensor_reduce(cmax[:], count[:], AX.X, ALU.max))
            step(V.tensor_copy(g.longest[:], cmax[:]))
            for k in range(2):
                step(V.tensor_tensor(tmp[:], pick[k][:], rank[:], ALU.mult))
                step(V.tensor_reduce(rk[:], tmp[:], AX.X, ALU.add))
                step(V.tensor_tensor(tmp[:], pick[k][:], idx[:].unsqueeze(1).broadcast_to([P, NT, NE]), ALU.mult))
                step(V.tensor_reduce(ei[:], tmp[:], AX.X, ALU.add))
                step(V.scalar_tensor_tensor(dd[:], ei[:], float(REGION), rk[:], ALU.mult, ALU.add))
                end = V.tensor_copy(dest[:, k, :], dd[:])
                if k == 0:
                    step(end)
            end.then_inc(placed, 1)


def phase_g(nc, io, g):
    with ExitStack() as stack:
        m = Memory(nc, stack)
        FT = DE // P
        wg = m.sb("g_wg", [P, 2, KD, DE])
        wu = m.sb("g_wu", [P, 2, KD, DE])
        wd = m.sb("g_wd", [P, 2, FT, D])
        ix = [m.sb(f"g_ix{b}", [P, 2], U32) for b in range(2)]
        sl = [m.sb(f"g_sl{b}", [P, 2], U32) for b in range(2)]
        xg = m.sb("g_xg", [P, 2, D])
        xT = m.sb("g_xT", [P, KD, P])
        sig = m.sb("g_sig", [P, FT, P])
        hid = m.sb("g_hid", [P, 2, FT, P])
        y = m.sb("g_y", [P, 2, D])
        X = m.ps("g_X", [P, D])
        GU = [m.ps(f"g_GU{b}", [P, 2 * FT, P]) for b in range(2)]
        Y = [m.ps(f"g_Y{b}", [P, D]) for b in range(2)]
        (wgu0, wgu1, wd0, wd1, ix0, ix1, xg0, xg1, xT_mm, xT_done, gu_mm, sig_done, hid_done, dn_mm, y_done, st_y,
         dve_step, started, sl0, sl1, out_of) = m.sems(
            "g_wgu0 g_wgu1 g_wd0 g_wd1 g_ix0 g_ix1 g_xg0 g_xg1 g_xT_mm g_xT_done g_gu_mm g_sig_done g_hid_done "
            "g_dn_mm g_y_done g_st_y g_dve_step g_started g_sl0 g_sl1 g_out_of")
        sl_in = (sl0, sl1)
        wgu_in, wd_in, ix_in, xg_in = (wgu0, wgu1), (wd0, wd1), (ix0, ix1), (xg0, xg1)
        (l_free, l_w, l_ix, l_xg, l_xT_mm, l_xT, l_gu, l_sig, l_hid, l_dn, l_y, l_st, l_step) = m.sems(
            "l_free l_w l_ix l_xg l_xT_mm l_xT l_gu l_sig l_hid l_dn l_y l_st l_step")
        block = stack.enter_context(nc.Block())
        w_gate, w_up, w_down = io["w_gate"], io["w_up"], io["w_down"]

        def experts(engine, body, steps=None):
            body(0, 0, 0)
            if steps:
                steps.straight()
            body(1, 1, 0)
            if steps:
                per = 2 * steps.n
                steps.straight()
            with engine.Fori(1, NE // 2) as j:
                if steps:
                    steps.enter(j - 1, per)
                body(2 * j, 0, j)
                body(2 * j + 1, 1, j)
            if steps:
                steps.leave(NE // 2 - 1)

        def later(e, than=0):
            return not isinstance(e, int) or e > than

        def long_lists(engine, body):
            longest = engine.value_load(g.longest[0:1, 0:1], min_val=0, max_val=TOK)
            done = engine.alloc_register("done")
            engine.reg_mov(done, 0)
            with engine.If(longest > P):
                with engine.Fori(0, NE) as e:
                    count = engine.value_load(g.count[0:1, bass.ds(e, 1)], min_val=0, max_val=TOK)
                    with engine.Fori(1, REGION // P) as r:
                        with engine.If(count > r * P):
                            body(e, r * P, engine.snap(done))
                            engine.reg_add(done, done, 1)

        def scatter(pool, b, sem):
            nc.gpsimd.indirect_dma_start(out=g.y_dram[:, :], in_=y[:, b, :], in_offset=None,
                                         out_offset=bass.IndirectOffsetOnAxis(ap=sl[b][:, 1:2], axis=0)
                                         ).then_inc(sem, 16)

        def gather(pool, b, sem):
            nc.gpsimd.indirect_dma_start(out=xg[:, b, :], out_offset=None, in_=g.h2_dram[:, :],
                                         in_offset=bass.IndirectOffsetOnAxis(ap=ix[b][:, 0:1], axis=0)
                                         ).then_inc(sem, 16)

        def transposes(b):
            for k in range(KD):
                end = nc.tensor.transpose(X[:, k * P:(k + 1) * P], xg[:, b, k * P:(k + 1) * P], g.ident[:])
            return end

        def gate_up(b):
            for f in range(2 * FT):
                w = (wg, wu)[f // FT]
                for k in range(KD):
                    end = nc.tensor.matmul(GU[b][:, f, :], lhsT=w[:, b, k, (f % FT) * P:(f % FT + 1) * P],
                                           rhs=xT[:, k, :], start=k == 0, stop=k == KD - 1)
            return end

        def down(b):
            for c in range(2):
                for k in range(FT):
                    end = nc.tensor.matmul(Y[b][:, c * 512:(c + 1) * 512], lhsT=hid[:, b, k, :],
                                           rhs=wd[:, b, k, c * 512:(c + 1) * 512], start=k == 0, stop=k == FT - 1)
            return end

        @block.sync
        def _(sp):
            def load(e, b, gu_sem, d_sem):
                sp.dma_start(wg[:, b], w_gate[e].rearrange("(k p) n -> p k n", p=P)).then_inc(gu_sem, 16)
                sp.dma_start(wu[:, b], w_up[e].rearrange("(k p) n -> p k n", p=P)).then_inc(gu_sem, 16)
                return lambda: sp.dma_start(wd[:, b], w_down[e].rearrange("(k p) n -> p k n", p=P)
                                            ).then_inc(d_sem, 16)

            def body(e, b, n):
                if later(e, 1):
                    sp.wait_ge(gu_mm, e - 1)
                rest = load(e, b, wgu_in[b], wd_in[b])
                if later(e, 1):
                    sp.wait_ge(dn_mm, e - 1)
                rest()

            experts(sp, body)
            sp.wait_ge(out_of, NE + 1)
            sp.sem_inc(l_free, 1)

            def long_body(e, row, n):
                sp.wait_ge(l_free, n + 1)
                load(e, 0, l_w, l_w)()
                sp.wait_ge(l_st, n * 16 + 16)
                sp.sem_inc(l_free, 1)

            long_lists(sp, long_body)

        @block.gpsimd
        def _(pool):
            def list_tile(row, b, sem):
                return nc.gpsimd.dma_start(ix[b][:], g.list_dram[bass.ds(row, P), :]).then_inc(sem, 16)

            def results_out(e, b, n):
                pool.wait_ge(sl_in[b], 16 * n + 16)
                pool.wait_ge(y_done, e + 1)
                pool.sem_inc(started, 1)
                scatter(pool, b, st_y)
                pool.wait_ge(st_y, e * 16 + 16)
                pool.sem_inc(out_of, 1)

            def body(e, b, n):
                pool.wait_ge(ix_in[b], 16 * n + 16)
                if later(e, 1):
                    pool.wait_ge(xT_mm, e - 1)
                pool.sem_inc(started, 1)
                gather(pool, b, xg_in[b])

            def with_next(e, b, n):
                body(e, b, n)
                if later(e):
                    pool.wait_ge(xg_in[1 - b], 16 * n if b == 0 else 16 * n + 16)
                    pool.sem_inc(started, 1)
                list_tile((e + 1) * REGION, 1 - b, ix_in[1 - b])
                if later(e, 1):
                    results_out(e - 2, b, n - 1)

            pool.sem_inc(out_of, 1)
            list_tile(0, 0, ix_in[0])
            with_next(0, 0, 0)
            with_next(1, 1, 0)
            with pool.Fori(1, NE // 2 - 1) as j:
                with_next(2 * j, 0, j)
                with_next(2 * j + 1, 1, j)
            with_next(NE - 2, 0, NE // 2 - 1)
            body(NE - 1, 1, NE // 2 - 1)
            results_out(NE - 3, 1, NE // 2 - 2)
            results_out(NE - 2, 0, NE // 2 - 1)
            results_out(NE - 1, 1, NE // 2 - 1)

            def long_body(e, row, n):
                pool.wait_ge(l_free, n + 1)
                pool.sem_inc(started, 1)
                list_tile(e * REGION + row, 0, l_ix)
                nc.gpsimd.dma_start(sl[0][:], g.list_dram[bass.ds(e * REGION + row, P), :]).then_inc(l_ix, 16)
                pool.wait_ge(l_ix, n * 32 + 32)
                pool.sem_inc(started, 1)
                gather(pool, 0, l_xg)
                pool.wait_ge(l_y, n + 1)
                pool.sem_inc(started, 1)
                scatter(pool, 0, l_st)

            long_lists(pool, long_body)

        @block.tensor
        def _(pe):
            def turn(e, b, n):
                pe.wait_ge(xg_in[b], 16 * n + 16)
                if later(e):
                    pe.wait_ge(xT_done, e)
                transposes(b).then_inc(xT_mm, 1)

            def finish(e, b):
                pe.wait_ge(hid_done, e + 1)
                if later(e, 1):
                    pe.wait_ge(y_done, e - 1)
                down(b).then_inc(dn_mm, 1)

            def body(e, b, n):
                pe.wait_ge(wgu_in[b], 32 * n + 32)
                pe.wait_ge(xT_done, e + 1)
                if later(e, 1):
                    pe.wait_ge(hid_done, e - 1)
                gate_up(b).then_inc(gu_mm, 1)
                if later(e):
                    pe.wait_ge(wd_in[1 - b], 16 * (n if b == 0 else n + 1))
                    finish(e - 1, 1 - b)

            def with_next(e, b, n):
                body(e, b, n)
                turn(e + 1, 1 - b, n if b == 0 else n + 1)

            turn(0, 0, 0)
            with_next(0, 0, 0)
            with_next(1, 1, 0)
            with pe.Fori(1, NE // 2 - 1) as j:
                with_next(2 * j, 0, j)
                with_next(2 * j + 1, 1, j)
            with_next(NE - 2, 0, NE // 2 - 1)
            body(NE - 1, 1, NE // 2 - 1)
            pe.wait_ge(wd_in[1], 16 * (NE // 2))
            finish(NE - 1, 1)

            def long_body(e, row, n):
                pe.wait_ge(l_xg, n * 16 + 16)
                transposes(0).then_inc(l_xT_mm, 1)
                pe.wait_ge(l_xT, n + 1)
                pe.wait_ge(l_w, n * 48 + 48)
                gate_up(0).then_inc(l_gu, 1)
                pe.wait_ge(l_hid, n + 1)
                down(0).then_inc(l_dn, 1)

            long_lists(pe, long_body)

        @block.scalar
        def _(act):
            def squash(b):
                return nc.scalar.activation(sig[:], GU[b][:, 0:FT, :], ACT.Sigmoid)

            def out(b):
                return nc.scalar.activation(y[:, b, :], Y[b][:], ACT.Copy)

            def finish(e, b, n):
                if later(e, 1):
                    act.wait_ge(out_of, e)
                act.dma_start(sl[b][:], g.list_dram[bass.ds(e * REGION, P), :]).then_inc(sl_in[b], 16)
                act.wait_ge(dn_mm, e + 1)
                out(b).then_inc(y_done, 1)

            def body(e, b, n):
                act.wait_ge(gu_mm, e + 1)
                if later(e):
                    act.wait_ge(hid_done, e)
                squash(b).then_inc(sig_done, 1)
                if later(e):
                    finish(e - 1, 1 - b, n - 1 if b == 0 else n)

            experts(act, body)
            finish(NE - 1, 1, NE // 2 - 1)

            def long_body(e, row, n):
                act.wait_ge(l_gu, n + 1)
                squash(0).then_inc(l_sig, 1)
                act.wait_ge(l_dn, n + 1)
                out(0).then_inc(l_y, 1)

            long_lists(act, long_body)

        @block.vector
        def _(dve):
            step = Steps(dve, dve_step)

            def rows_out():
                return nc.vector.tensor_copy(xT[:], X[:].rearrange("p (k t) -> p k t", t=P))

            def gated(b, mark):
                mark(nc.vector.tensor_tensor(sig[:], GU[b][:, 0:FT, :], sig[:], ALU.mult))
                return nc.vector.tensor_tensor(hid[:, b], GU[b][:, FT:, :], sig[:], ALU.mult)

            def body(e, b, n):
                dve.wait_ge(xT_mm, e + 1)
                if later(e):
                    dve.wait_ge(gu_mm, e)
                    rows_out().then_inc(xT_done, 1)
                    dve.wait_ge(sig_done, e)
                    if later(e, 2):
                        dve.wait_ge(dn_mm, e - 2)
                    gated(1 - b, step).then_inc(hid_done, 1)
                else:
                    rows_out().then_inc(xT_done, 1)

            experts(dve, body, step)
            dve.wait_ge(sig_done, NE)
            dve.wait_ge(dn_mm, NE - 2)
            gated(1, step).then_inc(hid_done, 1)

            def long_body(e, row, n):
                dve.wait_ge(l_xT_mm, n + 1)
                rows_out().then_inc(l_xT, 1)
                dve.wait_ge(l_sig, n + 1)

                def mark(ins):
                    ins.then_inc(l_step, 1)
                    dve.wait_ge(l_step, n + 1)

                gated(0, mark).then_inc(l_hid, 1)

            long_lists(dve, long_body)


def phase_h(nc, io, g):
    with ExitStack() as stack:
        m = Memory(nc, stack)
        y = [[m.sb(f"h_y{k}{b}", [P, D]) for b in range(2)] for k in range(2)]
        out = m.sb("h_out", [P, 2, D])
        y_in = [[m.sems(f"h_y_in{k}{b}")[0] for b in range(2)] for k in range(2)]
        summed, dve_step, st0, st1 = m.sems("h_summed h_dve_step h_st0 h_st1")
        st = (st0, st1)
        block = stack.enter_context(nc.Block())

        @block.vector
        def _(dve):
            step = Steps(dve, dve_step)

            def tile(i, b, n, T, mod):
                dve.wait_ge(y_in[0][b], 16 * n + 16)
                if not (isinstance(n, int) and n == 0):
                    dve.wait_ge(st[b], 16 * n)
                step(nc.vector.tensor_scalar(out[0:T, b], y[0][b][0:T], g.weight[0:T, 0, bass.ds(i, 1)], None,
                                             ALU.mult))
                dve.wait_ge(y_in[1][b], 16 * n + 16)
                step(nc.vector.scalar_tensor_tensor(out[0:T, b], y[1][b][0:T], g.weight[0:T, 1, bass.ds(i, 1)],
                                                    out[0:T, b], ALU.mult, ALU.add))
                step(nc.vector.tensor_tensor(out[0:T, b], out[0:T, b], g.gate_m[0:T, mod, :], ALU.mult))
                nc.vector.tensor_tensor(out[0:T, b], out[0:T, b], g.x2[0:T, i, :], ALU.add).then_inc(summed, 1)

            tile(0, 0, 0, P, 0)
            tile(1, 1, 0, P, 0)
            per = step.n
            step.straight()
            with dve.Fori(1, PT // 2) as j:
                step.enter(j - 1, per)
                tile(2 * j, 0, j, P, 0)
                tile(2 * j + 1, 1, j, P, 0)
            step.leave(PT // 2 - 1)
            tile(PT, 0, PT // 2, DEC, 1)

        @block.sync
        def _(sp):
            def load(i, b, T):
                for k in range(2):
                    sp.dma_start(y[k][b][0:T, :], g.y_dram[bass.ds(i * P + k * TOK, T), :]).then_inc(y_in[k][b], 16)

            def store(i, b, T):
                sp.wait_ge(summed, i + 1)
                sp.dma_start(io["y_p"][bass.ds(i * P, P), :], out[:, b]).then_inc(st[b], 16)
                if T:
                    load(i + 2, b, T)

            load(0, 0, P)
            load(1, 1, P)
            with sp.Fori(0, PT // 2 - 1) as j:
                store(2 * j, 0, P)
                store(2 * j + 1, 1, P)
            store(PT - 2, 0, DEC)
            store(PT - 1, 1, 0)
            sp.wait_ge(summed, NT)
            sp.dma_start(io["y_s"], out[0:DEC, 0]).then_inc(st[0], 16)
            sp.wait_ge(st[0], 16 * (PT // 2 + 1))
            sp.wait_ge(st[1], 16 * (PT // 2))


class Shared:
    pass


INPUTS = ("x_prompt", "x_sample", "cache_sb_k", "cache_sb_v", "cache_mla_ckv", "cache_mla_kpe", "c_prompt",
          "c_sample", "w_ada", "b_ada", "g_mix", "w_in", "g_sb_q", "g_sb_k", "g_qa", "w_qb", "g_kva", "w_kvb",
          "g_mq_nope", "g_mk_nope", "g_mq_pe", "g_mk_pe", "w_out", "g_ffn", "w_rg", "b_rg", "w_re", "b_re",
          "w_gate", "w_up", "w_down")


def program(nc, io):
    USED.clear()
    g = Shared()
    with ExitStack() as stack:
        m = Memory(nc, stack)
        g.qs_dram = nc.dram_tensor("qs_dram", [SBH // 2, P, TOK], F32, kind="Internal").ap()
        g.ks_dram = nc.dram_tensor("ks_dram", [SBH // 2, P, TOK], F32, kind="Internal").ap()
        g.o_dram = nc.dram_tensor("o_dram", [TOK, D], F32, kind="Internal").ap()
        g.h2_dram = nc.dram_tensor("h2_dram", [TOK + 1, D], F32, kind="Internal").ap()
        g.list_dram = nc.dram_tensor("list_dram", [NE * REGION, 2], U32, kind="Internal").ap()
        g.y_dram = nc.dram_tensor("y_dram", [2 * TOK + P, D], F32, kind="Internal").ap()
        g.qm_dram = nc.dram_tensor("qm_dram", [MH, MK, TOK], F32, kind="Internal").ap()
        g.ident = m.sb("ident", [P, P])
        g.identb = m.sb("identb", [P, P], BF16)
        g.mask_sb = m.sb("mask_sb", [P, P], BF16)
        g.mask_mla = m.sb("mask_mla", [P, P], BF16)
        g.tri = m.sb("tri", [P, P])
        g.ones = m.sb("ones", [P, P])
        g.eps = m.sb("eps", [P, 1])
        g.rows = m.sb("rows", [P, ROWW])
        g.modT = m.sb("modT", [P, 48, 2])
        g.scale_a = m.sb("scale_a", [P, KD, 2])
        g.scale_m = m.sb("scale_m", [P, KD, 2])
        g.ckv_new = m.sb("ckv_new", [P, KR])
        g.w_in_loaded, g.w_small_loaded = m.sems("w_in_loaded w_small_loaded")
        with ExitStack() as keys:
            m = Memory(nc, keys)
            g.kT_m = m.sb("kT_m", [MK, MH, TOK])
            g.values = m.sb("values", [P, 2 * NT * SBW])
            g.v_sb = g.values[:, 0:NT * SBW].rearrange("p (i n) -> p i n", n=SBW)
            g.v_m = g.values[:, NT * SBW:].rearrange("p (i n) -> p i n", n=MH * MV)
            g.w_kvb = m.sb("w_kvb_sb", [P, KR // P, MH * (NOPE + MV)])
            with ExitStack() as weights:
                m = Memory(nc, weights)
                g.w_in = m.sb("w_in_sb", [P, KD, INC])
                g.w_qb = m.sb("w_qb_sb", [P, QR // P, MH * MK])
                g.rope = m.sb("rope_sb", [P, NT, 2 * ROPE])
                phase_a(nc, io, g)
                phase_b(nc, io, g)
            phase_cd(nc, io, g)
            phase_e(nc, io, g, latent=False)
            phase_e(nc, io, g, latent=True)
        retire_semaphores(nc)
        m = Memory(nc, stack)
        g.x2 = m.sb("x2", [P, NT, D])
        g.gate_m = m.sb("gate_m", [P, 2, D])
        g.logits = m.sb("logits", [P, NT, NG + NE])
        g.weight = m.sb("weight", [P, 2, NT])
        g.count = m.sb("count", [P, NE], I32)
        g.longest = m.sb("longest", [P, 1], I32)
        phase_f(nc, io, g)
        phase_r(nc, io, g)
        phase_g(nc, io, g)
        phase_h(nc, io, g)


def rope_table():
    inv = np.float32(10000.0) ** (-np.arange(0, ROPE, 2, dtype=np.float32) / np.float32(ROPE))
    pos = np.zeros(NT * P, np.float32)
    pos[:SEQ] = np.arange(SEQ)
    pos[SEQ:TOK] = PAST + np.arange(DEC)
    ang = pos[:, None] * inv[None, :].astype(np.float32)
    c, s = np.cos(ang), np.sin(ang)
    t = np.concatenate([c, c, -s, s], axis=1).astype(np.float32)
    return np.ascontiguousarray(t.reshape(NT, P, 2 * ROPE).transpose(1, 0, 2))


def kernel(**inputs):
    import concourse.bacc as bacc
    from concourse.bass_utils import run_bass_kernel_spmd

    nc = bacc.Bacc("TRN2", target_bir_lowering=False, num_devices=1)
    shapes = {
        "x_prompt": (SEQ, D), "x_sample": (DEC, D), "cache_sb_k": (PAST, SBW), "cache_sb_v": (PAST, SBW),
        "cache_mla_ckv": (PAST, KR), "cache_mla_kpe": (PAST, ROPE), "c_prompt": (D,), "c_sample": (D,),
    }
    arrays, io = {}, {}
    for name in INPUTS:
        a = np.asarray(inputs[name])
        a = np.ascontiguousarray(a.reshape(shapes.get(name, a.shape[1:])))
        arrays[name] = a
        io[name] = nc.dram_tensor(name, a.shape, mybir.dt.from_np(a.dtype), kind="ExternalInput").ap()
    arrays["rope"] = rope_table()
    io["rope"] = nc.dram_tensor("rope", arrays["rope"].shape, F32, kind="ExternalInput").ap()
    outs = (("y_p", (SEQ, D), (1, SEQ, D)), ("y_s", (DEC, D), (1, DEC, D)),
            ("o_k_p", (SEQ, SBW), (1, 1, SEQ, SBH, SBD)), ("o_v_p", (SEQ, SBW), (1, 1, SEQ, SBH, SBD)),
            ("o_ckv_p", (SEQ, KR), (1, 1, SEQ, KR)), ("o_kpe_p", (SEQ, ROPE), (1, 1, SEQ, ROPE)),
            ("o_k_s", (DEC, SBW), (1, 1, DEC, SBH, SBD)), ("o_v_s", (DEC, SBW), (1, 1, DEC, SBH, SBD)),
            ("o_ckv_s", (DEC, KR), (1, 1, DEC, KR)), ("o_kpe_s", (DEC, ROPE), (1, 1, DEC, ROPE)))
    for name, shape, _ in outs:
        io[name] = nc.dram_tensor(name, shape, F32, kind="ExternalOutput").ap()
    program(nc, io)
    r = run_bass_kernel_spmd(nc, [arrays], core_ids=[0])
    return tuple(np.asarray(r.results[0][name]).reshape(shape) for name, _, shape in outs)
```

```python
from contextlib import ExitStack

import numpy as np

import concourse.bass as bass
from concourse import mybir

F32 = mybir.dt.float32
BF16 = mybir.dt.bfloat16
U32 = mybir.dt.uint32
I32 = mybir.dt.int32
ALU = mybir.AluOpType
ACT = mybir.ActivationFunctionType
AX = mybir.AxisListType

P = 128
D = 1024
KD = D // P
SEQ, DEC, PAST = 1024, 32, 2048
PT = SEQ // P
NT = PT + 1
TOK = SEQ + DEC
SBH, SBD = 8, 64
MH, NOPE, ROPE, MV = 8, 64, 32, 64
MK = NOPE + ROPE
QR, KR = 384, 256
SBW = SBH * SBD
INC = 3 * SBW + QR + KR + ROPE
EPS = 1e-6
NEG = -1e30
NG, EPG, NE, DE = 4, 8, 32, 256
SB_SCALE = SBD ** -0.5
MLA_SCALE = MK ** -0.5
PTILES = PAST // P
SKEYS = PAST + DEC
REGION = 9 * P
PAD = TOK

ROWS = {}
_at = 0
for _n, _w in (("g_sb_q", SBD), ("g_sb_k", SBD), ("g_mq_nope", NOPE), ("g_mk_nope", NOPE), ("g_mq_pe", ROPE),
               ("g_mk_pe", ROPE), ("g_kva", KR), ("g_qa", QR), ("b_rg", NG), ("b_re", NE)):
    ROWS[_n] = (_at, _at + _w)
    _at += _w
ROWW = _at
VEC = {"b_ada": (0, 48), "g_mix": (48, 56), "g_ffn": (56, 64), "c_prompt": (64, 72), "c_sample": (72, 80)}


class Steps:

    def __init__(self, engine, sem):
        self.engine, self.sem, self.base, self.n, self.total = engine, sem, 0, 0, 0

    def __call__(self, ins):
        ins.then_inc(self.sem, 1)
        self.n += 1
        self.engine.wait_ge(self.sem, self.base + self.n)

    def enter(self, turn, per):
        self.base, self.n, self.per = self.total + turn * per, 0, per

    def leave(self, turns):
        assert self.n == self.per, (self.n, self.per)
        self.total += turns * self.per
        self.base, self.n = self.total, 0

    def straight(self):
        self.total += self.n
        self.base, self.n = self.total, 0


class Memory:

    def __init__(self, nc, stack):
        self.nc, self.stack = nc, stack

    def sb(self, name, shape, dt=F32):
        t = self.stack.enter_context(self.nc.sbuf_tensor(name, shape, dt))
        return t

    def ps(self, name, shape, dt=F32):
        return self.stack.enter_context(self.nc.psum_tensor(name, shape, dt))

    def sems(self, names):
        made = [self.nc.alloc_semaphore(n) for n in names.split()]
        USED.extend(made)
        return made


USED = []


def retire_semaphores(nc):
    nc.clear_and_free_semaphores(list(USED))
    USED.clear()
    nc.all_engine_barrier()


def phase_a(nc, io, g):
    with ExitStack() as stack:
        m = Memory(nc, stack)
        WCOLS, WBUFS = 512, 2
        CHUNKS = 6 * D // WCOLS
        CT = WCOLS // P
        vrows = m.sb("vrows", [80, P])
        grow = m.sb("grow", [1, 1024])
        ones1 = m.sb("ones1", [1, P])
        vecT = m.sb("vecT", [P, 80])
        sig = m.sb("sig", [P, 16])
        silu_c = m.sb("silu_c", [P, KD, 2])
        wa = g.values[:, 0:WBUFS * KD * WCOLS].rearrange("p (b k n) -> p b k n", b=WBUFS, n=WCOLS)
        ps_vec = m.ps("ps_vec", [P, 512])
        mod_row = m.sb("mod_row", [2, WBUFS, WCOLS])
        ps_row = m.ps("ps_row", [P, 1024])
        ps_sum = [m.ps(f"ps_sum{b}", [P, WCOLS]) for b in range(WBUFS)]
        ps_mod = [m.ps(f"ps_mod{b}", [P, 512]) for b in range(WBUFS)]
        (vec_in, row_in, const_ready, vec_t, vec_done, sig_done, silu_done, row_mm, row_done, mod_mm, mod_done,
         dve_step, w_loaded0, w_loaded1, pool_step, sum_mm, sum_out) = m.sems(
            "vec_in row_in const_ready vec_t vec_done sig_done silu_done row_mm row_done mod_mm mod_done "
            "dve_step w_loaded0 w_loaded1 pool_step sum_mm sum_out")
        w_loaded = [w_loaded0, w_loaded1]
        block = stack.enter_context(nc.Block())
        w_ada = io["w_ada"].rearrange("(k p) n -> p k n", p=P)

        @block.sync
        def _(sp):
            for name, (a, b) in VEC.items():
                sp.dma_start(vrows[a:b, :], io[name].rearrange("(j p) -> j p", p=P)).then_inc(vec_in, 16)
            for name, (a, b) in ROWS.items():
                sp.dma_start(grow[0:1, a:b], io[name].rearrange("(o n) -> o n", o=1)).then_inc(row_in, 16)
            for b in range(WBUFS):
                sp.dma_start(wa[:, b], w_ada[:, :, b * WCOLS:(b + 1) * WCOLS]).then_inc(w_loaded[b], 16)
            w_in = io["w_in"].rearrange("(k p) n -> p k n", p=P)

            def turn(j, k):
                for b in range(WBUFS):
                    sp.wait_ge(sum_mm, j * WBUFS + (b - WBUFS + 1))
                    sp.dma_start(wa[:, b], w_ada[:, :, bass.ds((j * WBUFS + b) * WCOLS, WCOLS)]
                                 ).then_inc(w_loaded[b], 16)
                    if k is not None:
                        sp.dma_start(g.w_in[:, bass.ds(k + b, 1), :], w_in[:, bass.ds(k + b, 1), :]
                                     ).then_inc(g.w_in_loaded, 16)

            with sp.Fori(1, 1 + KD // WBUFS) as j:
                turn(j, (j - 1) * WBUFS)
            for j in range(1 + KD // WBUFS, CHUNKS // WBUFS):
                turn(j, None)
            sp.dma_start(g.w_qb[:], io["w_qb"].rearrange("(k p) n -> p k n", p=P)).then_inc(g.w_small_loaded, 16)
            sp.dma_start(g.w_kvb[:], io["w_kvb"].rearrange("(k p) n -> p k n", p=P)).then_inc(g.w_small_loaded, 16)
            sp.dma_start(g.rope[:], io["rope"]).then_inc(g.w_small_loaded, 16)

        @block.gpsimd
        def _(pool):
            step = Steps(pool, pool_step)
            step(nc.gpsimd.memset(g.ident[:], 0.0))
            step(nc.gpsimd.memset(ones1[:], 1.0))
            step(nc.gpsimd.memset(g.mask_sb[:], 0.0))
            step(nc.gpsimd.memset(g.mask_mla[:], 0.0))
            step(nc.gpsimd.memset(g.mask_mla[0:64, 64:P], NEG))
            step(nc.gpsimd.memset(g.tri[:], 1.0))
            step(nc.gpsimd.memset(g.ones[:], 1.0))
            step(nc.gpsimd.memset(g.eps[:], EPS))
            step(nc.gpsimd.affine_select(out=g.ident[:], in_=g.ident[:], compare_op=ALU.not_equal, fill=1.0,
                                         base=0, pattern=[[-1, P]], channel_multiplier=1))
            step(nc.gpsimd.affine_select(out=g.mask_sb[:], in_=g.mask_sb[:], compare_op=ALU.is_gt, fill=NEG,
                                         base=0, pattern=[[-1, P]], channel_multiplier=1))
            step(nc.gpsimd.affine_select(out=g.tri[:], in_=g.tri[:], compare_op=ALU.is_gt, fill=0.0,
                                         base=0, pattern=[[1, P]], channel_multiplier=-1))
            nc.gpsimd.tensor_copy(g.identb[:], g.ident[:]).then_inc(const_ready, 1)

        @block.scalar
        def _(act):
            act.wait_ge(vec_done, 1)
            a = VEC["c_prompt"][0]
            nc.scalar.activation(sig[:], vecT[:, a:a + 16], ACT.Sigmoid).then_inc(sig_done, 1)

            def rows_out(j, b):
                n = j * WBUFS + b
                act.wait_ge(sum_mm, n + 1)
                if not isinstance(j, int):
                    act.wait_ge(mod_mm, n - (WBUFS - 1))
                nc.scalar.activation(mod_row[:, b, :], ps_sum[b][0:2, :], ACT.Copy).then_inc(sum_out, 1)

            for b in range(WBUFS):
                rows_out(0, b)
            with act.Fori(1, CHUNKS // WBUFS) as j:
                for b in range(WBUFS):
                    rows_out(j, b)

        @block.tensor
        def _(pe):
            pe.wait_ge(const_ready, 1)
            pe.wait_ge(vec_in, 16 * len(VEC))
            nc.tensor.transpose(ps_vec[:, 0:80], vrows[:], g.ident[0:80, 0:80]).then_inc(vec_t, 1)
            pe.wait_ge(row_in, 16 * len(ROWS))
            nc.tensor.matmul(ps_row[:, 0:512], lhsT=ones1[:], rhs=grow[0:1, 0:512], start=True, stop=True)
            nc.tensor.matmul(ps_row[:, 512:ROWW], lhsT=ones1[:], rhs=grow[0:1, 512:ROWW], start=True,
                             stop=True).then_inc(row_mm, 1)
            pe.wait_ge(silu_done, 1)

            def sums(j, b):
                pe.wait_ge(w_loaded[b], 16 * j + 16)
                if not isinstance(j, int):
                    pe.wait_ge(sum_out, j * WBUFS + (b - WBUFS + 1))
                for k in range(KD):
                    last = nc.tensor.matmul(ps_sum[b][0:2, :], lhsT=silu_c[:, k, :], rhs=wa[:, b, k, :],
                                            start=k == 0, stop=k == KD - 1)
                last.then_inc(sum_mm, 1)

            def turned(j, b, first=False):
                n = j * WBUFS + b
                pe.wait_ge(sum_out, n + 1)
                if not first:
                    pe.wait_ge(mod_done, n - (WBUFS - 1))
                for t in range(CT):
                    last = nc.tensor.matmul(ps_mod[b][:, 2 * t:2 * t + 2], lhsT=mod_row[:, b, t * P:(t + 1) * P],
                                            rhs=g.ident[0:2, 0:2], start=True, stop=True)
                last.then_inc(mod_mm, 1)

            sums(0, 0)
            sums(0, 1)
            turned(0, 0, True)
            turned(0, 1, True)
            with pe.Fori(1, CHUNKS // WBUFS) as j:
                sums(j, 0)
                sums(j, 1)
                turned(j, 0)
                turned(j, 1)

        @block.vector
        def _(dve):
            step = Steps(dve, dve_step)
            dve.wait_ge(vec_t, 1)
            nc.vector.tensor_copy(vecT[:], ps_vec[:, 0:80]).then_inc(vec_done, 1)
            dve.wait_ge(row_mm, 1)
            nc.vector.tensor_copy(g.rows[:], ps_row[:, 0:ROWW]).then_inc(row_done, 1)
            dve.wait_ge(sig_done, 1)
            a = VEC["c_prompt"][0]
            dve.wait_ge(vec_done, 1)
            nc.vector.tensor_tensor(silu_c[:].rearrange("p k b -> p b k"),
                                    vecT[:, a:a + 16].rearrange("p (b k) -> p b k", b=2),
                                    sig[:].rearrange("p (b k) -> p b k", b=2), ALU.mult).then_inc(silu_done, 1)

            def chunk(j, b):
                at = (j * WBUFS + b) * CT
                dve.wait_ge(mod_mm, j * WBUFS + (b + 1))
                nc.vector.tensor_tensor(g.modT[:, bass.ds(at, CT), :],
                                        ps_mod[b][:, 0:2 * CT].rearrange("p (t b) -> p t b", b=2),
                                        vecT[:, bass.ds(at, CT)].unsqueeze(2).broadcast_to([P, CT, 2]),
                                        ALU.add).then_inc(mod_done, 1)

            with dve.Fori(0, CHUNKS // WBUFS) as j:
                for b in range(WBUFS):
                    chunk(j, b)
            dve.wait_ge(mod_done, CHUNKS)
            for out, name, chunk_at in ((g.scale_a, "g_mix", 1), (g.scale_m, "g_ffn", 4)):
                a, b = VEC[name]
                step(nc.vector.tensor_scalar(out[:], g.modT[:, 8 * chunk_at:8 * chunk_at + 8, :], 1.0, None,
                                             ALU.add))
                step(nc.vector.tensor_tensor(out[:], out[:], vecT[:, a:b].unsqueeze(2).broadcast_to([P, KD, 2]),
                                             ALU.mult))


def phase_b(nc, io, g):
    with ExitStack() as stack:
        m = Memory(nc, stack)
        x = m.sb("b_x", [P, D])
        hT = m.sb("b_hT", [P, KD, P])
        sq = m.sb("b_sq", [P, D])
        qk = m.sb("b_qk", [P, 2 * SBH, SBD])
        qlat = m.sb("b_qlat", [P, QR])
        qlatT = m.sb("b_qlatT", [P, QR // P, P])
        ckvT = m.sb("b_ckvT", [P, KR // P, P])
        kpe = m.sb("b_kpe", [P, 2 * ROPE])
        qf = m.sb("b_qf", [P, MH, MK])
        kf = m.sb("b_kf", [P, MH, MK])
        qsT = m.sb("b_qsT", [P, 4, P])
        ksT = m.sb("b_ksT", [P, 4, P])
        qmT = m.sb("b_qmT", [MK, MH, P])
        rot = m.sb("b_rot", [P, MH, ROPE])
        st = m.sb("b_st", [P, 8])
        sth = m.sb("b_sth", [P, 48])
        ckv = g.ckv_new
        U = [m.ps(f"b_U{n}", [P, 512]) for n in range(2)]
        U2 = m.ps("b_U2", [P, 512])
        UL = m.ps("b_UL", [P, 2, 512])
        TA, TB, X = (m.ps(n, [P, 512]) for n in ("b_TA", "b_TB", "b_X"))
        (x_in, xstat, xrms, xrec, xn_done, ht_mm, ht_done, lat_mm, lat_sq, lat_rms, lat_norm, kpe_done,
         latT_mm, latTa_done, latTb_done, q_mm, k_mm, v_mm, qk_evac, qk_sq, v_evac, qk_red, qk_rms, qk_norm,
         qmla_mm, kv_mm, qm_evac, kv_evac, mla_red, mla_rms, mla_norm, r0, r1, r2, r3, r4, r5, e0, e1, e2, e3,
         e4, e5, st_ckv, st_kpe, st_k, st_v, st_qs, st_ks, st_qm, dve_step) = m.sems(
            "x_in xstat xrms xrec xn_done ht_mm ht_done lat_mm lat_sq lat_rms lat_norm kpe_done latT_mm "
            "latTa_done latTb_done q_mm k_mm v_mm qk_evac qk_sq v_evac qk_red qk_rms qk_norm qmla_mm kv_mm "
            "qm_evac kv_evac mla_red mla_rms mla_norm r0 r1 r2 r3 r4 r5 e0 e1 e2 e3 e4 e5 st_ckv st_kpe st_k "
            "st_v st_qs st_ks st_qm b_dve_step")
        block = stack.enter_context(nc.Block())
        row = {n: g.rows[:, a:b] for n, (a, b) in ROWS.items()}

        def last(i):
            return isinstance(i, int) and i == PT

        def width(i):
            return DEC if last(i) else P

        def tiles(engine, body, steps=None):
            body(0)
            if steps:
                per = steps.n
                steps.straight()
            with engine.Fori(1, PT - 1) as i:
                if steps:
                    steps.enter(i - 1, per)
                body(i)
            if steps:
                steps.leave(PT - 2)
            body(PT - 1)
            body(PT)

        @block.sync
        def _(sp):
            sp.dma_start(x[:], io["x_prompt"][0:P, :]).then_inc(x_in, 16)

            def queries_out(i):
                T = width(i)
                sp.wait_ge(e0, i + 1)
                sp.dma_start(g.qs_dram[:, :, bass.ds(i * P, T)].rearrange("a p t -> p a t"),
                             qsT[:, :, 0:T]).then_inc(st_qs, 16)
                sp.wait_ge(e1, i + 1)
                sp.dma_start(g.ks_dram[:, :, bass.ds(i * P, T)].rearrange("a p t -> p a t"),
                             ksT[:, :, 0:T]).then_inc(st_ks, 16)
                sp.wait_ge(e3, i + 1)
                sp.wait_ge(e2, i + 1)
                sp.dma_start(g.qm_dram[:, :, bass.ds(i * P, T)].rearrange("h p t -> p h t"),
                             qmT[:, :, 0:T]).then_inc(st_qm, 16)

            def out(name, i):
                return io[name + "_s"] if last(i) else io[name + "_p"][bass.ds(i * P, P), :]

            def body(i):
                T = width(i)
                if not last(i):
                    sp.wait_ge(ht_mm, i + 1)
                    if last(i + 1):
                        sp.dma_start(x[0:DEC, :], io["x_sample"]).then_inc(x_in, 16)
                    else:
                        sp.dma_start(x[:], io["x_prompt"][bass.ds((i + 1) * P, P), :]).then_inc(x_in, 16)
                sp.wait_ge(kpe_done, i + 1)
                sp.dma_start(out("o_ckv", i), ckv[0:T, :]).then_inc(st_ckv, 16)
                sp.dma_start(out("o_kpe", i), kpe[0:T, ROPE:2 * ROPE]).then_inc(st_kpe, 16)
                if not (isinstance(i, int) and i == 0):
                    queries_out(i - 1)
                sp.wait_ge(qk_norm, i + 1)
                sp.dma_start(out("o_k", i), qk[0:T, SBH:, :].rearrange("p h d -> p (h d)")).then_inc(st_k, 16)
                sp.wait_ge(v_evac, i + 1)
                sp.dma_start(out("o_v", i), g.v_sb[0:T, i, :]).then_inc(st_v, 16)

            tiles(sp, body)
            queries_out(PT)
            for s in (st_ckv, st_kpe, st_v, st_k, st_qs, st_ks, st_qm):
                sp.wait_ge(s, 16 * NT)

        @block.tensor
        def _(pe):
            pe.wait_ge(g.w_in_loaded, 16 * KD)
            pe.wait_ge(g.w_small_loaded, 48)

            def transposes(dst, src, w, n, T, sem, wait):
                for s, v in wait:
                    pe.wait_ge(s, v)
                for j in range(n):
                    end = nc.tensor.transpose(dst[0:w, j * P:j * P + T], src(j), g.ident[0:T, 0:T])
                end.then_inc(sem, 1)

            def hT_of(i):
                T = width(i)
                pe.wait_ge(xn_done, i + 1)
                for k in range(KD):
                    end = nc.tensor.transpose(U[k // 4][:, (k % 4) * P:(k % 4) * P + T],
                                               x[0:T, k * P:(k + 1) * P], g.ident[0:T, 0:T])
                end.then_inc(ht_mm, 1)

            def project(dst, c0, c1, T, sem, val=None):
                for k in range(KD):
                    end = nc.tensor.matmul(dst[0:T, 0:c1 - c0], lhsT=hT[:, k, 0:T], rhs=g.w_in[:, k, c0:c1],
                                            start=k == 0, stop=k == KD - 1)
                if sem is not None:
                    end.then_inc(sem, 1)

            def pairs(first_head):
                return lambda j: qk[:, first_head + 2 * j:first_head + 2 * j + 2, :].rearrange("p h d -> p (h d)")

            def back(i, part):
                T = width(i)
                if part == 0:
                    pe.wait_ge(qk_norm, i + 1)
                    transposes(TA, lambda j: pairs(0)(j)[0:T], P, 4, T, r0, [(latTa_done, i + 1)])
                    transposes(TB, lambda j: pairs(SBH)(j)[0:T], P, 4, T, r1, [(kv_evac, i + 1)])
                    pe.wait_ge(mla_norm, i + 1)
                    transposes(X, lambda j: qf[0:T, j, :], MK, 4, T, r2, [(kv_evac, i + 1)])
                elif part == 1:
                    transposes(TA, lambda j: qf[0:T, 4 + j, :], MK, 4, T, r3, [(e0, i + 1)])
                    transposes(TB, lambda j: kf[0:T, j, :], MK, 4, T, r4, [(e1, i + 1)])
                    transposes(X, lambda j: kf[0:T, 4 + j, :], MK, 4, T, r5, [(e2, i + 1)])

            def body(i):
                T, first = width(i), isinstance(i, int) and i == 0
                pe.wait_ge(ht_done, i + 1)
                if not first:
                    pe.wait_ge(qm_evac, i)
                project(UL[:, 0, :], 3 * SBW, 3 * SBW + QR, T, None)
                project(UL[:, 1, :], 3 * SBW + QR, INC, T, lat_mm)
                if not first:
                    back(i - 1, 0)
                project(U[0], 0, SBW, T, q_mm)
                if not first:
                    back(i - 1, 1)
                project(U[1], SBW, 2 * SBW, T, k_mm)
                pe.wait_ge(lat_norm, i + 1)
                if not first:
                    pe.wait_ge(e3, i)
                    pe.wait_ge(e4, i)
                for j in range(QR // P):
                    nc.tensor.transpose(TA[:, j * P:j * P + T], qlat[0:T, j * P:(j + 1) * P], g.ident[0:T, 0:T])
                for j in range(KR // P):
                    end = nc.tensor.transpose(TB[:, j * P:j * P + T], ckv[0:T, j * P:(j + 1) * P],
                                               g.ident[0:T, 0:T])
                end.then_inc(latT_mm, 1)
                if not first:
                    pe.wait_ge(v_evac, i)
                project(U2, 2 * SBW, 3 * SBW, T, v_mm)
                if not last(i):
                    pe.wait_ge(qk_evac, i + 1)
                    hT_of(i + 1)
                pe.wait_ge(latTa_done, i + 1)
                pe.wait_ge(latTb_done, i + 1)
                pe.wait_ge(kpe_done, i + 1)
                for c in range(2):
                    for k in range(QR // P):
                        end = nc.tensor.matmul(UL[0:T, c, 0:QR], lhsT=qlatT[:, k, 0:T],
                                                rhs=g.w_qb[:, k, c * QR:(c + 1) * QR], start=k == 0,
                                                stop=k == QR // P - 1)
                end.then_inc(qmla_mm, 1)
                if not first:
                    pe.wait_ge(e5, i)
                for c, dst in enumerate((X, TB)):
                    for k in range(KR // P):
                        end = nc.tensor.matmul(dst[0:T, :], lhsT=ckvT[:, k, 0:T],
                                                rhs=g.w_kvb[:, k, c * 512:(c + 1) * 512], start=k == 0,
                                                stop=k == KR // P - 1)
                end.then_inc(kv_mm, 1)

            hT_of(0)
            tiles(pe, body)
            back(PT, 0)
            back(PT, 1)

        @block.scalar
        def _(act):
            def x_stats(i):
                T = width(i)
                act.wait_ge(x_in, 16 * i + 16)
                nc.scalar.activation(sq[0:T, :], x[0:T, :], ACT.Square, scale=D ** -0.5,
                                     accum_out=st[0:T, 0:1]).then_inc(xstat, 1)
                act.wait_ge(xstat, i + 1)
                nc.scalar.activation(st[0:T, 1:2], st[0:T, 0:1], ACT.Sqrt, bias=g.eps[0:T]).then_inc(xrms, 1)

            def back(i):
                T = width(i)
                cols = bass.ds(i * P, T)
                act.wait_ge(r1, i + 1)
                if not (isinstance(i, int) and i == 0):
                    act.wait_ge(st_ks, 16 * i)
                nc.scalar.activation(ksT[:, :, 0:T], TB[:, :].rearrange("p (j t) -> p j t", t=P)[:, :, 0:T],
                                     ACT.Copy).then_inc(e1, 1)
                act.wait_ge(r2, i + 1)
                if not (isinstance(i, int) and i == 0):
                    act.wait_ge(st_qm, 16 * i)
                nc.scalar.activation(qmT[:, 0:4, 0:T], X[0:MK, :].rearrange("p (j t) -> p j t", t=P)[:, :, 0:T],
                                     ACT.Copy).then_inc(e2, 1)
                act.wait_ge(r4, i + 1)
                nc.scalar.activation(g.kT_m[:, 0:4, cols],
                                     TB[0:MK, :].rearrange("p (j t) -> p j t", t=P)[:, :, 0:T],
                                     ACT.Copy).then_inc(e4, 1)
                act.wait_ge(r5, i + 1)
                nc.scalar.activation(g.kT_m[:, 4:8, cols],
                                     X[0:MK, :].rearrange("p (j t) -> p j t", t=P)[:, :, 0:T],
                                     ACT.Copy).then_inc(e5, 1)

            def body(i):
                T, first = width(i), isinstance(i, int) and i == 0
                act.wait_ge(lat_mm, i + 1)
                nc.scalar.activation(sq[0:T, 0:QR], UL[0:T, 0, 0:QR], ACT.Square, scale=QR ** -0.5,
                                     accum_out=st[0:T, 2:3])
                nc.scalar.activation(sq[0:T, QR:QR + KR], UL[0:T, 1, 0:KR], ACT.Square, scale=KR ** -0.5,
                                     accum_out=st[0:T, 3:4])
                nc.scalar.activation(sq[0:T, QR + KR:QR + KR + ROPE], UL[0:T, 1, KR:KR + ROPE], ACT.Square,
                                     scale=ROPE ** -0.5, accum_out=st[0:T, 4:5]).then_inc(lat_sq, 1)
                act.wait_ge(lat_sq, i + 1)
                nc.scalar.activation(st[0:T, 5:8], st[0:T, 2:5], ACT.Sqrt, bias=g.eps[0:T]).then_inc(lat_rms, 1)
                if not first:
                    back(i - 1)
                if not first:
                    act.wait_ge(st_k, 16 * i)
                act.wait_ge(q_mm, i + 1)
                nc.scalar.activation(qk[0:T, 0:SBH, :], U[0][0:T, :].rearrange("p (h d) -> p h d", d=SBD), ACT.Copy)
                act.wait_ge(k_mm, i + 1)
                nc.scalar.activation(qk[0:T, SBH:, :], U[1][0:T, :].rearrange("p (h d) -> p h d", d=SBD),
                                     ACT.Copy).then_inc(qk_evac, 1)
                act.wait_ge(qk_evac, i + 1)
                nc.scalar.activation(sq[0:T, :], qk[0:T, :, :].rearrange("p h d -> p (h d)"), ACT.Square,
                                     scale=SBD ** -0.5).then_inc(qk_sq, 1)
                act.wait_ge(latT_mm, i + 1)
                nc.scalar.activation(ckvT[:, :, 0:T], TB[:, 0:KR].rearrange("p (j t) -> p j t", t=P)[:, :, 0:T],
                                     ACT.Copy).then_inc(latTb_done, 1)
                act.wait_ge(qk_red, i + 1)
                nc.scalar.activation(sth[0:T, 16:32], sth[0:T, 0:16], ACT.Sqrt, bias=g.eps[0:T]
                                     ).then_inc(qk_rms, 1)
                if not last(i):
                    x_stats(i + 1)
                act.wait_ge(v_mm, i + 1)
                nc.scalar.activation(g.v_sb[0:T, i, :], U2[0:T, :], ACT.Copy).then_inc(v_evac, 1)
                act.wait_ge(qmla_mm, i + 1)
                nc.scalar.activation(qf[0:T, :, :].rearrange("p h d -> p (h d)").rearrange("p (c n) -> p c n", c=2),
                                     UL[0:T, :, 0:QR], ACT.Copy).then_inc(qm_evac, 1)
                act.wait_ge(kv_mm, i + 1)
                for c, src in enumerate((X, TB)):
                    heads = src[0:T, :].rearrange("p (h n) -> p h n", n=NOPE + MV)
                    nc.scalar.activation(kf[0:T, 4 * c:4 * c + 4, 0:NOPE], heads[:, :, 0:NOPE], ACT.Copy)
                    end = nc.scalar.activation(
                        g.v_m[0:T, i, c * 256:(c + 1) * 256].rearrange("p (h n) -> p h n", n=MV),
                        heads[:, :, NOPE:], ACT.Copy)
                end.then_inc(kv_evac, 1)
                act.wait_ge(mla_red, i + 1)
                nc.scalar.activation(sth[0:T, 24:48], sth[0:T, 0:24], ACT.Sqrt, bias=g.eps[0:T]
                                     ).then_inc(mla_rms, 1)

            x_stats(0)
            tiles(act, body)
            back(PT)

        @block.vector
        def _(dve):
            step = Steps(dve, dve_step)
            rope_c = lambda i, T: g.rope[0:T, i, 0:ROPE]
            rope_s = lambda i, T: g.rope[0:T, i, ROPE:2 * ROPE]

            def xn_of(i):
                T = width(i)
                dve.wait_ge(xrms, i + 1)
                nc.vector.reciprocal(st[0:T, 0:1], st[0:T, 1:2]).then_inc(xrec, 1)
                dve.wait_ge(xrec, i + 1)
                nc.vector.tensor_scalar(x[0:T, :], x[0:T, :], st[0:T, 0:1], None, ALU.mult).then_inc(xn_done, 1)

            def hT_of(i):
                T, b = width(i), 1 if last(i) else 0
                dve.wait_ge(ht_mm, i + 1)
                for k in range(KD):
                    end = nc.vector.tensor_scalar(hT[:, k, 0:T], U[k // 4][:, (k % 4) * P:(k % 4) * P + T],
                                                   g.scale_a[:, k, b:b + 1], g.modT[:, k, b:b + 1],
                                                   ALU.mult, ALU.add)
                end.then_inc(ht_done, 1)

            def back(i, part):
                T = width(i)
                if part == 0:
                    dve.wait_ge(r0, i + 1)
                    if not (isinstance(i, int) and i == 0):
                        dve.wait_ge(st_qs, 16 * i)
                    nc.vector.tensor_copy(qsT[:, :, 0:T], TA[:, :].rearrange("p (j t) -> p j t", t=P)[:, :, 0:T]
                                          ).then_inc(e0, 1)
                else:
                    dve.wait_ge(r3, i + 1)
                    if not (isinstance(i, int) and i == 0):
                        dve.wait_ge(st_qm, 16 * i)
                    nc.vector.tensor_copy(qmT[:, 4:8, 0:T],
                                          TA[0:MK, :].rearrange("p (j t) -> p j t", t=P)[:, :, 0:T]
                                          ).then_inc(e3, 1)

            def spread(ap, heads, width, T):
                return ap.unsqueeze(2).broadcast_to([T, heads, width])

            def body(i):
                T, first = width(i), isinstance(i, int) and i == 0
                dve.wait_ge(lat_rms, i + 1)
                step(nc.vector.reciprocal(st[0:T, 5:8], st[0:T, 5:8]))
                if not first:
                    dve.wait_ge(st_ckv, 16 * i)
                    dve.wait_ge(st_kpe, 16 * i)
                nc.vector.scalar_tensor_tensor(qlat[0:T, :], UL[0:T, 0, 0:QR], st[0:T, 5:6], row["g_qa"][0:T],
                                               ALU.mult, ALU.mult)
                nc.vector.scalar_tensor_tensor(ckv[0:T, :], UL[0:T, 1, 0:KR], st[0:T, 6:7], row["g_kva"][0:T],
                                               ALU.mult, ALU.mult).then_inc(lat_norm, 1)
                step(nc.vector.scalar_tensor_tensor(kpe[0:T, 0:ROPE], UL[0:T, 1, KR:KR + ROPE], st[0:T, 7:8],
                                                    row["g_mk_pe"][0:T], ALU.mult, ALU.mult))
                swapped = kpe[0:T, 0:ROPE].rearrange("p (a b) -> p a b", a=2)[:, ::-1, :]
                nc.vector.tensor_tensor(rot[0:T, 0, :].rearrange("p (a b) -> p a b", a=2), swapped,
                                        rope_s(i, T).rearrange("p (a b) -> p a b", a=2), ALU.mult)
                step(nc.vector.tensor_tensor(rot[0:T, 1, :], kpe[0:T, 0:ROPE], rope_c(i, T), ALU.mult))
                nc.vector.tensor_tensor(kpe[0:T, ROPE:2 * ROPE], rot[0:T, 0, :], rot[0:T, 1, :], ALU.add
                                        ).then_inc(kpe_done, 1)
                if not first:
                    back(i - 1, 0)
                    back(i - 1, 1)
                dve.wait_ge(latT_mm, i + 1)
                nc.vector.tensor_copy(qlatT[:, :, 0:T], TA[:, 0:QR].rearrange("p (j t) -> p j t", t=P)[:, :, 0:T]
                                      ).then_inc(latTa_done, 1)
                dve.wait_ge(qk_sq, i + 1)
                nc.vector.tensor_reduce(sth[0:T, 0:16], sq[0:T, :].rearrange("p (h d) -> p h d", d=SBD), AX.X,
                                        ALU.add).then_inc(qk_red, 1)
                dve.wait_ge(qk_rms, i + 1)
                step(nc.vector.reciprocal(sth[0:T, 16:32], sth[0:T, 16:32]))
                step(nc.vector.tensor_tensor(qk[0:T], qk[0:T], spread(sth[0:T, 16:32], 16, SBD, T), ALU.mult))
                for a, name in ((0, "g_sb_q"), (SBH, "g_sb_k")):
                    end = nc.vector.tensor_tensor(
                        qk[0:T, a:a + SBH, :], qk[0:T, a:a + SBH, :],
                        row[name][0:T].unsqueeze(1).broadcast_to([T, SBH, SBD]), ALU.mult)
                end.then_inc(qk_norm, 1)
                if not last(i):
                    xn_of(i + 1)
                    hT_of(i + 1)
                dve.wait_ge(qm_evac, i + 1)
                step(nc.vector.tensor_tensor(sq[0:T, 0:768], qf[0:T].rearrange("p h d -> p (h d)"),
                                             qf[0:T].rearrange("p h d -> p (h d)"), ALU.mult))
                sqh = sq[0:T, 0:768].rearrange("p (h d) -> p h d", d=MK)
                nc.vector.tensor_reduce(sth[0:T, 0:8], sqh[:, :, 0:NOPE], AX.X, ALU.add)
                step(nc.vector.tensor_reduce(sth[0:T, 16:24], sqh[:, :, NOPE:], AX.X, ALU.add))
                dve.wait_ge(kv_evac, i + 1)
                kn = sq[0:T, 0:512].rearrange("p (h d) -> p h d", d=NOPE)
                step(nc.vector.tensor_tensor(kn, kf[0:T, :, 0:NOPE], kf[0:T, :, 0:NOPE], ALU.mult))
                step(nc.vector.tensor_reduce(sth[0:T, 8:16], kn, AX.X, ALU.add))
                nc.vector.tensor_scalar(sth[0:T, 0:16], sth[0:T, 0:16], 1.0 / NOPE, None, ALU.mult)
                nc.vector.tensor_scalar(sth[0:T, 16:24], sth[0:T, 16:24], 1.0 / ROPE, None, ALU.mult
                                        ).then_inc(mla_red, 1)
                dve.wait_ge(mla_rms, i + 1)
                step(nc.vector.reciprocal(sth[0:T, 24:48], sth[0:T, 24:48]))
                nc.vector.tensor_tensor(qf[0:T, :, 0:NOPE], qf[0:T, :, 0:NOPE],
                                        spread(sth[0:T, 24:32], MH, NOPE, T), ALU.mult)
                nc.vector.tensor_tensor(kf[0:T, :, 0:NOPE], kf[0:T, :, 0:NOPE],
                                        spread(sth[0:T, 32:40], MH, NOPE, T), ALU.mult)
                step(nc.vector.tensor_tensor(qf[0:T, :, NOPE:], qf[0:T, :, NOPE:],
                                             spread(sth[0:T, 40:48], MH, ROPE, T), ALU.mult))
                gain = lambda name, w: row[name][0:T].unsqueeze(1).broadcast_to([T, MH, w])
                nc.vector.tensor_tensor(qf[0:T, :, 0:NOPE], qf[0:T, :, 0:NOPE], gain("g_mq_nope", NOPE), ALU.mult)
                nc.vector.tensor_tensor(kf[0:T, :, 0:NOPE], kf[0:T, :, 0:NOPE], gain("g_mk_nope", NOPE), ALU.mult)
                nc.vector.tensor_copy(kf[0:T, :, NOPE:],
                                      kpe[0:T, ROPE:2 * ROPE].unsqueeze(1).broadcast_to([T, MH, ROPE]))
                step(nc.vector.tensor_tensor(qf[0:T, :, NOPE:], qf[0:T, :, NOPE:], gain("g_mq_pe", ROPE), ALU.mult))
                half = ROPE // 2
                for a, b in ((0, half), (half, 0)):
                    end = nc.vector.tensor_tensor(
                        rot[0:T, :, a:a + half], qf[0:T, :, NOPE + b:NOPE + b + half],
                        rope_s(i, T)[:, a:a + half].unsqueeze(1).broadcast_to([T, MH, half]), ALU.mult)
                step(end)
                step(nc.vector.tensor_tensor(qf[0:T, :, NOPE:], qf[0:T, :, NOPE:],
                                             rope_c(i, T).unsqueeze(1).broadcast_to([T, MH, ROPE]), ALU.mult))
                nc.vector.tensor_tensor(qf[0:T, :, NOPE:], qf[0:T, :, NOPE:], rot[0:T], ALU.add
                                        ).then_inc(mla_norm, 1)

            dve.wait_ge(g.w_small_loaded, 48)
            xn_of(0)
            hT_of(0)
            tiles(dve, body, step)
            back(PT, 0)
            back(PT, 1)


def phase_cd(nc, io, g):
    with ExitStack() as stack:
        m = Memory(nc, stack)
        ROWG = P // DEC
        z = m.sb("c_z", [P, 4, SKEYS])
        v_s = m.sb("c_v", [P, PTILES, SBW])
        ckv_s = m.sb("c_ckv", [P, PTILES, KR])
        work = m.sb("c_work", [P, 4864])
        kc = work[:, 0:1024].rearrange("p (b n) -> p b n", b=2)
        cc = work[:, 1024:1536].rearrange("p (b n) -> p b n", b=2)
        kT4 = work[:, 1536:2560].rearrange("p (b j n) -> p b j n", b=2, j=4)
        kf = work[:, 2560:3328].rearrange("p (h n) -> p h n", h=MH)
        kTm = work[0:MK, 3328:4352].rearrange("p (h n) -> p h n", h=MH)
        sq = work[:, 4352:4864].rearrange("p (h n) -> p h n", h=MH)
        stick = work[:, 0:SKEYS + 1]
        beta = work[:, 2084:2084 + SKEYS]
        pc = m.sb("c_pc", [P, 2, ROPE])
        ccT = m.sb("c_ccT", [P, KR // P, P])
        ms = m.sb("c_ms", [P, 2 * MH])
        qbd = m.sb("c_qbd", [P, 4, 2 * DEC])
        qm = m.sb("c_qm", [MK, MH, DEC])
        ksn = m.sb("c_ksn", [P, 4, DEC])
        wT = m.sb("c_wT", [P, PTILES + 1, P])
        pcn = m.sb("c_pcn", [P, KR])
        pcT = m.sb("c_pcT", [P, KR // P, P])
        sm = m.sb("c_sm", [P, 8])
        o_s = m.sb("c_o", [DEC, D])
        A, B, C, DB, E, F = (m.ps(n, [P, 512]) for n in ("c_A", "c_B", "c_C", "c_D", "c_E", "c_F"))
        (kc0, kc1, cc0, cc1, pc0, pc1, q_in, v_in, ckv_in, z0, t1a, t1b, a_done, b_done, kn_mm, c_done, ms_done,
         rms_done, kn_done, t2, d_done, e_done, z_mm, z_done, masked, dve_step, pool_step, prob, tr, evA, evB,
         pv, o_done, pcn_done, pcT_mm, pcT_done, om, s_done, mx_done, st_o) = m.sems(
            "c_kc0 c_kc1 c_cc0 c_cc1 c_pc0 c_pc1 c_q_in c_v_in c_ckv_in c_zero c_t1a c_t1b c_a c_b c_kn_mm "
            "c_c c_ms c_rms c_kn c_t2 c_d c_e c_z_mm c_z_done c_masked c_dve_step c_pool_step c_prob c_tr c_evA "
            "c_evB c_pv c_o_done c_pcn_done c_pcT_mm c_pcT_done c_om c_s_done c_mx c_st_o")
        kc_in, cc_in, pc_in = (kc0, kc1), (cc0, cc1), (pc0, pc1)
        block = stack.enter_context(nc.Block())
        gain = g.rows[:, slice(*ROWS["g_mk_nope"])]
        w_nope = g.w_kvb[:].rearrange("p k (h n) -> p k h n", n=NOPE + MV)

        def tiles(engine, body, steps=None):
            body(0, 0, 0)
            body(1, 1, 0)
            if steps:
                per = steps.n
                steps.straight()
            with engine.Fori(1, PTILES // 2) as j:
                if steps:
                    steps.enter(j - 1, per)
                body(2 * j, 0, j)
                body(2 * j + 1, 1, j)
            if steps:
                steps.leave(PTILES // 2 - 1)

        def later(t, than=0):
            return not isinstance(t, int) or t > than

        GROUPS = (0, 2, 1, 3)
        BATCHES = [(b * 4, min(4, PTILES + 1 - b * 4)) for b in range((PTILES + 4) // 4)]

        def keys_of(t):
            return P if t < PTILES else DEC

        @block.sync
        def _(sp):
            sp.wait_ge(z0, 1)
            new = slice(SEQ, TOK)
            sp.dma_start(qbd[0:64, :, 0:DEC], g.qs_dram[:, 0:64, new].rearrange("a p t -> p a t")).then_inc(q_in, 16)
            sp.dma_start(qbd[64:P, :, DEC:], g.qs_dram[:, 64:P, new].rearrange("a p t -> p a t")).then_inc(q_in, 16)
            sp.dma_start(qm[:], g.qm_dram[:, :, new].rearrange("h p t -> p h t")).then_inc(q_in, 16)
            sp.dma_start(ksn[:], g.ks_dram[:, :, new].rearrange("a p t -> p a t")).then_inc(q_in, 16)

            def body(t, b, n):
                rows = bass.ds(t * P, P)
                if later(t, 1):
                    sp.wait_ge(t1a, t - 1)
                sp.dma_start(kc[:, b], io["cache_sb_k"][rows, :]).then_inc(kc_in[b], 16)
                if later(t, 1):
                    sp.wait_ge(t1b, t - 1)
                sp.dma_start(cc[:, b], io["cache_mla_ckv"][rows, :]).then_inc(cc_in[b], 16)
                if later(t, 1):
                    sp.wait_ge(kn_done, t - 1)
                sp.dma_start(pc[:, b], io["cache_mla_kpe"][rows, :]).then_inc(pc_in[b], 16)

            tiles(sp, body)
            sp.wait_ge(o_done, 4)
            sp.dma_start(g.o_dram[SEQ:TOK, :], o_s[:]).then_inc(st_o, 16)
            sp.wait_ge(st_o, 16)

        @block.gpsimd
        def _(pool):
            nc.gpsimd.memset(qbd[:], 0.0).then_inc(z0, 1)
            pool.wait_ge(z_done, PTILES + 1)
            nc.gpsimd.memset(stick[:, SKEYS:], 1.0).then_inc(pool_step, 1)
            pool.wait_ge(pool_step, 1)
            for a in range(ROWG):
                if a:
                    pool.wait_ge(masked, a)
                part = z[a * DEC:(a + 1) * DEC, 0:2, PAST:]
                nc.gpsimd.affine_select(out=part, in_=part, compare_op=ALU.is_gt, fill=NEG, base=0,
                                        pattern=[[0, 2], [-1, DEC]], channel_multiplier=1).then_inc(masked, 1)

        @block.tensor
        def _(pe):
            def finish_transposes(t):
                pe.wait_ge(kn_done, t + 1)
                if later(t):
                    pe.wait_ge(d_done, t)
                    pe.wait_ge(e_done, t)
                for c, dst in enumerate((DB, E)):
                    for j in range(4):
                        end = nc.tensor.transpose(dst[0:MK, j * P:(j + 1) * P], kf[:, 4 * c + j, :], g.ident[:])
                end.then_inc(t2, 1)

            def scores(t, keys_sb, keys_m, n):
                if later(t):
                    pe.wait_ge(z_done, t)
                out = F[:, :].rearrange("p (a k) -> p a k", k=P)
                for j in range(4):
                    r = (j % 2) * 2 * DEC
                    nc.tensor.matmul(out[r:r + 2 * DEC, j // 2, 0:n], lhsT=qbd[:, j, :], rhs=keys_sb(j),
                                     start=True, stop=True)
                for h in range(MH):
                    r = (h % ROWG) * DEC
                    end = nc.tensor.matmul(out[r:r + DEC, 2 + h // ROWG, 0:n], lhsT=qm[:, h, :], rhs=keys_m(h),
                                           start=True, stop=True, tile_position=(0, r))
                end.then_inc(z_mm, 1)

            def tile_scores(t, b):
                pe.wait_ge(a_done, t + 1)
                pe.wait_ge(d_done, t + 1)
                pe.wait_ge(e_done, t + 1)
                scores(t, lambda j: kT4[:, b, j, :], lambda h: kTm[:, h, :], P)

            def body(t, b, n):
                pe.wait_ge(kc_in[b], 16 * n + 16)
                if later(t):
                    pe.wait_ge(a_done, t)
                    pe.wait_ge(b_done, t)
                for j in range(4):
                    end = nc.tensor.transpose(A[:, j * P:(j + 1) * P], kc[:, b, j * P:(j + 1) * P], g.ident[:])
                end.then_inc(t1a, 1)
                pe.wait_ge(cc_in[b], 16 * n + 16)
                for j in range(KR // P):
                    end = nc.tensor.transpose(B[:, j * P:(j + 1) * P], cc[:, b, j * P:(j + 1) * P], g.ident[:])
                end.then_inc(t1b, 1)
                if later(t):
                    finish_transposes(t - 1)
                    pe.wait_ge(c_done, t)
                pe.wait_ge(b_done, t + 1)
                for k in range(KR // P):
                    end = nc.tensor.matmul(C[:, :], lhsT=ccT[:, k, :], rhs=w_nope[:, k, :, 0:NOPE],
                                           start=k == 0, stop=k == KR // P - 1)
                end.then_inc(kn_mm, 1)
                if later(t):
                    tile_scores(t - 1, 1 - b)

            pe.wait_ge(q_in, 64)
            tiles(pe, body)
            finish_transposes(PTILES - 1)
            tile_scores(PTILES - 1, 1)
            scores(PTILES, lambda j: ksn[:, j, :], lambda h: g.kT_m[:, h, SEQ:TOK], DEC)

            pe.wait_ge(v_in, 16)
            pe.wait_ge(ckv_in, 16)
            for n, a in enumerate(GROUPS):
                src = stick if a >= 2 else beta
                pe.wait_ge(prob, n + 1)
                for i, (t0, cnt) in enumerate(BATCHES):
                    dst = (A, B)[i % 2]
                    if i % 2 == 0:
                        pe.wait_ge(evA, 3 * n + i // 2) if 3 * n + i // 2 else None
                    else:
                        pe.wait_ge(evB, 2 * n + i // 2) if 2 * n + i // 2 else None
                    for j in range(cnt):
                        k = keys_of(t0 + j)
                        end = nc.tensor.transpose(dst[0:k, j * P:(j + 1) * P],
                                                  src[:, (t0 + j) * P:(t0 + j) * P + k], g.ident[:])
                    end.then_inc(tr, 1)
                pe.wait_ge(evA, 3 * n + 3)
                pe.wait_ge(evB, 2 * n + 2)
                if n:
                    pe.wait_ge(o_done, n)
                for t in range(PTILES + 1):
                    k = keys_of(t)
                    if a < 2:
                        v = v_s[:, t, a * 256:(a + 1) * 256] if t < PTILES else \
                            g.v_sb[0:k, PT, a * 256:(a + 1) * 256]
                    else:
                        v = ckv_s[:, t, :] if t < PTILES else g.ckv_new[0:k, :]
                    end = nc.tensor.matmul(C[:, 0:256], lhsT=wT[0:k, t, :], rhs=v, start=t == 0, stop=t == PTILES)
                end.then_inc(pv, 1)
                if a >= 2:
                    pe.wait_ge(pcn_done, a - 1)
                    for j in range(KR // P):
                        end = nc.tensor.transpose(E[:, j * P:(j + 1) * P], pcn[:, j * P:(j + 1) * P], g.ident[:])
                    end.then_inc(pcT_mm, 1)
                    pe.wait_ge(pcT_done, a - 1)
                    for j in range(ROWG):
                        h = (a - 2) * ROWG + j
                        for k in range(KR // P):
                            end = nc.tensor.matmul(F[0:DEC, j * MV:(j + 1) * MV],
                                                   lhsT=pcT[:, k, j * DEC:(j + 1) * DEC],
                                                   rhs=w_nope[:, k, h, NOPE:], start=k == 0,
                                                   stop=k == KR // P - 1)
                    end.then_inc(om, 1)

        @block.scalar
        def _(act):
            act.dma_start(v_s[:], io["cache_sb_v"].rearrange("(t p) n -> p t n", p=P)).then_inc(v_in, 16)
            act.dma_start(ckv_s[:], io["cache_mla_ckv"].rearrange("(t p) n -> p t n", p=P)).then_inc(ckv_in, 16)

            def evac_keys(t):
                act.wait_ge(t2, t + 1)
                if later(t):
                    act.wait_ge(z_mm, t)
                nc.scalar.activation(kTm[:, 4:8, :], E[0:MK, :].rearrange("p (j t) -> p j t", t=P), ACT.Copy
                                     ).then_inc(e_done, 1)

            def evac_scores(t, n):
                act.wait_ge(z_mm, t + 1)
                nc.scalar.activation(z[:, :, bass.ds(t * P, n)],
                                     F[:, :].rearrange("p (a k) -> p a k", k=P)[:, :, 0:n], ACT.Copy
                                     ).then_inc(z_done, 1)

            def body(t, b, n):
                act.wait_ge(t1b, t + 1)
                if later(t):
                    act.wait_ge(kn_mm, t)
                nc.scalar.activation(ccT[:], B[:, 0:KR].rearrange("p (j t) -> p j t", t=P), ACT.Copy
                                     ).then_inc(b_done, 1)
                if later(t):
                    evac_keys(t - 1)
                act.wait_ge(kn_mm, t + 1)
                nc.scalar.activation(kf[:, :, 0:NOPE], C[:, :].rearrange("p (h n) -> p h n", n=NOPE), ACT.Copy
                                     ).then_inc(c_done, 1)
                act.wait_ge(ms_done, t + 1)
                nc.scalar.activation(ms[:, MH:], ms[:, 0:MH], ACT.Sqrt, bias=g.eps[:], scale=1.0 / NOPE
                                     ).then_inc(rms_done, 1)
                if later(t):
                    evac_scores(t - 1, P)

            tiles(act, body)
            evac_keys(PTILES - 1)
            evac_scores(PTILES - 1, P)
            evac_scores(PTILES, DEC)

            act.wait_ge(masked, ROWG)
            act.wait_ge(pool_step, 1)
            act.wait_ge(z_done, PTILES + 1)
            for n, a in enumerate(GROUPS):
                if a < 2:
                    if n:
                        act.wait_ge(pv, n)
                    nc.scalar.activation(stick[:, 0:SKEYS], z[:, a, :], ACT.Sigmoid, scale=-SB_SCALE
                                         ).then_inc(s_done, 1)
                    nc.scalar.activation(beta[:], z[:, a, :], ACT.Sigmoid, scale=SB_SCALE).then_inc(s_done, 1)
                else:
                    act.wait_ge(mx_done, a - 1)
                    act.wait_ge(prob, n)
                    nc.scalar.activation(stick[:, 0:SKEYS], z[:, a, :], ACT.Exp, bias=sm[:, a:a + 1],
                                         scale=MLA_SCALE, accum_out=sm[:, 2 + a:3 + a]).then_inc(prob, 1)
                for i in (1, 3):
                    t0, cnt = BATCHES[i]
                    act.wait_ge(tr, 5 * n + i + 1)
                    if n:
                        act.wait_ge(pv, n)
                    nc.scalar.activation(wT[:, t0:t0 + cnt, :], B[:, 0:cnt * P].rearrange("p (j t) -> p j t", t=P),
                                         ACT.Copy).then_inc(evB, 1)
                if a >= 2:
                    act.wait_ge(pcT_mm, a - 1)
                    nc.scalar.activation(pcT[:], E[:, 0:KR].rearrange("p (j t) -> p j t", t=P), ACT.Copy
                                         ).then_inc(pcT_done, 1)

        @block.vector
        def _(dve):
            step = Steps(dve, dve_step)

            def evac_keys(t):
                dve.wait_ge(t2, t + 1)
                if later(t):
                    dve.wait_ge(z_mm, t)
                nc.vector.tensor_copy(kTm[:, 0:4, :], DB[0:MK, :].rearrange("p (j t) -> p j t", t=P)
                                      ).then_inc(d_done, 1)

            def body(t, b, n):
                dve.wait_ge(t1a, t + 1)
                if later(t, 1):
                    dve.wait_ge(z_mm, t - 1)
                nc.vector.tensor_copy(kT4[:, b], A[:, :].rearrange("p (j t) -> p j t", t=P)).then_inc(a_done, 1)
                if later(t):
                    evac_keys(t - 1)
                dve.wait_ge(c_done, t + 1)
                step(nc.vector.tensor_tensor(sq[:], kf[:, :, 0:NOPE], kf[:, :, 0:NOPE], ALU.mult))
                nc.vector.tensor_reduce(ms[:, 0:MH], sq[:], AX.X, ALU.add).then_inc(ms_done, 1)
                dve.wait_ge(pc_in[b], 16 * n + 16)
                nc.vector.tensor_copy(kf[:, :, NOPE:], pc[:, b, :].unsqueeze(1).broadcast_to([P, MH, ROPE]))
                dve.wait_ge(rms_done, t + 1)
                step(nc.vector.reciprocal(ms[:, MH:], ms[:, MH:]))
                step(nc.vector.tensor_tensor(kf[:, :, 0:NOPE], kf[:, :, 0:NOPE],
                                             ms[:, MH:].unsqueeze(2).broadcast_to([P, MH, NOPE]), ALU.mult))
                nc.vector.tensor_tensor(kf[:, :, 0:NOPE], kf[:, :, 0:NOPE],
                                        gain.unsqueeze(1).broadcast_to([P, MH, NOPE]), ALU.mult
                                        ).then_inc(kn_done, 1)

            tiles(dve, body, step)
            evac_keys(PTILES - 1)

            dve.wait_ge(z_done, PTILES + 1)
            for a in (2, 3):
                step(nc.vector.tensor_reduce(sm[:, 6:7], z[:, a, :], AX.X, ALU.max))
                nc.vector.tensor_scalar(sm[:, a:a + 1], sm[:, 6:7], -MLA_SCALE, None, ALU.mult
                                        ).then_inc(mx_done, 1)
                dve.wait_ge(mx_done, a - 1)
            sb = 0
            for n, a in enumerate(GROUPS):
                if a < 2:
                    dve.wait_ge(s_done, 2 * sb + 1)
                    back = stick[:, 0:SKEYS][:, ::-1]
                    step(nc.vector.tensor_tensor_scan(back, back, back, 1.0, ALU.mult, ALU.bypass))
                    dve.wait_ge(s_done, 2 * sb + 2)
                    nc.vector.tensor_tensor(beta[:], beta[:], stick[:, 1:], ALU.mult).then_inc(prob, 1)
                    sb += 1
                for i in (0, 2, 4):
                    t0, cnt = BATCHES[i]
                    dve.wait_ge(tr, 5 * n + i + 1)
                    if n:
                        dve.wait_ge(pv, n)
                    k = keys_of(t0)
                    nc.vector.tensor_copy(wT[0:k, t0:t0 + cnt, :],
                                          A[0:k, 0:cnt * P].rearrange("p (j t) -> p j t", t=P)).then_inc(evA, 1)
                dve.wait_ge(pv, n + 1)
                if a < 2:
                    for j in range(ROWG):
                        h = a * ROWG + j
                        end = nc.vector.tensor_copy(o_s[:, h * SBD:(h + 1) * SBD],
                                                    C[j * DEC:(j + 1) * DEC, j * SBD:(j + 1) * SBD])
                    end.then_inc(o_done, 1)
                else:
                    step(nc.vector.reciprocal(sm[:, 2 + a:3 + a], sm[:, 2 + a:3 + a]))
                    nc.vector.tensor_scalar(pcn[:], C[:, 0:256], sm[:, 2 + a:3 + a], None, ALU.mult
                                            ).then_inc(pcn_done, 1)
                    dve.wait_ge(om, a - 1)
                    nc.vector.tensor_copy(o_s[:, SBW + (a - 2) * 256:SBW + (a - 1) * 256], F[0:DEC, 0:256]
                                          ).then_inc(o_done, 1)


def phase_e(nc, io, g, latent):
    with ExitStack() as stack:
        n_ = "m_" if latent else "s_"
        m = Memory(nc, stack)
        UNITS = 2 * PT
        ORDER = list(range(PT))
        HEADS = SBH
        TR, PV, WBUFS = 2, 3, 4
        KROWS = MK if latent else P
        q = m.sb(n_ + "q", [KROWS, 2, SEQ])
        keys = None if latent else m.sb(n_ + "keys", [P, SBH // 2, SEQ])
        stick = m.sb(n_ + "stick", [P, 2, SEQ + 1])
        w = m.sb(n_ + "w", [P, WBUFS, SEQ])
        wT = m.sb(n_ + "wT", [P, 2, PT, P])
        o = m.sb(n_ + "o", [P, 2, PT, SBD])
        sm = m.sb(n_ + "sm", [P, WBUFS, 4])
        Z = [m.ps(f"{n_}Z{b}", [P, SEQ]) for b in range(2)]
        TA, TB = (m.ps(n_ + x, [P, 512]) for x in ("TA", "TB"))
        O = [m.ps(f"{n_}O{b}", [P, 512]) for b in range(2)]
        (zero, q0, q1, keys_in, z_mm, z_read, s_done, b_done, w_done, tr_a, tr_b, evA, evB, tr_end, pv, o_done,
         mx_done, dve_step, st_o0, st_o1) = m.sems(" ".join(n_ + x for x in (
             "zero q0 q1 keys_in z_mm z_read s_done b_done w_done tr_a tr_b evA evB tr_end pv o_done mx_done "
             "dve_step st_o0 st_o1").split()))
        q_in, st_o = (q0, q1), (st_o0, st_o1)
        block = stack.enter_context(nc.Block())
        mask = g.mask_mla if latent else g.mask_sb
        values = g.v_m if latent else g.v_sb
        BIG = [t >= 4 for t in ORDER] * 2

        def big(p, u):
            return p * sum(BIG) + sum(BIG[:u])

        def unit(p, u):
            return p * UNITS + u, ORDER[u % PT], u // PT

        def first(p, u, n=1):
            return isinstance(p, int) and p == 0 and u < n

        def units(engine, body, behind, steps=None, per=0):
            def turn(p, u):
                body(p, u)
                for lag, part in behind:
                    if u >= lag:
                        part(p, u - lag)
                    elif not (isinstance(p, int) and p == 0):
                        part(p - 1, u - lag + UNITS)

            for u in range(UNITS):
                turn(0, u)
            if steps:
                steps.straight()
            with engine.Fori(1, HEADS // 2) as p:
                if steps:
                    steps.enter(p - 1, per)
                for u in range(UNITS):
                    turn(p, u)
            if steps:
                steps.leave(HEADS // 2 - 1)
            for u in range(UNITS, UNITS + PV):
                for lag, part in behind:
                    if u - lag < UNITS:
                        part(HEADS // 2 - 1, u - lag)

        @block.sync
        def _(sp):
            def load_q(p, hh):
                if latent:
                    sp.dma_start(q[:, hh, :], g.qm_dram[2 * p + hh, :, 0:SEQ]).then_inc(q_in[hh], 16)
                else:
                    r = slice(hh * SBD, (hh + 1) * SBD)
                    sp.dma_start(q[r, hh, :], g.qs_dram[p, r, 0:SEQ]).then_inc(q_in[hh], 16)

            if not latent:
                sp.wait_ge(zero, 3)
                sp.dma_start(keys[:], g.ks_dram[:, :, 0:SEQ].rearrange("a p t -> p a t")).then_inc(keys_in, 16)
            for hh in range(2):
                load_q(0, hh)

            def store(p, hh):
                sp.wait_ge(o_done, p * UNITS + (hh + 1) * PT)
                col = bass.ds((SBW if latent else 0) + (2 * p + hh) * SBD, SBD)
                sp.dma_start(g.o_dram[0:SEQ, col].rearrange("(t p) c -> p t c", p=P), o[:, hh]
                             ).then_inc(st_o[hh], 16)

            with sp.Fori(0, HEADS // 2 - 1) as p:
                for hh in range(2):
                    sp.wait_ge(z_mm, p * UNITS + (hh + 1) * PT)
                    load_q(p + 1, hh)
                    store(p, hh)
            for hh in range(2):
                store(HEADS // 2 - 1, hh)
            for hh in range(2):
                sp.wait_ge(st_o[hh], 16 * (HEADS // 2))

        @block.gpsimd
        def _(pool):
            if not latent:
                nc.gpsimd.memset(q[SBD:P, 0, :], 0.0).then_inc(zero, 1)
                pool.wait_ge(zero, 1)
                nc.gpsimd.memset(q[0:SBD, 1, :], 0.0).then_inc(zero, 1)
                pool.wait_ge(zero, 2)
                nc.gpsimd.memset(stick[:, :, SEQ:], 1.0).then_inc(zero, 1)

        @block.tensor
        def _(pe):
            def transpose(p, u):
                n, t, hh = unit(p, u)
                pe.wait_ge(w_done, n + 1)
                if not first(p, u):
                    pe.wait_ge(evA, n)
                for j in range(min(4, t + 1)):
                    src = w[:, u % WBUFS, SEQ - (t + 1 - j) * P:SEQ - (t - j) * P]
                    end = nc.tensor.transpose(TA[:, j * P:(j + 1) * P], src, g.ident[:])
                end.then_inc(tr_a, 1)
                if BIG[u]:
                    nb = big(p, u)
                    if not (isinstance(nb, int) and nb == 0):
                        pe.wait_ge(evB, nb)
                    for j in range(4, t + 1):
                        src = w[:, u % WBUFS, SEQ - (t + 1 - j) * P:SEQ - (t - j) * P]
                        end = nc.tensor.transpose(TB[:, (j - 4) * P:(j - 3) * P], src, g.ident[:])
                    end.then_inc(tr_b, 1)

            def product(p, u):
                n, t, hh = unit(p, u)
                b = u % 2
                pe.wait_ge(evA, n + 1)
                if not first(p, u, 2):
                    pe.wait_ge(o_done, n - 1)
                col = (2 * p + hh) * SBD
                for j in range(t + 1):
                    if j == 4:
                        pe.wait_ge(evB, big(p, u) + 1)
                    end = nc.tensor.matmul(O[b][:, 0:SBD], lhsT=wT[:, b, j, :], rhs=values[:, j, bass.ds(col, SBD)],
                                           start=j == 0, stop=j == t)
                end.then_inc(pv, 1)

            def body(p, u):
                n, t, hh = unit(p, u)
                if u % PT == 0:
                    pe.wait_ge(q_in[hh], 16 * p + 16)
                if not first(p, u, 2):
                    pe.wait_ge(w_done if latent else z_read, n - 1)
                for c in range(0, (t + 1) * P, 512):
                    c1 = min(c + 512, (t + 1) * P)
                    rhs = g.kT_m[:, 2 * p + hh, c:c1] if latent else keys[:, p, c:c1]
                    nc.tensor.matmul(Z[u % 2][:, c:c1], lhsT=q[:, hh, t * P:(t + 1) * P], rhs=rhs, start=True,
                                     stop=c1 < (t + 1) * P)
                nc.tensor.matmul(Z[u % 2][:, t * P:(t + 1) * P], lhsT=g.identb[:], rhs=mask[:], start=False,
                                 stop=True).then_inc(z_mm, 1)

            if not latent:
                pe.wait_ge(keys_in, 16)
                pe.wait_ge(zero, 3)
            units(pe, body, ((TR, transpose), (PV, product)))

        @block.scalar
        def _(act):
            def out_a(p, u):
                n, t, hh = unit(p, u)
                act.wait_ge(tr_a, n + 1)
                if not first(p, u, 2):
                    act.wait_ge(pv, n - 1)
                cnt = min(4, t + 1)
                nc.scalar.activation(wT[:, u % 2, 0:cnt, :], TA[:, 0:cnt * P].rearrange("p (j t) -> p j t", t=P),
                                     ACT.Copy).then_inc(evA, 1)

            def body(p, u):
                n, t, hh = unit(p, u)
                b, bw, W = u % 2, u % WBUFS, (t + 1) * P
                act.wait_ge(z_mm, n + 1)
                if latent:
                    act.wait_ge(mx_done, n + 1)
                    if not first(p, u, WBUFS):
                        act.wait_ge(pv, n - (WBUFS - 1))
                        act.wait_ge(o_done, n - (WBUFS - 1))
                    nc.scalar.activation(w[:, bw, SEQ - W:], Z[b][:, 0:W], ACT.Exp, bias=sm[:, bw, 1:2],
                                         scale=MLA_SCALE, accum_out=sm[:, bw, 2:3]).then_inc(w_done, 1)
                else:
                    if not first(p, u, 2):
                        act.wait_ge(w_done, n - 1)
                    nc.scalar.activation(stick[:, b, SEQ - W:SEQ], Z[b][:, 0:W], ACT.Sigmoid, scale=-SB_SCALE
                                         ).then_inc(s_done, 1)
                    if not first(p, u, WBUFS):
                        act.wait_ge(pv, n - (WBUFS - 1))
                    nc.scalar.activation(w[:, bw, SEQ - W:], Z[b][:, 0:W], ACT.Sigmoid, scale=SB_SCALE
                                         ).then_inc(z_read, 1)

            units(act, body, ((TR, out_a),))

        @block.vector
        def _(dve):
            step = Steps(dve, dve_step)

            def evac_b(p, u):
                n, t, hh = unit(p, u)
                if BIG[u]:
                    dve.wait_ge(tr_b, big(p, u) + 1)
                    if not first(p, u, 2):
                        dve.wait_ge(pv, n - 1)
                    nc.vector.tensor_copy(wT[:, u % 2, 4:t + 1, :],
                                          TB[:, 0:(t - 3) * P].rearrange("p (j t) -> p j t", t=P)).then_inc(evB, 1)

            def out(p, u):
                n, t, hh = unit(p, u)
                b, bw = u % 2, u % WBUFS
                dve.wait_ge(pv, n + 1)
                if u % PT == 0 and not (isinstance(p, int) and p == 0):
                    dve.wait_ge(st_o[hh], 16 * p)
                if latent:
                    step(nc.vector.reciprocal(sm[:, bw, 3:4], sm[:, bw, 2:3]))
                    nc.vector.tensor_scalar(o[:, hh, t, :], O[b][:, 0:SBD], sm[:, bw, 3:4], None, ALU.mult
                                            ).then_inc(o_done, 1)
                else:
                    nc.vector.tensor_copy(o[:, hh, t, :], O[b][:, 0:SBD]).then_inc(o_done, 1)

            def body(p, u):
                n, t, hh = unit(p, u)
                b, bw, W = u % 2, u % WBUFS, (t + 1) * P
                if latent:
                    dve.wait_ge(z_mm, n + 1)
                    step(nc.vector.tensor_reduce(sm[:, bw, 0:1], Z[b][:, 0:W], AX.X, ALU.max))
                    if not first(p, u, WBUFS):
                        dve.wait_ge(w_done, n - (WBUFS - 1))
                    nc.vector.tensor_scalar(sm[:, bw, 1:2], sm[:, bw, 0:1], -MLA_SCALE, None, ALU.mult
                                            ).then_inc(mx_done, 1)
                else:
                    dve.wait_ge(s_done, n + 1)
                    back = stick[:, b, SEQ - W:SEQ][:, ::-1]
                    step(nc.vector.tensor_tensor_scan(back, back, back, 1.0, ALU.mult, ALU.bypass))
                    dve.wait_ge(z_read, n + 1)
                    nc.vector.tensor_tensor(w[:, bw, SEQ - W:], w[:, bw, SEQ - W:], stick[:, b, SEQ - W + 1:],
                                            ALU.mult).then_inc(w_done, 1)

            if not latent:
                dve.wait_ge(zero, 3)
            units(dve, body, ((TR, evac_b), (PV, out)), step, UNITS * (2 if latent else 1))


def phase_f(nc, io, g):
    with ExitStack() as stack:
        m = Memory(nc, stack)
        wo = m.sb("f_wo", [P, KD, D])
        wr = m.sb("f_wr", [P, KD, NG + NE])
        rows = m.sb("f_rows", [P, 3, 2, D])
        o = m.sb("f_o", [P, D])
        oT = m.sb("f_oT", [P, KD, P])
        xr = m.sb("f_xr", [P, D])
        h2 = m.sb("f_h2", [P, D])
        h2T = m.sb("f_h2T", [P, 2, KD, P])
        sq = m.sb("f_sq", [P, D])
        st = m.sb("f_st", [P, 3])
        zero = m.sb("f_zero", [1, D])
        LROWS = NE * REGION // P
        rown = m.sb("f_rown", [P, LROWS], I32)
        padt = m.sb("f_padt", [P, LROWS], I32)
        rowf = m.sb("f_rowf", [P, LROWS])
        pad = m.sb("f_pad", [P, LROWS, 2], U32)
        A = m.ps("f_A", [P, D])
        B = m.ps("f_B", [P, D])
        C = m.ps("f_C", [P, D])
        R = m.ps("f_R", [P, 512])
        (w_in, r_in, o_in, x_in, z0, z_out, row_mm, row_done, oT_mm, oT_done, pr_mm, x2_done, ssq, rms, h2_done,
         h2T_mm, h2T_done, rt_mm, rt_done, st_h2, dve_step, pool_step, pad_done) = m.sems(
            "f_w_in f_r_in f_o_in f_x_in f_z0 f_z_out f_row_mm f_row_done f_oT_mm f_oT_done f_pr_mm f_x2_done "
            "f_ssq f_rms f_h2_done f_h2T_mm f_h2T_done f_rt_mm f_rt_done f_st_h2 f_dve_step f_pool_step f_pad_done")
        block = stack.enter_context(nc.Block())
        bias = g.rows[:, ROWS["b_rg"][0]:ROWS["b_re"][1]]

        def last(i):
            return isinstance(i, int) and i == PT

        def width(i):
            return DEC if last(i) else P

        FIRST = 4

        def tiles(engine, parts, steps=None, per=0):
            def step(i, odd):
                for lag, part in parts:
                    if not isinstance(i, int) or 0 <= i - lag <= PT:
                        part(i - lag, (odd + lag) % 2)

            for i in range(FIRST):
                step(i, i % 2)
            if steps:
                steps.straight()
            with engine.Fori(FIRST // 2, PT // 2) as j:
                if steps:
                    steps.enter(j - FIRST // 2, 2 * per)
                for odd in range(2):
                    step(j * 2 + odd, odd)
            if steps:
                steps.leave((PT - FIRST) // 2)
            for i in range(PT, PT + 1 + max(lag for lag, _ in parts)):
                step(i, i % 2)

        def later(i):
            return not (isinstance(i, int) and i == 0)

        SPREADS = [(rows[:, 0, b, :], g.modT[:, 16:24, b]) for b in range(2)] + \
                  [(rows[:, 1, b, :], g.scale_m[:, :, b]) for b in range(2)] + \
                  [(rows[:, 2, b, :], g.modT[:, 24:32, b]) for b in range(2)] + \
                  [(g.gate_m[:, b, :], g.modT[:, 40:48, b]) for b in range(2)]

        @block.sync
        def _(sp):
            sp.dma_start(wo[:], io["w_out"].rearrange("(k p) n -> p k n", p=P)).then_inc(w_in, 16)
            sp.dma_start(wr[:, :, 0:NG], io["w_rg"].rearrange("(k p) n -> p k n", p=P)).then_inc(r_in, 16)
            sp.dma_start(wr[:, :, NG:], io["w_re"].rearrange("(k p) n -> p k n", p=P)).then_inc(r_in, 16)
            sp.wait_ge(z0, 1)
            sp.wait_ge(pad_done, 1)
            sp.dma_start(g.h2_dram[PAD:PAD + 1, :], zero[:]).then_inc(z_out, 16)
            sp.dma_start(g.list_dram.rearrange("(p n) o -> p n o", p=P), pad[:]).then_inc(z_out, 16)

            def store(i):
                sp.wait_ge(h2_done, i + 1)
                sp.dma_start(g.h2_dram[bass.ds(i * P, width(i)), :], h2[0:width(i), :]).then_inc(st_h2, 16)

            def body(i, odd):
                T = width(i)
                if later(i):
                    sp.wait_ge(oT_mm, i)
                sp.dma_start(o[0:T, :], g.o_dram[bass.ds(i * P, T), :]).then_inc(o_in, 16)
                if later(i):
                    sp.wait_ge(x2_done, i)
                x = io["x_sample"] if last(i) else io["x_prompt"][bass.ds(i * P, P), :]
                sp.dma_start(xr[0:T, :], x).then_inc(x_in, 16)
                if later(i):
                    store(i - 1)

            tiles(sp, ((0, body),))
            store(PT)
            sp.wait_ge(st_h2, 16 * NT)
            sp.wait_ge(z_out, 32)

        @block.gpsimd
        def _(pool):
            nc.gpsimd.iota(rown[:], pattern=[[1, LROWS]], base=0, channel_multiplier=LROWS).then_inc(pool_step, 1)
            pool.wait_ge(pool_step, 1)
            nc.gpsimd.iota(padt[:], pattern=[[0, LROWS]], base=PAD, channel_multiplier=0).then_inc(pool_step, 1)
            pool.wait_ge(pool_step, 2)
            nc.gpsimd.memset(zero[:], 0.0).then_inc(z0, 1)

        @block.tensor
        def _(pe):
            for n, (_, col) in enumerate(SPREADS):
                dst = (A, B, C)[n % 3]
                if n >= 3:
                    pe.wait_ge(row_done, n - 2)
                for k in range(KD):
                    end = nc.tensor.transpose(dst[:, k * P:(k + 1) * P], col[:, k:k + 1].broadcast_to([P, P]),
                                              g.ident[:])
                end.then_inc(row_mm, 1)
            pe.wait_ge(row_done, len(SPREADS))

            def turned(i, odd):
                T = width(i)
                pe.wait_ge(o_in, 16 * i + 16)
                if later(i):
                    pe.wait_ge(oT_done, i)
                for k in range(KD):
                    end = nc.tensor.transpose(A[:, k * P:k * P + T], o[0:T, k * P:(k + 1) * P], g.ident[0:T, 0:T])
                end.then_inc(oT_mm, 1)

            def projected(i, odd):
                T = width(i)
                if later(i):
                    pe.wait_ge(x2_done, i)
                pe.wait_ge(oT_done, i + 1)
                if not later(i):
                    pe.wait_ge(w_in, 16)
                for c in range(2):
                    for k in range(KD):
                        end = nc.tensor.matmul(C[0:T, c * 512:(c + 1) * 512], lhsT=oT[:, k, 0:T],
                                               rhs=wo[:, k, c * 512:(c + 1) * 512], start=k == 0, stop=k == KD - 1)
                end.then_inc(pr_mm, 1)

            def normed_turned(i, odd):
                T = width(i)
                pe.wait_ge(h2_done, i + 1)
                if later(i):
                    pe.wait_ge(h2T_done, i)
                for k in range(KD):
                    end = nc.tensor.transpose(B[:, k * P:k * P + T], h2[0:T, k * P:(k + 1) * P],
                                              g.ident[0:T, 0:T])
                end.then_inc(h2T_mm, 1)

            def routed(i, odd):
                T = width(i)
                pe.wait_ge(h2T_done, i + 1)
                if later(i):
                    pe.wait_ge(rt_done, i)
                for k in range(KD):
                    end = nc.tensor.matmul(R[0:T, 0:NG + NE], lhsT=h2T[:, odd, k, 0:T], rhs=wr[:, k, :],
                                           start=k == 0, stop=k == KD - 1)
                end.then_inc(rt_mm, 1)

            pe.wait_ge(r_in, 32)
            tiles(pe, ((0, turned), (2, normed_turned), (3, routed), (0, projected)))

        @block.scalar
        def _(act):
            for n, (dst, _) in enumerate(SPREADS):
                act.wait_ge(row_mm, n + 1)
                nc.scalar.activation(dst, (A, B, C)[n % 3][:], ACT.Copy).then_inc(row_done, 1)

            def o_out(i, odd):
                T = width(i)
                act.wait_ge(oT_mm, i + 1)
                if later(i):
                    act.wait_ge(pr_mm, i)
                nc.scalar.activation(oT[:, :, 0:T], A[:].rearrange("p (k t) -> p k t", t=P)[:, :, 0:T], ACT.Copy
                                     ).then_inc(oT_done, 1)

            def h2_out(i, odd):
                T = width(i)
                act.wait_ge(h2T_mm, i + 1)
                if not isinstance(i, int) or i > 1:
                    act.wait_ge(rt_mm, i - 1)
                nc.scalar.activation(h2T[:, odd, :, 0:T],
                                     B[:].rearrange("p (k t) -> p k t", t=P)[:, :, 0:T], ACT.Copy
                                     ).then_inc(h2T_done, 1)

            def norm(i, odd):
                T = width(i)
                act.wait_ge(x2_done, i + 1)
                nc.scalar.activation(sq[0:T], g.x2[0:T, i, :], ACT.Square, scale=D ** -0.5,
                                     accum_out=st[0:T, 0:1]).then_inc(ssq, 1)
                act.wait_ge(ssq, i + 1)
                nc.scalar.activation(st[0:T, 1:2], st[0:T, 0:1], ACT.Sqrt, bias=g.eps[0:T]).then_inc(rms, 1)

            tiles(act, ((0, o_out), (2, h2_out), (1, norm)))

        @block.vector
        def _(dve):
            step = Steps(dve, dve_step)
            step(nc.vector.memset(g.logits[:], 0.0))
            dve.wait_ge(pool_step, 2)
            step(nc.vector.tensor_scalar(rown[:], rown[:], P - 1, None, ALU.bitwise_and))
            step(nc.vector.tensor_scalar(rowf[:], rown[:], float(2 * TOK), None, ALU.add))
            step(nc.vector.tensor_copy(pad[:, :, 0], padt[:]))
            nc.vector.tensor_copy(pad[:, :, 1], rowf[:]).then_inc(pad_done, 1)
            dve.wait_ge(row_done, len(SPREADS))

            def logits(i, odd):
                T = width(i)
                dve.wait_ge(rt_mm, i + 1)
                nc.vector.tensor_tensor(g.logits[0:T, i, :], R[0:T, 0:NG + NE], bias[0:T], ALU.add
                                        ).then_inc(rt_done, 1)

            def body(i, odd):
                T, b = width(i), 1 if last(i) else 0
                dve.wait_ge(pr_mm, i + 1)
                step(nc.vector.tensor_tensor(g.x2[0:T, i, :], C[0:T], rows[0:T, 0, b, :], ALU.mult))
                dve.wait_ge(x_in, 16 * i + 16)
                nc.vector.tensor_tensor(g.x2[0:T, i, :], g.x2[0:T, i, :], xr[0:T], ALU.add).then_inc(x2_done, 1)
                dve.wait_ge(rms, i + 1)
                step(nc.vector.reciprocal(st[0:T, 2:3], st[0:T, 1:2]))
                if later(i):
                    dve.wait_ge(h2T_mm, i)
                    dve.wait_ge(st_h2, 16 * i)
                step(nc.vector.scalar_tensor_tensor(h2[0:T], g.x2[0:T, i, :], st[0:T, 2:3], rows[0:T, 1, b, :],
                                                    ALU.mult, ALU.mult))
                nc.vector.tensor_tensor(h2[0:T], h2[0:T], rows[0:T, 2, b, :], ALU.add).then_inc(h2_done, 1)

            tiles(dve, ((3, logits), (0, body)), step, 3)


def phase_r(nc, io, g):
    with ExitStack() as stack:
        m = Memory(nc, stack)
        gm = m.sb("r_gm", [P, NT])
        ex = m.sb("r_ex", [P, NT, NG])
        den = m.sb("r_den", [P, NT])
        pg = m.sb("r_pg", [P, NT])
        eq = m.sb("r_eq", [P, NT, EPG])
        sc = m.sb("r_sc", [P, NT])
        og = m.sb("r_og", [P, NT, NG])
        oe = [m.sb(f"r_oe{k}", [P, NT, EPG]) for k in range(2)]
        full = m.sb("r_full", [P, NT, NG, EPG])
        e_in = m.sb("r_e_in", [P, NT, EPG])
        v = [m.sb(f"r_v{k}", [P, NT]) for k in range(2)]
        pick = [m.sb(f"r_pick{k}", [P, NT, NE]) for k in range(2)]
        both = m.sb("r_both", [P, NT, NE])
        cum = m.sb("r_cum", [P, NT + 1, NE])
        rank = m.sb("r_rank", [P, NT, NE])
        tmp = m.sb("r_tmp", [P, NT, NE])
        rk = m.sb("r_rk", [P, NT])
        ei = m.sb("r_ei", [P, NT])
        dd = m.sb("r_dd", [P, NT])
        valid = m.sb("r_valid", [P, NT])
        count = m.sb("r_count", [P, NE])
        cmax = m.sb("r_cmax", [P, 1])
        i32 = m.sb("r_i32", [P, NE], I32)
        dest = m.sb("r_dest", [P, 2, NT], U32)
        idx = m.sb("r_idx", [P, NE])
        rev = m.sb("r_rev", [P, EPG])
        pair = m.sb("r_pair", [P, 2, NT, 2], U32)
        ranks = m.ps("r_ranks", [P, 512])
        counts = m.ps("r_counts", [P, 512])
        dve_step, pool_step, diff, expd, picked, ranked, placed, listed = m.sems(
            "r_dve_step r_pool_step r_diff r_expd r_picked r_ranked r_placed r_listed")
        block = stack.enter_context(nc.Block())

        @block.sync
        def _(sp):
            for e in range(2):
                load_gate_up(nc, io, g, sp, e, e, g.wgu_in[e])
                load_down(nc, io, g, sp, e, e, g.wd_in[e])

        def over(ap, n):
            return ap.unsqueeze(2).broadcast_to([P, NT, n])

        @block.gpsimd
        def _(pool):
            step = Steps(pool, pool_step)
            step(nc.gpsimd.iota(i32[:], pattern=[[1, NE]], base=0, channel_multiplier=0))
            for k in range(2):
                step(nc.gpsimd.iota(pair[:, k, :, 0], pattern=[[P, NT]], base=0, channel_multiplier=1))
                step(nc.gpsimd.iota(pair[:, k, :, 1], pattern=[[P, NT]], base=k * TOK, channel_multiplier=1))
            step(nc.gpsimd.memset(valid[:], 1.0))
            step(nc.gpsimd.memset(valid[:, PT:], 0.0))
            step(nc.gpsimd.memset(valid[0:DEC, PT:], 1.0))
            pool.wait_ge(placed, 1)
            for k in range(2):
                for i in range(NT):
                    T = P if i < PT else DEC
                    nc.gpsimd.indirect_dma_start(out=g.list_dram[:, :],
                                                 out_offset=bass.IndirectOffsetOnAxis(ap=dest[0:T, k, i:i + 1],
                                                                                      axis=0),
                                                 in_=pair[0:T, k, i, :], in_offset=None).then_inc(listed, 16)
            pool.wait_ge(listed, 2 * 16 * NT)

        @block.tensor
        def _(pe):
            pe.wait_ge(picked, 1)
            flat = lambda ap: ap.rearrange("p i e -> p (i e)")
            nc.tensor.matmul(ranks[:, 0:NT * NE], lhsT=g.tri[:], rhs=flat(both[:]), start=True, stop=False)
            nc.tensor.matmul(ranks[:, 0:NT * NE], lhsT=g.ones[:], rhs=flat(cum[:, 0:NT, :]), start=False, stop=True)
            nc.tensor.matmul(counts[:, 0:NE], lhsT=g.ones[:], rhs=cum[:, NT, :], start=True, stop=True
                             ).then_inc(ranked, 1)

        @block.scalar
        def _(act):
            act.wait_ge(diff, 1)
            nc.scalar.activation(ex[:], ex[:], ACT.Exp).then_inc(expd, 1)
            act.wait_ge(diff, 2)
            nc.scalar.activation(v[1][:], v[1][:], ACT.Exp).then_inc(expd, 1)

        @block.vector
        def _(dve):
            step = Steps(dve, dve_step)
            V = nc.vector
            dve.wait_ge(pool_step, 8)
            step(V.tensor_copy(idx[:], i32[:]))
            step(V.tensor_scalar(rev[:], idx[:, 0:EPG], -1.0, float(EPG), ALU.mult, ALU.add))
            lg = g.logits[:, :, 0:NG]
            le = g.logits[:, :, NG:].rearrange("p i (a e) -> p i a e", e=EPG)

            def first_max(out, values, top, n):
                r = rev[:, 0:n].unsqueeze(1).broadcast_to([P, NT, n])
                step(V.tensor_reduce(top, values, AX.X, ALU.max))
                step(V.tensor_tensor(eq[:, :, 0:n], values, over(top, n), ALU.is_equal))
                step(V.tensor_tensor(eq[:, :, 0:n], eq[:, :, 0:n], r, ALU.mult))
                step(V.tensor_reduce(sc[:], eq[:, :, 0:n], AX.X, ALU.max))
                step(V.tensor_tensor(out, eq[:, :, 0:n], over(sc[:], n), ALU.is_equal))

            first_max(og[:], lg, gm[:], NG)
            V.tensor_tensor(ex[:], lg, over(gm[:], NG), ALU.subtract).then_inc(diff, 1)
            step(V.tensor_tensor(full[:], le, og[:].unsqueeze(3).broadcast_to([P, NT, NG, EPG]), ALU.mult))
            step(V.tensor_reduce(e_in[:], full[:].rearrange("p i a e -> p i e a"), AX.X, ALU.add))
            first_max(oe[0][:], e_in[:], v[0][:], EPG)
            step(V.scalar_tensor_tensor(e_in[:].rearrange("p i e -> p (i e)"),
                                        oe[0][:].rearrange("p i e -> p (i e)"), 3.0 * NEG,
                                        e_in[:].rearrange("p i e -> p (i e)"), ALU.mult, ALU.add))
            first_max(oe[1][:], e_in[:], v[1][:], EPG)
            V.tensor_tensor(v[1][:], v[1][:], v[0][:], ALU.subtract).then_inc(diff, 1)
            dve.wait_ge(expd, 2)
            step(V.tensor_reduce(den[:], ex[:], AX.X, ALU.add))
            step(V.tensor_scalar(pg[:], v[1][:], 1.0, None, ALU.add))
            step(V.tensor_tensor(den[:], den[:], pg[:], ALU.mult))
            step(V.reciprocal(g.weight[:, 0, :], den[:]))
            step(V.tensor_tensor(g.weight[:, 1, :], g.weight[:, 0, :], v[1][:], ALU.mult))
            for k in range(2):
                p4 = pick[k][:].rearrange("p i (a e) -> p i a e", e=EPG)
                step(V.tensor_tensor(oe[k][:], oe[k][:], over(valid[:], EPG), ALU.mult))
                step(V.tensor_tensor(p4, og[:].unsqueeze(3).broadcast_to([P, NT, NG, EPG]),
                                     oe[k][:].unsqueeze(2).broadcast_to([P, NT, NG, EPG]), ALU.mult))
            step(V.memset(cum[:, 0, :], 0.0))
            step(V.tensor_tensor(both[:], pick[0][:], pick[1][:], ALU.add))
            for i in range(NT):
                end = V.tensor_tensor(cum[:, i + 1, :], cum[:, i, :], both[:, i, :], ALU.add)
                if i < NT - 1:
                    step(end)
            end.then_inc(picked, 1)
            dve.wait_ge(ranked, 1)
            step(V.tensor_copy(rank[:], ranks[:, 0:NT * NE].rearrange("p (i e) -> p i e", e=NE)))
            step(V.tensor_copy(count[:], counts[:, 0:NE]))
            step(V.tensor_copy(g.count[:], count[:]))
            step(V.tensor_reduce(cmax[:], count[:], AX.X, ALU.max))
            step(V.tensor_copy(g.longest[:], cmax[:]))
            for k in range(2):
                step(V.tensor_tensor(tmp[:], pick[k][:], rank[:], ALU.mult))
                step(V.tensor_reduce(rk[:], tmp[:], AX.X, ALU.add))
                step(V.tensor_tensor(tmp[:], pick[k][:], idx[:].unsqueeze(1).broadcast_to([P, NT, NE]), ALU.mult))
                step(V.tensor_reduce(ei[:], tmp[:], AX.X, ALU.add))
                step(V.scalar_tensor_tensor(dd[:], ei[:], float(REGION), rk[:], ALU.mult, ALU.add))
                end = V.tensor_copy(dest[:, k, :], dd[:])
                if k == 0:
                    step(end)
            end.then_inc(placed, 1)


def load_gate_up(nc, io, g, engine, e, b, sem):
    engine.dma_start(g.w_gate[:, b], io["w_gate"][e].rearrange("(k p) n -> p k n", p=P)).then_inc(sem, 16)
    engine.dma_start(g.w_up[:, b], io["w_up"][e].rearrange("(k p) n -> p k n", p=P)).then_inc(sem, 16)


def load_down(nc, io, g, engine, e, b, sem):
    engine.dma_start(g.w_down[:, b], io["w_down"][e].rearrange("(k p) n -> p k n", p=P)).then_inc(sem, 16)


def phase_g(nc, io, g):
    with ExitStack() as stack:
        m = Memory(nc, stack)
        FT = DE // P
        TURN = 4
        wg, wu, wd = g.w_gate, g.w_up, g.w_down
        ix = [m.sb(f"g_ix{r}", [P, 2], U32) for r in range(TURN)]
        sl = [m.sb(f"g_sl{b}", [P, 2], U32) for b in range(2)]
        xg = m.sb("g_xg", [P, TURN, D])
        xT = m.sb("g_xT", [P, KD, P])
        sig = m.sb("g_sig", [P, FT, P])
        hid = m.sb("g_hid", [P, 2, FT, P])
        y = m.sb("g_y", [P, 2, D])
        X = m.ps("g_X", [P, D])
        GU = [m.ps(f"g_GU{b}", [P, 2 * FT, P]) for b in range(2)]
        Y = [m.ps(f"g_Y{b}", [P, D]) for b in range(2)]
        xT_mm, xT_done, gu_mm, sig_done, hid_done, dn_mm, y_done, st_y, dve_step, started = m.sems(
            "g_xT_mm g_xT_done g_gu_mm g_sig_done g_hid_done g_dn_mm g_y_done g_st_y g_dve_step g_started")
        sl_in = m.sems("g_sl0 g_sl1")
        wgu_in, wd_in = g.wgu_in, g.wd_in
        ix_in = m.sems("g_ix_in0 g_ix_in1 g_ix_in2 g_ix_in3")
        xg_in = m.sems("g_xg_in0 g_xg_in1 g_xg_in2 g_xg_in3")
        (l_free, l_w, l_ix, l_xg, l_xT_mm, l_xT, l_gu, l_sig, l_hid, l_dn, l_y, l_st, l_step) = m.sems(
            "l_free l_w l_ix l_xg l_xT_mm l_xT l_gu l_sig l_hid l_dn l_y l_st l_step")
        block = stack.enter_context(nc.Block())

        def experts(engine, parts, steps=None, per=0):
            def step(j, r):
                for lag, part in parts:
                    if r >= lag:
                        part(j * TURN + (r - lag), j, r - lag)
                    elif not (isinstance(j, int) and j == 0):
                        part(j * TURN + (r - lag), j - 1, r - lag + TURN)

            for r in range(TURN):
                step(0, r)
            if steps:
                steps.straight()
            with engine.Fori(1, NE // TURN) as j:
                if steps:
                    steps.enter(j - 1, per)
                for r in range(TURN):
                    step(j, r)
            if steps:
                steps.leave(NE // TURN - 1)
            for e in range(NE, NE + max(lag for lag, _ in parts)):
                for lag, part in parts:
                    if e - lag < NE:
                        part(e - lag, (e - lag) // TURN, (e - lag) % TURN)

        def later(e, than=0):
            return not isinstance(e, int) or e > than

        def use(j, r):
            return j * (TURN // 2) + r // 2

        def long_lists(engine, body):
            longest = engine.value_load(g.longest[0:1, 0:1], min_val=0, max_val=TOK)
            done = engine.alloc_register("done")
            engine.reg_mov(done, 0)
            with engine.If(longest > P):
                with engine.Fori(0, NE) as e:
                    count = engine.value_load(g.count[0:1, bass.ds(e, 1)], min_val=0, max_val=TOK)
                    with engine.Fori(1, REGION // P) as r:
                        with engine.If(count > r * P):
                            body(e, r * P, engine.snap(done))
                            engine.reg_add(done, done, 1)

        def scatter(pool, b, sem):
            nc.gpsimd.indirect_dma_start(out=g.y_dram[:, :], in_=y[:, b, :], in_offset=None,
                                         out_offset=bass.IndirectOffsetOnAxis(ap=sl[b][:, 1:2], axis=0)
                                         ).then_inc(sem, 16)

        def gather(pool, r, sem):
            nc.gpsimd.indirect_dma_start(out=xg[:, r, :], out_offset=None, in_=g.h2_dram[:, :],
                                         in_offset=bass.IndirectOffsetOnAxis(ap=ix[r][:, 0:1], axis=0)
                                         ).then_inc(sem, 16)

        def transposes(r):
            for k in range(KD):
                end = nc.tensor.transpose(X[:, k * P:(k + 1) * P], xg[:, r, k * P:(k + 1) * P], g.ident[:])
            return end

        def gate_up(b):
            for f in range(2 * FT):
                w = (wg, wu)[f // FT]
                for k in range(KD):
                    end = nc.tensor.matmul(GU[b][:, f, :], lhsT=w[:, b, k, (f % FT) * P:(f % FT + 1) * P],
                                           rhs=xT[:, k, :], start=k == 0, stop=k == KD - 1)
            return end

        def down(b):
            for c in range(2):
                for k in range(FT):
                    end = nc.tensor.matmul(Y[b][:, c * 512:(c + 1) * 512], lhsT=hid[:, b, k, :],
                                           rhs=wd[:, b, k, c * 512:(c + 1) * 512], start=k == 0, stop=k == FT - 1)
            return end

        @block.sync
        def _(sp):
            def list_in(e, j, r):
                if later(e, TURN - 1):
                    sp.wait_ge(xg_in[r], j * 16)
                sp.dma_start(ix[r][:], g.list_dram[bass.ds(e * REGION, P), :]).then_inc(ix_in[r], 16)

            def weights(e, j, r):
                if not later(e, 1):
                    return
                sp.wait_ge(gu_mm, e - 1)
                load_gate_up(nc, io, g, sp, e, r % 2, wgu_in[r % 2])
                sp.wait_ge(dn_mm, e - 1)
                load_down(nc, io, g, sp, e, r % 2, wd_in[r % 2])

            experts(sp, ((0, list_in), (2, weights)))
            sp.wait_ge(st_y, 16 * NE)
            sp.sem_inc(l_free, 1)

            def long_body(e, row, n):
                sp.wait_ge(l_free, n + 1)
                load_gate_up(nc, io, g, sp, e, 0, l_w)
                load_down(nc, io, g, sp, e, 0, l_w)
                sp.wait_ge(l_st, n * 16 + 16)
                sp.sem_inc(l_free, 1)

            long_lists(sp, long_body)

        @block.gpsimd
        def _(pool):
            def rows_in(e, j, r):
                pool.wait_ge(ix_in[r], j * 16 + 16)
                if later(e, TURN - 1):
                    pool.wait_ge(xT_mm, e - (TURN - 1))
                pool.sem_inc(started, 1)
                gather(pool, r, xg_in[r])

            def results_out(e, j, r):
                pool.wait_ge(sl_in[r % 2], use(j, r) * 16 + 16)
                pool.wait_ge(y_done, e + 1)
                if later(e):
                    pool.wait_ge(st_y, e * 16)
                pool.sem_inc(started, 1)
                scatter(pool, r % 2, st_y)

            experts(pool, ((0, rows_in), (3, results_out)))

            def long_body(e, row, n):
                pool.wait_ge(l_free, n + 1)
                pool.sem_inc(started, 1)
                nc.gpsimd.dma_start(ix[0][:], g.list_dram[bass.ds(e * REGION + row, P), :]).then_inc(l_ix, 16)
                nc.gpsimd.dma_start(sl[0][:], g.list_dram[bass.ds(e * REGION + row, P), :]).then_inc(l_ix, 16)
                pool.wait_ge(l_ix, n * 32 + 32)
                pool.sem_inc(started, 1)
                gather(pool, 0, l_xg)
                pool.wait_ge(l_y, n + 1)
                pool.sem_inc(started, 1)
                scatter(pool, 0, l_st)

            long_lists(pool, long_body)

        @block.tensor
        def _(pe):
            def rows_turned(e, j, r):
                pe.wait_ge(xg_in[r], j * 16 + 16)
                if later(e):
                    pe.wait_ge(xT_done, e)
                transposes(r).then_inc(xT_mm, 1)

            def first_products(e, j, r):
                pe.wait_ge(wgu_in[r % 2], use(j, r) * 32 + 32)
                pe.wait_ge(xT_done, e + 1)
                if later(e, 1):
                    pe.wait_ge(hid_done, e - 1)
                gate_up(r % 2).then_inc(gu_mm, 1)

            def second_products(e, j, r):
                pe.wait_ge(wd_in[r % 2], use(j, r) * 16 + 16)
                pe.wait_ge(hid_done, e + 1)
                if later(e, 1):
                    pe.wait_ge(y_done, e - 1)
                down(r % 2).then_inc(dn_mm, 1)

            experts(pe, ((1, first_products), (0, rows_turned), (2, second_products)))

            def long_body(e, row, n):
                pe.wait_ge(l_xg, n * 16 + 16)
                transposes(0).then_inc(l_xT_mm, 1)
                pe.wait_ge(l_xT, n + 1)
                pe.wait_ge(l_w, n * 48 + 48)
                gate_up(0).then_inc(l_gu, 1)
                pe.wait_ge(l_hid, n + 1)
                down(0).then_inc(l_dn, 1)

            long_lists(pe, long_body)

        @block.scalar
        def _(act):
            def squash(b):
                return nc.scalar.activation(sig[:], GU[b][:, 0:FT, :], ACT.Sigmoid)

            def out(b):
                return nc.scalar.activation(y[:, b, :], Y[b][:], ACT.Copy)

            def sigmoids(e, j, r):
                act.wait_ge(gu_mm, e + 1)
                if later(e):
                    act.wait_ge(hid_done, e)
                squash(r % 2).then_inc(sig_done, 1)

            def results(e, j, r):
                if later(e, 1):
                    act.wait_ge(st_y, (e - 1) * 16)
                act.dma_start(sl[r % 2][:], g.list_dram[bass.ds(e * REGION, P), :]).then_inc(sl_in[r % 2], 16)
                act.wait_ge(dn_mm, e + 1)
                out(r % 2).then_inc(y_done, 1)

            experts(act, ((0, sigmoids), (1, results)))

            def long_body(e, row, n):
                act.wait_ge(l_gu, n + 1)
                squash(0).then_inc(l_sig, 1)
                act.wait_ge(l_dn, n + 1)
                out(0).then_inc(l_y, 1)

            long_lists(act, long_body)

        @block.vector
        def _(dve):
            step = Steps(dve, dve_step)

            def rows_out():
                return nc.vector.tensor_copy(xT[:], X[:].rearrange("p (k t) -> p k t", t=P))

            def gated(b, mark):
                mark(nc.vector.tensor_tensor(sig[:], GU[b][:, 0:FT, :], sig[:], ALU.mult))
                return nc.vector.tensor_tensor(hid[:, b], GU[b][:, FT:, :], sig[:], ALU.mult)

            def rows_turned(e, j, r):
                dve.wait_ge(xT_mm, e + 1)
                if later(e):
                    dve.wait_ge(gu_mm, e)
                rows_out().then_inc(xT_done, 1)

            def products(e, j, r):
                dve.wait_ge(sig_done, e + 1)
                if later(e, 1):
                    dve.wait_ge(dn_mm, e - 1)
                gated(r % 2, step).then_inc(hid_done, 1)

            experts(dve, ((0, rows_turned), (1, products)), step, TURN)

            def long_body(e, row, n):
                dve.wait_ge(l_xT_mm, n + 1)
                rows_out().then_inc(l_xT, 1)
                dve.wait_ge(l_sig, n + 1)

                def mark(ins):
                    ins.then_inc(l_step, 1)
                    dve.wait_ge(l_step, n + 1)

                gated(0, mark).then_inc(l_hid, 1)

            long_lists(dve, long_body)


def phase_h(nc, io, g):
    with ExitStack() as stack:
        m = Memory(nc, stack)
        y = [[m.sb(f"h_y{k}{b}", [P, D]) for b in range(2)] for k in range(2)]
        out = m.sb("h_out", [P, 2, D])
        y_in = [[m.sems(f"h_y_in{k}{b}")[0] for b in range(2)] for k in range(2)]
        summed, first_done, dve_step, st0, st1 = m.sems("h_summed h_first_done h_dve_step h_st0 h_st1")
        st = (st0, st1)
        block = stack.enter_context(nc.Block())

        @block.scalar
        def _(act):
            def first_pick(i, b, n, T):
                act.wait_ge(y_in[0][b], 16 * n + 16)
                if not (isinstance(n, int) and n == 0):
                    act.wait_ge(st[b], 16 * n)
                nc.scalar.activation(out[0:T, b], y[0][b][0:T], ACT.Copy, scale=g.weight[0:T, 0, bass.ds(i, 1)]
                                     ).then_inc(first_done, 1)

            first_pick(0, 0, 0, P)
            first_pick(1, 1, 0, P)
            with act.Fori(1, PT // 2) as j:
                first_pick(2 * j, 0, j, P)
                first_pick(2 * j + 1, 1, j, P)
            first_pick(PT, 0, PT // 2, DEC)

        @block.vector
        def _(dve):
            step = Steps(dve, dve_step)

            def tile(i, b, n, T, mod):
                dve.wait_ge(first_done, i + 1)
                dve.wait_ge(y_in[1][b], 16 * n + 16)
                step(nc.vector.scalar_tensor_tensor(out[0:T, b], y[1][b][0:T], g.weight[0:T, 1, bass.ds(i, 1)],
                                                    out[0:T, b], ALU.mult, ALU.add))
                step(nc.vector.tensor_tensor(out[0:T, b], out[0:T, b], g.gate_m[0:T, mod, :], ALU.mult))
                nc.vector.tensor_tensor(out[0:T, b], out[0:T, b], g.x2[0:T, i, :], ALU.add).then_inc(summed, 1)

            tile(0, 0, 0, P, 0)
            tile(1, 1, 0, P, 0)
            per = step.n
            step.straight()
            with dve.Fori(1, PT // 2) as j:
                step.enter(j - 1, per)
                tile(2 * j, 0, j, P, 0)
                tile(2 * j + 1, 1, j, P, 0)
            step.leave(PT // 2 - 1)
            tile(PT, 0, PT // 2, DEC, 1)

        @block.sync
        def _(sp):
            def load(i, b, T):
                for k in range(2):
                    sp.dma_start(y[k][b][0:T, :], g.y_dram[bass.ds(i * P + k * TOK, T), :]).then_inc(y_in[k][b], 16)

            def store(i, b, T):
                sp.wait_ge(summed, i + 1)
                sp.dma_start(io["y_p"][bass.ds(i * P, P), :], out[:, b]).then_inc(st[b], 16)
                if T:
                    load(i + 2, b, T)

            load(0, 0, P)
            load(1, 1, P)
            with sp.Fori(0, PT // 2 - 1) as j:
                store(2 * j, 0, P)
                store(2 * j + 1, 1, P)
            store(PT - 2, 0, DEC)
            store(PT - 1, 1, 0)
            sp.wait_ge(summed, NT)
            sp.dma_start(io["y_s"], out[0:DEC, 0]).then_inc(st[0], 16)
            sp.wait_ge(st[0], 16 * (PT // 2 + 1))
            sp.wait_ge(st[1], 16 * (PT // 2))


class Shared:
    pass


INPUTS = ("x_prompt", "x_sample", "cache_sb_k", "cache_sb_v", "cache_mla_ckv", "cache_mla_kpe", "c_prompt",
          "c_sample", "w_ada", "b_ada", "g_mix", "w_in", "g_sb_q", "g_sb_k", "g_qa", "w_qb", "g_kva", "w_kvb",
          "g_mq_nope", "g_mk_nope", "g_mq_pe", "g_mk_pe", "w_out", "g_ffn", "w_rg", "b_rg", "w_re", "b_re",
          "w_gate", "w_up", "w_down")


def program(nc, io):
    USED.clear()
    g = Shared()
    with ExitStack() as stack:
        m = Memory(nc, stack)
        g.qs_dram = nc.dram_tensor("qs_dram", [SBH // 2, P, TOK], F32, kind="Internal").ap()
        g.ks_dram = nc.dram_tensor("ks_dram", [SBH // 2, P, TOK], F32, kind="Internal").ap()
        g.o_dram = nc.dram_tensor("o_dram", [TOK, D], F32, kind="Internal").ap()
        g.h2_dram = nc.dram_tensor("h2_dram", [TOK + 1, D], F32, kind="Internal").ap()
        g.list_dram = nc.dram_tensor("list_dram", [NE * REGION, 2], U32, kind="Internal").ap()
        g.y_dram = nc.dram_tensor("y_dram", [2 * TOK + P, D], F32, kind="Internal").ap()
        g.qm_dram = nc.dram_tensor("qm_dram", [MH, MK, TOK], F32, kind="Internal").ap()
        g.ident = m.sb("ident", [P, P])
        g.identb = m.sb("identb", [P, P], BF16)
        g.mask_sb = m.sb("mask_sb", [P, P], BF16)
        g.mask_mla = m.sb("mask_mla", [P, P], BF16)
        g.tri = m.sb("tri", [P, P])
        g.ones = m.sb("ones", [P, P])
        g.eps = m.sb("eps", [P, 1])
        g.rows = m.sb("rows", [P, ROWW])
        g.modT = m.sb("modT", [P, 48, 2])
        g.scale_a = m.sb("scale_a", [P, KD, 2])
        g.scale_m = m.sb("scale_m", [P, KD, 2])
        g.ckv_new = m.sb("ckv_new", [P, KR])
        g.w_in_loaded, g.w_small_loaded = m.sems("w_in_loaded w_small_loaded")
        with ExitStack() as keys:
            m = Memory(nc, keys)
            g.kT_m = m.sb("kT_m", [MK, MH, TOK])
            g.values = m.sb("values", [P, 2 * NT * SBW])
            g.v_sb = g.values[:, 0:NT * SBW].rearrange("p (i n) -> p i n", n=SBW)
            g.v_m = g.values[:, NT * SBW:].rearrange("p (i n) -> p i n", n=MH * MV)
            g.w_kvb = m.sb("w_kvb_sb", [P, KR // P, MH * (NOPE + MV)])
            with ExitStack() as weights:
                m = Memory(nc, weights)
                g.w_in = m.sb("w_in_sb", [P, KD, INC])
                g.w_qb = m.sb("w_qb_sb", [P, QR // P, MH * MK])
                g.rope = m.sb("rope_sb", [P, NT, 2 * ROPE])
                phase_a(nc, io, g)
                phase_b(nc, io, g)
            phase_cd(nc, io, g)
            phase_e(nc, io, g, latent=False)
            phase_e(nc, io, g, latent=True)
        retire_semaphores(nc)
        m = Memory(nc, stack)
        g.x2 = m.sb("x2", [P, NT, D])
        g.gate_m = m.sb("gate_m", [P, 2, D])
        g.logits = m.sb("logits", [P, NT, NG + NE])
        g.weight = m.sb("weight", [P, 2, NT])
        g.count = m.sb("count", [P, NE], I32)
        g.longest = m.sb("longest", [P, 1], I32)
        phase_f(nc, io, g)
        g.w_gate = m.sb("w_gate_sb", [P, 2, KD, DE])
        g.w_up = m.sb("w_up_sb", [P, 2, KD, DE])
        g.w_down = m.sb("w_down_sb", [P, 2, DE // P, D])
        g.wgu_in = m.sems("wgu_in0 wgu_in1")
        g.wd_in = m.sems("wd_in0 wd_in1")
        phase_r(nc, io, g)
        phase_g(nc, io, g)
        phase_h(nc, io, g)


def rope_table():
    inv = np.float32(10000.0) ** (-np.arange(0, ROPE, 2, dtype=np.float32) / np.float32(ROPE))
    pos = np.zeros(NT * P, np.float32)
    pos[:SEQ] = np.arange(SEQ)
    pos[SEQ:TOK] = PAST + np.arange(DEC)
    ang = pos[:, None] * inv[None, :].astype(np.float32)
    c, s = np.cos(ang), np.sin(ang)
    t = np.concatenate([c, c, -s, s], axis=1).astype(np.float32)
    return np.ascontiguousarray(t.reshape(NT, P, 2 * ROPE).transpose(1, 0, 2))


def kernel(**inputs):
    import concourse.bacc as bacc
    from concourse.bass_utils import run_bass_kernel_spmd

    nc = bacc.Bacc("TRN2", target_bir_lowering=False, num_devices=1)
    shapes = {
        "x_prompt": (SEQ, D), "x_sample": (DEC, D), "cache_sb_k": (PAST, SBW), "cache_sb_v": (PAST, SBW),
        "cache_mla_ckv": (PAST, KR), "cache_mla_kpe": (PAST, ROPE), "c_prompt": (D,), "c_sample": (D,),
    }
    arrays, io = {}, {}
    for name in INPUTS:
        a = np.asarray(inputs[name])
        a = np.ascontiguousarray(a.reshape(shapes.get(name, a.shape[1:])))
        arrays[name] = a
        io[name] = nc.dram_tensor(name, a.shape, mybir.dt.from_np(a.dtype), kind="ExternalInput").ap()
    arrays["rope"] = rope_table()
    io["rope"] = nc.dram_tensor("rope", arrays["rope"].shape, F32, kind="ExternalInput").ap()
    outs = (("y_p", (SEQ, D), (1, SEQ, D)), ("y_s", (DEC, D), (1, DEC, D)),
            ("o_k_p", (SEQ, SBW), (1, 1, SEQ, SBH, SBD)), ("o_v_p", (SEQ, SBW), (1, 1, SEQ, SBH, SBD)),
            ("o_ckv_p", (SEQ, KR), (1, 1, SEQ, KR)), ("o_kpe_p", (SEQ, ROPE), (1, 1, SEQ, ROPE)),
            ("o_k_s", (DEC, SBW), (1, 1, DEC, SBH, SBD)), ("o_v_s", (DEC, SBW), (1, 1, DEC, SBH, SBD)),
            ("o_ckv_s", (DEC, KR), (1, 1, DEC, KR)), ("o_kpe_s", (DEC, ROPE), (1, 1, DEC, ROPE)))
    for name, shape, _ in outs:
        io[name] = nc.dram_tensor(name, shape, F32, kind="ExternalOutput").ap()
    program(nc, io)
    r = run_bass_kernel_spmd(nc, [arrays], core_ids=[0])
    return tuple(np.asarray(r.results[0][name]).reshape(shape) for name, _, shape in outs)
```

```python
from contextlib import ExitStack

import numpy as np

import concourse.bass as bass
from concourse import mybir

F32 = mybir.dt.float32
BF16 = mybir.dt.bfloat16
U32 = mybir.dt.uint32
I32 = mybir.dt.int32
ALU = mybir.AluOpType
ACT = mybir.ActivationFunctionType
AX = mybir.AxisListType

P = 128
D = 1024
KD = D // P
SEQ, DEC, PAST = 1024, 32, 2048
PT = SEQ // P
NT = PT + 1
TOK = SEQ + DEC
SBH, SBD = 8, 64
MH, NOPE, ROPE, MV = 8, 64, 32, 64
MK = NOPE + ROPE
QR, KR = 384, 256
SBW = SBH * SBD
INC = 3 * SBW + QR + KR + ROPE
EPS = 1e-6
NEG = -1e30
NG, EPG, NE, DE = 4, 8, 32, 256
SB_SCALE = SBD ** -0.5
MLA_SCALE = MK ** -0.5
PTILES = PAST // P
SKEYS = PAST + DEC
REGION = 9 * P
PAD = TOK

ROWS = {}
_at = 0
for _n, _w in (("g_sb_q", SBD), ("g_sb_k", SBD), ("g_mq_nope", NOPE), ("g_mk_nope", NOPE), ("g_mq_pe", ROPE),
               ("g_mk_pe", ROPE), ("g_kva", KR), ("g_qa", QR), ("b_rg", NG), ("b_re", NE)):
    ROWS[_n] = (_at, _at + _w)
    _at += _w
ROWW = _at
VEC = {"b_ada": (0, 48), "g_mix": (48, 56), "g_ffn": (56, 64), "c_prompt": (64, 72), "c_sample": (72, 80)}


class Steps:

    def __init__(self, engine, sem):
        self.engine, self.sem, self.base, self.n, self.total = engine, sem, 0, 0, 0

    def __call__(self, ins):
        ins.then_inc(self.sem, 1)
        self.n += 1
        self.engine.wait_ge(self.sem, self.base + self.n)

    def enter(self, turn, per):
        self.base, self.n, self.per = self.total + turn * per, 0, per

    def leave(self, turns):
        assert self.n == self.per, (self.n, self.per)
        self.total += turns * self.per
        self.base, self.n = self.total, 0

    def straight(self):
        self.total += self.n
        self.base, self.n = self.total, 0


class Memory:

    def __init__(self, nc, stack):
        self.nc, self.stack = nc, stack

    def sb(self, name, shape, dt=F32):
        t = self.stack.enter_context(self.nc.sbuf_tensor(name, shape, dt))
        return t

    def ps(self, name, shape, dt=F32):
        return self.stack.enter_context(self.nc.psum_tensor(name, shape, dt))

    def sems(self, names):
        made = [self.nc.alloc_semaphore(n) for n in names.split()]
        USED.extend(made)
        return made


USED = []


def retire_semaphores(nc):
    nc.clear_and_free_semaphores(list(USED))
    USED.clear()
    nc.all_engine_barrier()


def phase_a(nc, io, g):
    with ExitStack() as stack:
        m = Memory(nc, stack)
        WCOLS, WBUFS = 512, 2
        CHUNKS = 6 * D // WCOLS
        CT = WCOLS // P
        vrows = m.sb("vrows", [80, P])
        grow = m.sb("grow", [1, 1024])
        ones1 = m.sb("ones1", [1, P])
        vecT = m.sb("vecT", [P, 80])
        sig = m.sb("sig", [P, 16])
        silu_c = m.sb("silu_c", [P, KD, 2])
        wa = g.values[:, 0:WBUFS * KD * WCOLS].rearrange("p (b k n) -> p b k n", b=WBUFS, n=WCOLS)
        ps_vec = m.ps("ps_vec", [P, 512])
        mod_row = m.sb("mod_row", [2, WBUFS, WCOLS])
        ps_row = m.ps("ps_row", [P, 1024])
        ps_sum = [m.ps(f"ps_sum{b}", [P, WCOLS]) for b in range(WBUFS)]
        ps_mod = [m.ps(f"ps_mod{b}", [P, 512]) for b in range(WBUFS)]
        (vec_in, row_in, const_ready, vec_t, vec_done, sig_done, silu_done, row_mm, row_done, mod_mm, mod_done,
         dve_step, w_loaded0, w_loaded1, pool_step, sum_mm, sum_out) = m.sems(
            "vec_in row_in const_ready vec_t vec_done sig_done silu_done row_mm row_done mod_mm mod_done "
            "dve_step w_loaded0 w_loaded1 pool_step sum_mm sum_out")
        w_loaded = [w_loaded0, w_loaded1]
        block = stack.enter_context(nc.Block())
        w_ada = io["w_ada"].rearrange("(k p) n -> p k n", p=P)

        @block.sync
        def _(sp):
            for name, (a, b) in VEC.items():
                sp.dma_start(vrows[a:b, :], io[name].rearrange("(j p) -> j p", p=P)).then_inc(vec_in, 16)
            for b in range(WBUFS):
                sp.dma_start(wa[:, b], w_ada[:, :, b * WCOLS:(b + 1) * WCOLS]).then_inc(w_loaded[b], 16)
            for name, (a, b) in ROWS.items():
                sp.dma_start(grow[0:1, a:b], io[name].rearrange("(o n) -> o n", o=1)).then_inc(row_in, 16)
            sp.dma_start(g.x[:], io["x_prompt"][0:P, :]).then_inc(g.x_in, 16)
            w_in = io["w_in"].rearrange("(k p) n -> p k n", p=P)
            for k in range(WBUFS):
                sp.dma_start(g.w_in[:, k, :], w_in[:, k, :]).then_inc(g.w_in_loaded, 16)

            def turn(j, k):
                for b in range(WBUFS):
                    sp.wait_ge(sum_mm, j * WBUFS + (b - WBUFS + 1))
                    sp.dma_start(wa[:, b], w_ada[:, :, bass.ds((j * WBUFS + b) * WCOLS, WCOLS)]
                                 ).then_inc(w_loaded[b], 16)
                    if k is not None:
                        sp.dma_start(g.w_in[:, bass.ds(k + b, 1), :], w_in[:, bass.ds(k + b, 1), :]
                                     ).then_inc(g.w_in_loaded, 16)

            with sp.Fori(1, KD // WBUFS) as j:
                turn(j, j * WBUFS)
            for j in range(KD // WBUFS, CHUNKS // WBUFS):
                turn(j, None)
            sp.dma_start(g.w_qb[:], io["w_qb"].rearrange("(k p) n -> p k n", p=P)).then_inc(g.w_small_loaded, 16)
            sp.dma_start(g.w_kvb[:], io["w_kvb"].rearrange("(k p) n -> p k n", p=P)).then_inc(g.w_small_loaded, 16)
            sp.dma_start(g.rope[:], io["rope"]).then_inc(g.w_small_loaded, 16)

        @block.gpsimd
        def _(pool):
            step = Steps(pool, pool_step)
            step(nc.gpsimd.memset(g.ident[:], 0.0))
            step(nc.gpsimd.memset(ones1[:], 1.0))
            step(nc.gpsimd.memset(g.mask_sb[:], 0.0))
            step(nc.gpsimd.memset(g.mask_mla[:], 0.0))
            step(nc.gpsimd.memset(g.mask_mla[0:64, 64:P], NEG))
            step(nc.gpsimd.memset(g.tri[:], 1.0))
            step(nc.gpsimd.memset(g.ones[:], 1.0))
            step(nc.gpsimd.memset(g.eps[:], EPS))
            step(nc.gpsimd.affine_select(out=g.ident[:], in_=g.ident[:], compare_op=ALU.not_equal, fill=1.0,
                                         base=0, pattern=[[-1, P]], channel_multiplier=1))
            step(nc.gpsimd.affine_select(out=g.mask_sb[:], in_=g.mask_sb[:], compare_op=ALU.is_gt, fill=NEG,
                                         base=0, pattern=[[-1, P]], channel_multiplier=1))
            step(nc.gpsimd.affine_select(out=g.tri[:], in_=g.tri[:], compare_op=ALU.is_gt, fill=0.0,
                                         base=0, pattern=[[1, P]], channel_multiplier=-1))
            nc.gpsimd.tensor_copy(g.identb[:], g.ident[:]).then_inc(const_ready, 1)

        @block.scalar
        def _(act):
            act.wait_ge(vec_done, 1)
            a = VEC["c_prompt"][0]
            nc.scalar.activation(sig[:], vecT[:, a:a + 16], ACT.Sigmoid).then_inc(sig_done, 1)

            def rows_out(j, b):
                n = j * WBUFS + b
                act.wait_ge(sum_mm, n + 1)
                if not isinstance(j, int):
                    act.wait_ge(mod_mm, n - (WBUFS - 1))
                nc.scalar.activation(mod_row[:, b, :], ps_sum[b][0:2, :], ACT.Copy).then_inc(sum_out, 1)

            for b in range(WBUFS):
                rows_out(0, b)
            with act.Fori(1, CHUNKS // WBUFS) as j:
                for b in range(WBUFS):
                    rows_out(j, b)

        @block.tensor
        def _(pe):
            pe.wait_ge(const_ready, 1)
            pe.wait_ge(vec_in, 16 * len(VEC))
            nc.tensor.transpose(ps_vec[:, 0:80], vrows[:], g.ident[0:80, 0:80]).then_inc(vec_t, 1)
            pe.wait_ge(silu_done, 1)

            def sums(j, b):
                pe.wait_ge(w_loaded[b], 16 * j + 16)
                if not isinstance(j, int):
                    pe.wait_ge(sum_out, j * WBUFS + (b - WBUFS + 1))
                for k in range(KD):
                    last = nc.tensor.matmul(ps_sum[b][0:2, :], lhsT=silu_c[:, k, :], rhs=wa[:, b, k, :],
                                            start=k == 0, stop=k == KD - 1)
                last.then_inc(sum_mm, 1)

            def turned(j, b, first=False):
                n = j * WBUFS + b
                pe.wait_ge(sum_out, n + 1)
                if not first:
                    pe.wait_ge(mod_done, n - (WBUFS - 1))
                for t in range(CT):
                    last = nc.tensor.matmul(ps_mod[b][:, 2 * t:2 * t + 2], lhsT=mod_row[:, b, t * P:(t + 1) * P],
                                            rhs=g.ident[0:2, 0:2], start=True, stop=True)
                last.then_inc(mod_mm, 1)

            sums(0, 0)
            pe.wait_ge(row_in, 16 * len(ROWS))
            nc.tensor.matmul(ps_row[:, 0:512], lhsT=ones1[:], rhs=grow[0:1, 0:512], start=True, stop=True)
            nc.tensor.matmul(ps_row[:, 512:ROWW], lhsT=ones1[:], rhs=grow[0:1, 512:ROWW], start=True,
                             stop=True).then_inc(row_mm, 1)
            sums(0, 1)
            turned(0, 0, True)
            turned(0, 1, True)
            with pe.Fori(1, CHUNKS // WBUFS) as j:
                sums(j, 0)
                sums(j, 1)
                turned(j, 0)
                turned(j, 1)

        @block.vector
        def _(dve):
            step = Steps(dve, dve_step)
            dve.wait_ge(vec_t, 1)
            nc.vector.tensor_copy(vecT[:], ps_vec[:, 0:80]).then_inc(vec_done, 1)
            dve.wait_ge(sig_done, 1)
            a = VEC["c_prompt"][0]
            dve.wait_ge(vec_done, 1)
            nc.vector.tensor_tensor(silu_c[:].rearrange("p k b -> p b k"),
                                    vecT[:, a:a + 16].rearrange("p (b k) -> p b k", b=2),
                                    sig[:].rearrange("p (b k) -> p b k", b=2), ALU.mult).then_inc(silu_done, 1)
            dve.wait_ge(row_mm, 1)
            nc.vector.tensor_copy(g.rows[:], ps_row[:, 0:ROWW]).then_inc(row_done, 1)

            def chunk(j, b):
                at = (j * WBUFS + b) * CT
                dve.wait_ge(mod_mm, j * WBUFS + (b + 1))
                nc.vector.tensor_tensor(g.modT[:, bass.ds(at, CT), :],
                                        ps_mod[b][:, 0:2 * CT].rearrange("p (t b) -> p t b", b=2),
                                        vecT[:, bass.ds(at, CT)].unsqueeze(2).broadcast_to([P, CT, 2]),
                                        ALU.add).then_inc(mod_done, 1)

            with dve.Fori(0, CHUNKS // WBUFS) as j:
                for b in range(WBUFS):
                    chunk(j, b)
            dve.wait_ge(mod_done, CHUNKS)
            for out, name, chunk_at in ((g.scale_a, "g_mix", 1), (g.scale_m, "g_ffn", 4)):
                a, b = VEC[name]
                step(nc.vector.tensor_scalar(out[:], g.modT[:, 8 * chunk_at:8 * chunk_at + 8, :], 1.0, None,
                                             ALU.add))
                step(nc.vector.tensor_tensor(out[:], out[:], vecT[:, a:b].unsqueeze(2).broadcast_to([P, KD, 2]),
                                             ALU.mult))


def phase_b(nc, io, g):
    with ExitStack() as stack:
        m = Memory(nc, stack)
        x, x_in = g.x, g.x_in
        hT = m.sb("b_hT", [P, KD, P])
        sq = m.sb("b_sq", [P, D])
        qk = m.sb("b_qk", [P, 2 * SBH, SBD])
        qlat = m.sb("b_qlat", [P, QR])
        qlatT = m.sb("b_qlatT", [P, QR // P, P])
        ckvT = m.sb("b_ckvT", [P, KR // P, P])
        kpe = m.sb("b_kpe", [P, 2 * ROPE])
        qf = m.sb("b_qf", [P, MH, MK])
        kf = m.sb("b_kf", [P, MH, MK])
        qsT = m.sb("b_qsT", [P, 4, P])
        ksT = m.sb("b_ksT", [P, 4, P])
        qmT = m.sb("b_qmT", [MK, MH, P])
        rot = m.sb("b_rot", [P, MH, ROPE])
        st = m.sb("b_st", [P, 8])
        sth = m.sb("b_sth", [P, 48])
        ckv = g.ckv_new
        U = [m.ps(f"b_U{n}", [P, 512]) for n in range(2)]
        U2 = m.ps("b_U2", [P, 512])
        UL = m.ps("b_UL", [P, 2, 512])
        TA, TB, X = (m.ps(n, [P, 512]) for n in ("b_TA", "b_TB", "b_X"))
        (xstat, xrms, xrec, xn_done, ht_mm, ht_done, lat_mm, lat_sq, lat_rms, lat_norm, kpe_done,
         latT_mm, latTa_done, latTb_done, q_mm, k_mm, v_mm, qk_evac, qk_sq, v_evac, qk_red, qk_rms, qk_norm,
         qmla_mm, kv_mm, qm_evac, kv_evac, mla_red, mla_rms, mla_norm, r0, r1, r2, r3, r4, r5, e0, e1, e2, e3,
         e4, e5, st_ckv, st_kpe, st_k, st_v, st_qs, st_ks, st_qm, dve_step) = m.sems(
            "xstat xrms xrec xn_done ht_mm ht_done lat_mm lat_sq lat_rms lat_norm kpe_done latT_mm "
            "latTa_done latTb_done q_mm k_mm v_mm qk_evac qk_sq v_evac qk_red qk_rms qk_norm qmla_mm kv_mm "
            "qm_evac kv_evac mla_red mla_rms mla_norm r0 r1 r2 r3 r4 r5 e0 e1 e2 e3 e4 e5 st_ckv st_kpe st_k "
            "st_v st_qs st_ks st_qm b_dve_step")
        block = stack.enter_context(nc.Block())
        row = {n: g.rows[:, a:b] for n, (a, b) in ROWS.items()}

        def last(i):
            return isinstance(i, int) and i == PT

        def width(i):
            return DEC if last(i) else P

        def tiles(engine, body, steps=None):
            body(0)
            if steps:
                per = steps.n
                steps.straight()
            with engine.Fori(1, PT - 1) as i:
                if steps:
                    steps.enter(i - 1, per)
                body(i)
            if steps:
                steps.leave(PT - 2)
            body(PT - 1)
            body(PT)

        @block.sync
        def _(sp):

            def queries_out(i):
                T = width(i)
                sp.wait_ge(e0, i + 1)
                sp.dma_start(g.qs_dram[:, :, bass.ds(i * P, T)].rearrange("a p t -> p a t"),
                             qsT[:, :, 0:T]).then_inc(st_qs, 16)
                sp.wait_ge(e1, i + 1)
                sp.dma_start(g.ks_dram[:, :, bass.ds(i * P, T)].rearrange("a p t -> p a t"),
                             ksT[:, :, 0:T]).then_inc(st_ks, 16)
                sp.wait_ge(e3, i + 1)
                sp.wait_ge(e2, i + 1)
                sp.dma_start(g.qm_dram[:, :, bass.ds(i * P, T)].rearrange("h p t -> p h t"),
                             qmT[:, :, 0:T]).then_inc(st_qm, 16)

            def out(name, i):
                return io[name + "_s"] if last(i) else io[name + "_p"][bass.ds(i * P, P), :]

            def body(i):
                T = width(i)
                if not last(i):
                    sp.wait_ge(ht_mm, i + 1)
                    if last(i + 1):
                        sp.dma_start(x[0:DEC, :], io["x_sample"]).then_inc(x_in, 16)
                    else:
                        sp.dma_start(x[:], io["x_prompt"][bass.ds((i + 1) * P, P), :]).then_inc(x_in, 16)
                sp.wait_ge(kpe_done, i + 1)
                sp.dma_start(out("o_ckv", i), ckv[0:T, :]).then_inc(st_ckv, 16)
                sp.dma_start(out("o_kpe", i), kpe[0:T, ROPE:2 * ROPE]).then_inc(st_kpe, 16)
                if not (isinstance(i, int) and i == 0):
                    queries_out(i - 1)
                sp.wait_ge(qk_norm, i + 1)
                sp.dma_start(out("o_k", i), qk[0:T, SBH:, :].rearrange("p h d -> p (h d)")).then_inc(st_k, 16)
                sp.wait_ge(v_evac, i + 1)
                sp.dma_start(out("o_v", i), g.v_sb[0:T, i, :]).then_inc(st_v, 16)

            tiles(sp, body)
            queries_out(PT)
            for s in (st_ckv, st_kpe, st_v, st_k, st_qs, st_ks, st_qm):
                sp.wait_ge(s, 16 * NT)

        @block.tensor
        def _(pe):
            pe.wait_ge(g.w_in_loaded, 16 * KD)
            pe.wait_ge(g.w_small_loaded, 48)

            def transposes(dst, src, w, n, T, sem, wait):
                for s, v in wait:
                    pe.wait_ge(s, v)
                for j in range(n):
                    end = nc.tensor.transpose(dst[0:w, j * P:j * P + T], src(j), g.ident[0:T, 0:T])
                end.then_inc(sem, 1)

            def hT_of(i):
                T = width(i)
                pe.wait_ge(xn_done, i + 1)
                for k in range(KD):
                    end = nc.tensor.transpose(U[k // 4][:, (k % 4) * P:(k % 4) * P + T],
                                               x[0:T, k * P:(k + 1) * P], g.ident[0:T, 0:T])
                end.then_inc(ht_mm, 1)

            def project(dst, c0, c1, T, sem, val=None):
                for k in range(KD):
                    end = nc.tensor.matmul(dst[0:T, 0:c1 - c0], lhsT=hT[:, k, 0:T], rhs=g.w_in[:, k, c0:c1],
                                            start=k == 0, stop=k == KD - 1)
                if sem is not None:
                    end.then_inc(sem, 1)

            def pairs(first_head):
                return lambda j: qk[:, first_head + 2 * j:first_head + 2 * j + 2, :].rearrange("p h d -> p (h d)")

            def back(i, part):
                T = width(i)
                if part == 0:
                    pe.wait_ge(qk_norm, i + 1)
                    transposes(TA, lambda j: pairs(0)(j)[0:T], P, 4, T, r0, [(latTa_done, i + 1)])
                    transposes(TB, lambda j: pairs(SBH)(j)[0:T], P, 4, T, r1, [(kv_evac, i + 1)])
                    pe.wait_ge(mla_norm, i + 1)
                    transposes(X, lambda j: qf[0:T, j, :], MK, 4, T, r2, [(kv_evac, i + 1)])
                elif part == 1:
                    transposes(TA, lambda j: qf[0:T, 4 + j, :], MK, 4, T, r3, [(e0, i + 1)])
                    transposes(TB, lambda j: kf[0:T, j, :], MK, 4, T, r4, [(e1, i + 1)])
                    transposes(X, lambda j: kf[0:T, 4 + j, :], MK, 4, T, r5, [(e2, i + 1)])

            def body(i):
                T, first = width(i), isinstance(i, int) and i == 0
                pe.wait_ge(ht_done, i + 1)
                if not first:
                    pe.wait_ge(qm_evac, i)
                project(UL[:, 0, :], 3 * SBW, 3 * SBW + QR, T, None)
                project(UL[:, 1, :], 3 * SBW + QR, INC, T, lat_mm)
                if not first:
                    back(i - 1, 0)
                project(U[0], 0, SBW, T, q_mm)
                if not first:
                    back(i - 1, 1)
                project(U[1], SBW, 2 * SBW, T, k_mm)
                pe.wait_ge(lat_norm, i + 1)
                if not first:
                    pe.wait_ge(e3, i)
                    pe.wait_ge(e4, i)
                for j in range(QR // P):
                    nc.tensor.transpose(TA[:, j * P:j * P + T], qlat[0:T, j * P:(j + 1) * P], g.ident[0:T, 0:T])
                for j in range(KR // P):
                    end = nc.tensor.transpose(TB[:, j * P:j * P + T], ckv[0:T, j * P:(j + 1) * P],
                                               g.ident[0:T, 0:T])
                end.then_inc(latT_mm, 1)
                if not first:
                    pe.wait_ge(v_evac, i)
                project(U2, 2 * SBW, 3 * SBW, T, v_mm)
                if not last(i):
                    pe.wait_ge(qk_evac, i + 1)
                    hT_of(i + 1)
                pe.wait_ge(latTa_done, i + 1)
                pe.wait_ge(latTb_done, i + 1)
                pe.wait_ge(kpe_done, i + 1)
                for c in range(2):
                    for k in range(QR // P):
                        end = nc.tensor.matmul(UL[0:T, c, 0:QR], lhsT=qlatT[:, k, 0:T],
                                                rhs=g.w_qb[:, k, c * QR:(c + 1) * QR], start=k == 0,
                                                stop=k == QR // P - 1)
                end.then_inc(qmla_mm, 1)
                if not first:
                    pe.wait_ge(e5, i)
                for c, dst in enumerate((X, TB)):
                    for k in range(KR // P):
                        end = nc.tensor.matmul(dst[0:T, :], lhsT=ckvT[:, k, 0:T],
                                                rhs=g.w_kvb[:, k, c * 512:(c + 1) * 512], start=k == 0,
                                                stop=k == KR // P - 1)
                end.then_inc(kv_mm, 1)

            hT_of(0)
            tiles(pe, body)
            back(PT, 0)
            back(PT, 1)

        @block.scalar
        def _(act):
            def x_stats(i):
                T = width(i)
                act.wait_ge(x_in, 16 * i + 16)
                nc.scalar.activation(sq[0:T, :], x[0:T, :], ACT.Square, scale=D ** -0.5,
                                     accum_out=st[0:T, 0:1]).then_inc(xstat, 1)
                act.wait_ge(xstat, i + 1)
                nc.scalar.activation(st[0:T, 1:2], st[0:T, 0:1], ACT.Sqrt, bias=g.eps[0:T]).then_inc(xrms, 1)

            def back(i):
                T = width(i)
                cols = bass.ds(i * P, T)
                act.wait_ge(r1, i + 1)
                if not (isinstance(i, int) and i == 0):
                    act.wait_ge(st_ks, 16 * i)
                nc.scalar.activation(ksT[:, :, 0:T], TB[:, :].rearrange("p (j t) -> p j t", t=P)[:, :, 0:T],
                                     ACT.Copy).then_inc(e1, 1)
                act.wait_ge(r2, i + 1)
                if not (isinstance(i, int) and i == 0):
                    act.wait_ge(st_qm, 16 * i)
                nc.scalar.activation(qmT[:, 0:4, 0:T], X[0:MK, :].rearrange("p (j t) -> p j t", t=P)[:, :, 0:T],
                                     ACT.Copy).then_inc(e2, 1)
                act.wait_ge(r4, i + 1)
                nc.scalar.activation(g.kT_m[:, 0:4, cols],
                                     TB[0:MK, :].rearrange("p (j t) -> p j t", t=P)[:, :, 0:T],
                                     ACT.Copy).then_inc(e4, 1)
                act.wait_ge(r5, i + 1)
                nc.scalar.activation(g.kT_m[:, 4:8, cols],
                                     X[0:MK, :].rearrange("p (j t) -> p j t", t=P)[:, :, 0:T],
                                     ACT.Copy).then_inc(e5, 1)

            def body(i):
                T, first = width(i), isinstance(i, int) and i == 0
                act.wait_ge(lat_mm, i + 1)
                nc.scalar.activation(sq[0:T, 0:QR], UL[0:T, 0, 0:QR], ACT.Square, scale=QR ** -0.5,
                                     accum_out=st[0:T, 2:3])
                nc.scalar.activation(sq[0:T, QR:QR + KR], UL[0:T, 1, 0:KR], ACT.Square, scale=KR ** -0.5,
                                     accum_out=st[0:T, 3:4])
                nc.scalar.activation(sq[0:T, QR + KR:QR + KR + ROPE], UL[0:T, 1, KR:KR + ROPE], ACT.Square,
                                     scale=ROPE ** -0.5, accum_out=st[0:T, 4:5]).then_inc(lat_sq, 1)
                act.wait_ge(lat_sq, i + 1)
                nc.scalar.activation(st[0:T, 5:8], st[0:T, 2:5], ACT.Sqrt, bias=g.eps[0:T]).then_inc(lat_rms, 1)
                if not first:
                    back(i - 1)
                if not first:
                    act.wait_ge(st_k, 16 * i)
                act.wait_ge(q_mm, i + 1)
                nc.scalar.activation(qk[0:T, 0:SBH, :], U[0][0:T, :].rearrange("p (h d) -> p h d", d=SBD), ACT.Copy)
                act.wait_ge(k_mm, i + 1)
                nc.scalar.activation(qk[0:T, SBH:, :], U[1][0:T, :].rearrange("p (h d) -> p h d", d=SBD),
                                     ACT.Copy).then_inc(qk_evac, 1)
                act.wait_ge(qk_evac, i + 1)
                nc.scalar.activation(sq[0:T, :], qk[0:T, :, :].rearrange("p h d -> p (h d)"), ACT.Square,
                                     scale=SBD ** -0.5).then_inc(qk_sq, 1)
                act.wait_ge(latT_mm, i + 1)
                nc.scalar.activation(ckvT[:, :, 0:T], TB[:, 0:KR].rearrange("p (j t) -> p j t", t=P)[:, :, 0:T],
                                     ACT.Copy).then_inc(latTb_done, 1)
                act.wait_ge(qk_red, i + 1)
                nc.scalar.activation(sth[0:T, 16:32], sth[0:T, 0:16], ACT.Sqrt, bias=g.eps[0:T]
                                     ).then_inc(qk_rms, 1)
                if not last(i):
                    x_stats(i + 1)
                act.wait_ge(v_mm, i + 1)
                nc.scalar.activation(g.v_sb[0:T, i, :], U2[0:T, :], ACT.Copy).then_inc(v_evac, 1)
                act.wait_ge(qmla_mm, i + 1)
                nc.scalar.activation(qf[0:T, :, :].rearrange("p h d -> p (h d)").rearrange("p (c n) -> p c n", c=2),
                                     UL[0:T, :, 0:QR], ACT.Copy).then_inc(qm_evac, 1)
                act.wait_ge(kv_mm, i + 1)
                for c, src in enumerate((X, TB)):
                    heads = src[0:T, :].rearrange("p (h n) -> p h n", n=NOPE + MV)
                    nc.scalar.activation(kf[0:T, 4 * c:4 * c + 4, 0:NOPE], heads[:, :, 0:NOPE], ACT.Copy)
                    end = nc.scalar.activation(
                        g.v_m[0:T, i, c * 256:(c + 1) * 256].rearrange("p (h n) -> p h n", n=MV),
                        heads[:, :, NOPE:], ACT.Copy)
                end.then_inc(kv_evac, 1)
                act.wait_ge(mla_red, i + 1)
                nc.scalar.activation(sth[0:T, 24:48], sth[0:T, 0:24], ACT.Sqrt, bias=g.eps[0:T]
                                     ).then_inc(mla_rms, 1)

            x_stats(0)
            tiles(act, body)
            back(PT)

        @block.vector
        def _(dve):
            step = Steps(dve, dve_step)
            rope_c = lambda i, T: g.rope[0:T, i, 0:ROPE]
            rope_s = lambda i, T: g.rope[0:T, i, ROPE:2 * ROPE]

            def xn_of(i):
                T = width(i)
                dve.wait_ge(xrms, i + 1)
                nc.vector.reciprocal(st[0:T, 0:1], st[0:T, 1:2]).then_inc(xrec, 1)
                dve.wait_ge(xrec, i + 1)
                nc.vector.tensor_scalar(x[0:T, :], x[0:T, :], st[0:T, 0:1], None, ALU.mult).then_inc(xn_done, 1)

            def hT_of(i):
                T, b = width(i), 1 if last(i) else 0
                dve.wait_ge(ht_mm, i + 1)
                for k in range(KD):
                    end = nc.vector.tensor_scalar(hT[:, k, 0:T], U[k // 4][:, (k % 4) * P:(k % 4) * P + T],
                                                   g.scale_a[:, k, b:b + 1], g.modT[:, k, b:b + 1],
                                                   ALU.mult, ALU.add)
                end.then_inc(ht_done, 1)

            def back(i, part):
                T = width(i)
                if part == 0:
                    dve.wait_ge(r0, i + 1)
                    if not (isinstance(i, int) and i == 0):
                        dve.wait_ge(st_qs, 16 * i)
                    nc.vector.tensor_copy(qsT[:, :, 0:T], TA[:, :].rearrange("p (j t) -> p j t", t=P)[:, :, 0:T]
                                          ).then_inc(e0, 1)
                else:
                    dve.wait_ge(r3, i + 1)
                    if not (isinstance(i, int) and i == 0):
                        dve.wait_ge(st_qm, 16 * i)
                    nc.vector.tensor_copy(qmT[:, 4:8, 0:T],
                                          TA[0:MK, :].rearrange("p (j t) -> p j t", t=P)[:, :, 0:T]
                                          ).then_inc(e3, 1)

            def spread(ap, heads, width, T):
                return ap.unsqueeze(2).broadcast_to([T, heads, width])

            def body(i):
                T, first = width(i), isinstance(i, int) and i == 0
                dve.wait_ge(lat_rms, i + 1)
                step(nc.vector.reciprocal(st[0:T, 5:8], st[0:T, 5:8]))
                if not first:
                    dve.wait_ge(st_ckv, 16 * i)
                    dve.wait_ge(st_kpe, 16 * i)
                nc.vector.scalar_tensor_tensor(qlat[0:T, :], UL[0:T, 0, 0:QR], st[0:T, 5:6], row["g_qa"][0:T],
                                               ALU.mult, ALU.mult)
                nc.vector.scalar_tensor_tensor(ckv[0:T, :], UL[0:T, 1, 0:KR], st[0:T, 6:7], row["g_kva"][0:T],
                                               ALU.mult, ALU.mult).then_inc(lat_norm, 1)
                step(nc.vector.scalar_tensor_tensor(kpe[0:T, 0:ROPE], UL[0:T, 1, KR:KR + ROPE], st[0:T, 7:8],
                                                    row["g_mk_pe"][0:T], ALU.mult, ALU.mult))
                swapped = kpe[0:T, 0:ROPE].rearrange("p (a b) -> p a b", a=2)[:, ::-1, :]
                nc.vector.tensor_tensor(rot[0:T, 0, :].rearrange("p (a b) -> p a b", a=2), swapped,
                                        rope_s(i, T).rearrange("p (a b) -> p a b", a=2), ALU.mult)
                step(nc.vector.tensor_tensor(rot[0:T, 1, :], kpe[0:T, 0:ROPE], rope_c(i, T), ALU.mult))
                nc.vector.tensor_tensor(kpe[0:T, ROPE:2 * ROPE], rot[0:T, 0, :], rot[0:T, 1, :], ALU.add
                                        ).then_inc(kpe_done, 1)
                if not first:
                    back(i - 1, 0)
                    back(i - 1, 1)
                dve.wait_ge(latT_mm, i + 1)
                nc.vector.tensor_copy(qlatT[:, :, 0:T], TA[:, 0:QR].rearrange("p (j t) -> p j t", t=P)[:, :, 0:T]
                                      ).then_inc(latTa_done, 1)
                dve.wait_ge(qk_sq, i + 1)
                nc.vector.tensor_reduce(sth[0:T, 0:16], sq[0:T, :].rearrange("p (h d) -> p h d", d=SBD), AX.X,
                                        ALU.add).then_inc(qk_red, 1)
                dve.wait_ge(qk_rms, i + 1)
                step(nc.vector.reciprocal(sth[0:T, 16:32], sth[0:T, 16:32]))
                step(nc.vector.tensor_tensor(qk[0:T], qk[0:T], spread(sth[0:T, 16:32], 16, SBD, T), ALU.mult))
                for a, name in ((0, "g_sb_q"), (SBH, "g_sb_k")):
                    end = nc.vector.tensor_tensor(
                        qk[0:T, a:a + SBH, :], qk[0:T, a:a + SBH, :],
                        row[name][0:T].unsqueeze(1).broadcast_to([T, SBH, SBD]), ALU.mult)
                end.then_inc(qk_norm, 1)
                if not last(i):
                    xn_of(i + 1)
                    hT_of(i + 1)
                dve.wait_ge(qm_evac, i + 1)
                step(nc.vector.tensor_tensor(sq[0:T, 0:768], qf[0:T].rearrange("p h d -> p (h d)"),
                                             qf[0:T].rearrange("p h d -> p (h d)"), ALU.mult))
                sqh = sq[0:T, 0:768].rearrange("p (h d) -> p h d", d=MK)
                nc.vector.tensor_reduce(sth[0:T, 0:8], sqh[:, :, 0:NOPE], AX.X, ALU.add)
                step(nc.vector.tensor_reduce(sth[0:T, 16:24], sqh[:, :, NOPE:], AX.X, ALU.add))
                dve.wait_ge(kv_evac, i + 1)
                kn = sq[0:T, 0:512].rearrange("p (h d) -> p h d", d=NOPE)
                step(nc.vector.tensor_tensor(kn, kf[0:T, :, 0:NOPE], kf[0:T, :, 0:NOPE], ALU.mult))
                step(nc.vector.tensor_reduce(sth[0:T, 8:16], kn, AX.X, ALU.add))
                nc.vector.tensor_scalar(sth[0:T, 0:16], sth[0:T, 0:16], 1.0 / NOPE, None, ALU.mult)
                nc.vector.tensor_scalar(sth[0:T, 16:24], sth[0:T, 16:24], 1.0 / ROPE, None, ALU.mult
                                        ).then_inc(mla_red, 1)
                dve.wait_ge(mla_rms, i + 1)
                step(nc.vector.reciprocal(sth[0:T, 24:48], sth[0:T, 24:48]))
                nc.vector.tensor_tensor(qf[0:T, :, 0:NOPE], qf[0:T, :, 0:NOPE],
                                        spread(sth[0:T, 24:32], MH, NOPE, T), ALU.mult)
                nc.vector.tensor_tensor(kf[0:T, :, 0:NOPE], kf[0:T, :, 0:NOPE],
                                        spread(sth[0:T, 32:40], MH, NOPE, T), ALU.mult)
                step(nc.vector.tensor_tensor(qf[0:T, :, NOPE:], qf[0:T, :, NOPE:],
                                             spread(sth[0:T, 40:48], MH, ROPE, T), ALU.mult))
                gain = lambda name, w: row[name][0:T].unsqueeze(1).broadcast_to([T, MH, w])
                nc.vector.tensor_tensor(qf[0:T, :, 0:NOPE], qf[0:T, :, 0:NOPE], gain("g_mq_nope", NOPE), ALU.mult)
                nc.vector.tensor_tensor(kf[0:T, :, 0:NOPE], kf[0:T, :, 0:NOPE], gain("g_mk_nope", NOPE), ALU.mult)
                nc.vector.tensor_copy(kf[0:T, :, NOPE:],
                                      kpe[0:T, ROPE:2 * ROPE].unsqueeze(1).broadcast_to([T, MH, ROPE]))
                step(nc.vector.tensor_tensor(qf[0:T, :, NOPE:], qf[0:T, :, NOPE:], gain("g_mq_pe", ROPE), ALU.mult))
                half = ROPE // 2
                for a, b in ((0, half), (half, 0)):
                    end = nc.vector.tensor_tensor(
                        rot[0:T, :, a:a + half], qf[0:T, :, NOPE + b:NOPE + b + half],
                        rope_s(i, T)[:, a:a + half].unsqueeze(1).broadcast_to([T, MH, half]), ALU.mult)
                step(end)
                step(nc.vector.tensor_tensor(qf[0:T, :, NOPE:], qf[0:T, :, NOPE:],
                                             rope_c(i, T).unsqueeze(1).broadcast_to([T, MH, ROPE]), ALU.mult))
                nc.vector.tensor_tensor(qf[0:T, :, NOPE:], qf[0:T, :, NOPE:], rot[0:T], ALU.add
                                        ).then_inc(mla_norm, 1)

            dve.wait_ge(g.w_small_loaded, 48)
            xn_of(0)
            hT_of(0)
            tiles(dve, body, step)
            back(PT, 0)
            back(PT, 1)


def phase_cd(nc, io, g):
    with ExitStack() as stack:
        m = Memory(nc, stack)
        ROWG = P // DEC
        z = m.sb("c_z", [P, 4, SKEYS])
        v_s = m.sb("c_v", [P, PTILES, SBW])
        ckv_s = m.sb("c_ckv", [P, PTILES, KR])
        work = m.sb("c_work", [P, 5632])
        kc = work[:, 0:1024].rearrange("p (b n) -> p b n", b=2)
        cc = work[:, 1024:1536].rearrange("p (b n) -> p b n", b=2)
        kT4 = work[:, 1536:2560].rearrange("p (b j n) -> p b j n", b=2, j=4)
        kf = work[:, 2560:4096].rearrange("p (b h n) -> p b h n", b=2, h=MH)
        kTm = work[0:MK, 4096:5120].rearrange("p (h n) -> p h n", h=MH)
        sq = work[:, 5120:5632].rearrange("p (h n) -> p h n", h=MH)
        stick = work[:, 0:2 * (SKEYS + 1)].rearrange("p (a n) -> p a n", a=2)
        pc = m.sb("c_pc", [P, 2, ROPE])
        ccT = m.sb("c_ccT", [P, KR // P, P])
        ms = m.sb("c_ms", [P, 2 * MH])
        qbd = m.sb("c_qbd", [P, 4, 2 * DEC])
        qm = m.sb("c_qm", [MK, MH, DEC])
        ksn = m.sb("c_ksn", [P, 4, DEC])
        wT = m.sb("c_wT", [P, PTILES + 1, P])
        pcn = m.sb("c_pcn", [P, KR])
        pcT = m.sb("c_pcT", [P, KR // P, P])
        sm = m.sb("c_sm", [P, 8])
        o_s = m.sb("c_o", [DEC, D])
        A, B, C, DB, E, F = (m.ps(n, [P, 512]) for n in ("c_A", "c_B", "c_C", "c_D", "c_E", "c_F"))
        (kc0, kc1, cc0, cc1, pc0, pc1, q_in, v_in, ckv_in, z0, t1a, t1b, a_done, b_done, kn_mm, c_done, ms_done,
         rms_done, kn_done, t2, d_done, e_done, z_mm, z_done, masked, dve_step, pool_step, prob, tr, evA, evB,
         pv, o_done, pcn_done, pcT_mm, pcT_done, om, s_done, mx_done, st_o) = m.sems(
            "c_kc0 c_kc1 c_cc0 c_cc1 c_pc0 c_pc1 c_q_in c_v_in c_ckv_in c_zero c_t1a c_t1b c_a c_b c_kn_mm "
            "c_c c_ms c_rms c_kn c_t2 c_d c_e c_z_mm c_z_done c_masked c_dve_step c_pool_step c_prob c_tr c_evA "
            "c_evB c_pv c_o_done c_pcn_done c_pcT_mm c_pcT_done c_om c_s_done c_mx c_st_o")
        kc_in, cc_in, pc_in = (kc0, kc1), (cc0, cc1), (pc0, pc1)
        block = stack.enter_context(nc.Block())
        gain = g.rows[:, slice(*ROWS["g_mk_nope"])]
        w_nope = g.w_kvb[:].rearrange("p k (h n) -> p k h n", n=NOPE + MV)

        def tiles(engine, parts, steps=None, per=0):
            def step(j, b):
                for lag, part in parts:
                    if not isinstance(j, int) or 0 <= 2 * j + b - lag < PTILES:
                        part(j * 2 + (b - lag), (b - lag) % 2, j + (b - lag) // 2)

            for t in range(4):
                step(t // 2, t % 2)
            if steps:
                steps.straight()
            with engine.Fori(2, PTILES // 2) as j:
                if steps:
                    steps.enter(j - 2, 2 * per)
                for b in range(2):
                    step(j, b)
            if steps:
                steps.leave(PTILES // 2 - 2)
            for t in range(PTILES, PTILES + max(lag for lag, _ in parts)):
                step(t // 2, t % 2)

        def later(t, than=0):
            return not isinstance(t, int) or t > than

        GROUPS = range(4)
        BATCHES = [(b * 4, min(4, PTILES + 1 - b * 4)) for b in range((PTILES + 4) // 4)]

        def keys_of(t):
            return P if t < PTILES else DEC

        @block.sync
        def _(sp):
            sp.wait_ge(z0, 1)
            new = slice(SEQ, TOK)
            sp.dma_start(qbd[0:64, :, 0:DEC], g.qs_dram[:, 0:64, new].rearrange("a p t -> p a t")).then_inc(q_in, 16)
            sp.dma_start(qbd[64:P, :, DEC:], g.qs_dram[:, 64:P, new].rearrange("a p t -> p a t")).then_inc(q_in, 16)
            sp.dma_start(qm[:], g.qm_dram[:, :, new].rearrange("h p t -> p h t")).then_inc(q_in, 16)
            sp.dma_start(ksn[:], g.ks_dram[:, :, new].rearrange("a p t -> p a t")).then_inc(q_in, 16)

            def body(t, b, n):
                rows = bass.ds(t * P, P)
                if later(t, 1):
                    sp.wait_ge(t1b, t - 1)
                sp.dma_start(cc[:, b], io["cache_mla_ckv"][rows, :]).then_inc(cc_in[b], 16)
                if later(t, 1):
                    sp.wait_ge(kn_done, t - 1)
                sp.dma_start(pc[:, b], io["cache_mla_kpe"][rows, :]).then_inc(pc_in[b], 16)
                sp.dma_start(v_s[:, bass.ds(t, 1), :], io["cache_sb_v"][rows, :].unsqueeze(1)).then_inc(v_in, 16)
                sp.dma_start(ckv_s[:, bass.ds(t, 1), :], io["cache_mla_ckv"][rows, :].unsqueeze(1)
                             ).then_inc(ckv_in, 16)
                if later(t, 1):
                    sp.wait_ge(t1a, t - 1)
                sp.dma_start(kc[:, b], io["cache_sb_k"][rows, :]).then_inc(kc_in[b], 16)

            tiles(sp, ((0, body),))
            sp.wait_ge(o_done, 4)
            sp.dma_start(g.o_dram[SEQ:TOK, :], o_s[:]).then_inc(st_o, 16)
            sp.wait_ge(st_o, 16)

        @block.gpsimd
        def _(pool):
            nc.gpsimd.memset(qbd[:], 0.0).then_inc(z0, 1)
            pool.wait_ge(z_done, PTILES + 1)
            nc.gpsimd.memset(stick[:, :, SKEYS:], 1.0).then_inc(pool_step, 1)
            pool.wait_ge(pool_step, 1)
            for a in range(ROWG):
                if a:
                    pool.wait_ge(masked, a)
                part = z[a * DEC:(a + 1) * DEC, 0:2, PAST:]
                nc.gpsimd.affine_select(out=part, in_=part, compare_op=ALU.is_gt, fill=NEG, base=0,
                                        pattern=[[0, 2], [-1, DEC]], channel_multiplier=1).then_inc(masked, 1)

        @block.tensor
        def _(pe):
            def keys_turned(t, b, n):
                pe.wait_ge(kn_done, t + 1)
                if later(t):
                    pe.wait_ge(d_done, t)
                    pe.wait_ge(e_done, t)
                for c, dst in enumerate((DB, E)):
                    for j in range(4):
                        end = nc.tensor.transpose(dst[0:MK, j * P:(j + 1) * P], kf[:, b, 4 * c + j, :], g.ident[:])
                end.then_inc(t2, 1)

            def scores(t, keys_sb, keys_m, n):
                if later(t):
                    pe.wait_ge(z_done, t)
                out = F[:, :].rearrange("p (a k) -> p a k", k=P)
                for j in range(4):
                    r = (j % 2) * 2 * DEC
                    nc.tensor.matmul(out[r:r + 2 * DEC, j // 2, 0:n], lhsT=qbd[:, j, :], rhs=keys_sb(j),
                                     start=True, stop=True)
                for h in range(MH):
                    r = (h % ROWG) * DEC
                    end = nc.tensor.matmul(out[r:r + DEC, 2 + h // ROWG, 0:n], lhsT=qm[:, h, :], rhs=keys_m(h),
                                           start=True, stop=True, tile_position=(0, r))
                end.then_inc(z_mm, 1)

            def tile_scores(t, b, n):
                pe.wait_ge(a_done, t + 1)
                pe.wait_ge(d_done, t + 1)
                pe.wait_ge(e_done, t + 1)
                scores(t, lambda j: kT4[:, b, j, :], lambda h: kTm[:, h, :], P)

            def cached_turned(t, b, n):
                pe.wait_ge(kc_in[b], 16 * n + 16)
                if later(t):
                    pe.wait_ge(a_done, t)
                for j in range(4):
                    end = nc.tensor.transpose(A[:, j * P:(j + 1) * P], kc[:, b, j * P:(j + 1) * P], g.ident[:])
                end.then_inc(t1a, 1)

            def latents_turned(t, b, n):
                pe.wait_ge(cc_in[b], 16 * n + 16)
                if later(t):
                    pe.wait_ge(b_done, t)
                for j in range(KR // P):
                    end = nc.tensor.transpose(B[:, j * P:(j + 1) * P], cc[:, b, j * P:(j + 1) * P], g.ident[:])
                end.then_inc(t1b, 1)

            def latent_keys(t, b, n):
                if later(t):
                    pe.wait_ge(c_done, t)
                pe.wait_ge(b_done, t + 1)
                for k in range(KR // P):
                    end = nc.tensor.matmul(C[:, :], lhsT=ccT[:, k, :], rhs=w_nope[:, k, :, 0:NOPE],
                                           start=k == 0, stop=k == KR // P - 1)
                end.then_inc(kn_mm, 1)

            pe.wait_ge(q_in, 64)
            tiles(pe, ((0, latents_turned), (2, keys_turned), (0, latent_keys), (1, cached_turned),
                       (2, tile_scores)))
            scores(PTILES, lambda j: ksn[:, j, :], lambda h: g.kT_m[:, h, SEQ:TOK], DEC)

            pe.wait_ge(v_in, 16 * PTILES)
            pe.wait_ge(ckv_in, 16 * PTILES)
            for n, a in enumerate(GROUPS):
                pe.wait_ge(prob, n + 1)
                for i, (t0, cnt) in enumerate(BATCHES):
                    dst = (A, B)[i % 2]
                    if i % 2 == 0:
                        pe.wait_ge(evA, 3 * n + i // 2) if 3 * n + i // 2 else None
                    else:
                        pe.wait_ge(evB, 2 * n + i // 2) if 2 * n + i // 2 else None
                    for j in range(cnt):
                        k = keys_of(t0 + j)
                        end = nc.tensor.transpose(dst[0:k, j * P:(j + 1) * P],
                                                  z[:, a, (t0 + j) * P:(t0 + j) * P + k], g.ident[:])
                    end.then_inc(tr, 1)
                pe.wait_ge(evA, 3 * n + 3)
                pe.wait_ge(evB, 2 * n + 2)
                if n:
                    pe.wait_ge(o_done, n)
                for t in range(PTILES + 1):
                    k = keys_of(t)
                    if a < 2:
                        v = v_s[:, t, a * 256:(a + 1) * 256] if t < PTILES else \
                            g.v_sb[0:k, PT, a * 256:(a + 1) * 256]
                    else:
                        v = ckv_s[:, t, :] if t < PTILES else g.ckv_new[0:k, :]
                    end = nc.tensor.matmul(C[:, 0:256], lhsT=wT[0:k, t, :], rhs=v, start=t == 0, stop=t == PTILES)
                end.then_inc(pv, 1)
                if a >= 2:
                    pe.wait_ge(pcn_done, a - 1)
                    for j in range(KR // P):
                        end = nc.tensor.transpose(E[:, j * P:(j + 1) * P], pcn[:, j * P:(j + 1) * P], g.ident[:])
                    end.then_inc(pcT_mm, 1)
                    pe.wait_ge(pcT_done, a - 1)
                    for j in range(ROWG):
                        h = (a - 2) * ROWG + j
                        for k in range(KR // P):
                            end = nc.tensor.matmul(F[0:DEC, j * MV:(j + 1) * MV],
                                                   lhsT=pcT[:, k, j * DEC:(j + 1) * DEC],
                                                   rhs=w_nope[:, k, h, NOPE:], start=k == 0,
                                                   stop=k == KR // P - 1)
                    end.then_inc(om, 1)

        @block.scalar
        def _(act):
            def evac_keys(t, b, n):
                act.wait_ge(t2, t + 1)
                if later(t):
                    act.wait_ge(z_mm, t)
                nc.scalar.activation(kTm[:, 4:8, :], E[0:MK, :].rearrange("p (j t) -> p j t", t=P), ACT.Copy
                                     ).then_inc(e_done, 1)

            def evac_scores(t, b=0, n=0, keys=P):
                act.wait_ge(z_mm, t + 1)
                nc.scalar.activation(z[:, :, bass.ds(t * P, keys)],
                                     F[:, :].rearrange("p (a k) -> p a k", k=P)[:, :, 0:keys], ACT.Copy
                                     ).then_inc(z_done, 1)

            def evac_latents(t, b, n):
                act.wait_ge(t1b, t + 1)
                if later(t):
                    act.wait_ge(kn_mm, t)
                nc.scalar.activation(ccT[:], B[:, 0:KR].rearrange("p (j t) -> p j t", t=P), ACT.Copy
                                     ).then_inc(b_done, 1)

            def norm(t, b, n):
                act.wait_ge(kn_mm, t + 1)
                if later(t, 1):
                    act.wait_ge(t2, t - 1)
                nc.scalar.activation(kf[:, b, :, 0:NOPE], C[:, :].rearrange("p (h n) -> p h n", n=NOPE), ACT.Copy
                                     ).then_inc(c_done, 1)
                act.wait_ge(ms_done, t + 1)
                nc.scalar.activation(ms[:, MH:], ms[:, 0:MH], ACT.Sqrt, bias=g.eps[:], scale=1.0 / NOPE
                                     ).then_inc(rms_done, 1)

            tiles(act, ((0, evac_latents), (2, evac_keys), (0, norm), (2, evac_scores)))
            evac_scores(PTILES, keys=DEC)

            act.wait_ge(masked, ROWG)
            act.wait_ge(pool_step, 1)
            act.wait_ge(z_done, PTILES + 1)

            def weights(a):
                if a < 2:
                    nc.scalar.activation(stick[:, a, 0:SKEYS], z[:, a, :], ACT.Sigmoid, scale=-SB_SCALE
                                         ).then_inc(s_done, 1)
                    act.wait_ge(s_done, 2 * a + 1)
                    nc.scalar.activation(z[:, a, :], z[:, a, :], ACT.Sigmoid, scale=SB_SCALE).then_inc(s_done, 1)
                else:
                    act.wait_ge(mx_done, a - 1)
                    nc.scalar.activation(z[:, a, :], z[:, a, :], ACT.Exp, bias=sm[:, a:a + 1],
                                         scale=MLA_SCALE, accum_out=sm[:, 2 + a:3 + a]).then_inc(prob, 1)

            weights(0)
            weights(1)
            for n, a in enumerate(GROUPS):
                for i in (1, 3):
                    t0, cnt = BATCHES[i]
                    act.wait_ge(tr, 5 * n + i + 1)
                    if n:
                        act.wait_ge(pv, n)
                    nc.scalar.activation(wT[:, t0:t0 + cnt, :], B[:, 0:cnt * P].rearrange("p (j t) -> p j t", t=P),
                                         ACT.Copy).then_inc(evB, 1)
                if 2 <= a + 1 < 4:
                    weights(a + 1)
                if a >= 2:
                    act.wait_ge(pcT_mm, a - 1)
                    nc.scalar.activation(pcT[:], E[:, 0:KR].rearrange("p (j t) -> p j t", t=P), ACT.Copy
                                         ).then_inc(pcT_done, 1)

        @block.vector
        def _(dve):
            step = Steps(dve, dve_step)

            def evac_keys(t, b, n):
                dve.wait_ge(t2, t + 1)
                if later(t):
                    dve.wait_ge(z_mm, t)
                nc.vector.tensor_copy(kTm[:, 0:4, :], DB[0:MK, :].rearrange("p (j t) -> p j t", t=P)
                                      ).then_inc(d_done, 1)

            def evac_cached(t, b, n):
                dve.wait_ge(t1a, t + 1)
                if later(t, 1):
                    dve.wait_ge(z_mm, t - 1)
                nc.vector.tensor_copy(kT4[:, b], A[:, :].rearrange("p (j t) -> p j t", t=P)).then_inc(a_done, 1)

            def norm(t, b, n):
                f = kf[:, b, :, 0:NOPE]
                dve.wait_ge(c_done, t + 1)
                step(nc.vector.tensor_tensor(sq[:], f, f, ALU.mult))
                nc.vector.tensor_reduce(ms[:, 0:MH], sq[:], AX.X, ALU.add).then_inc(ms_done, 1)
                dve.wait_ge(pc_in[b], 16 * n + 16)
                nc.vector.tensor_copy(kf[:, b, :, NOPE:], pc[:, b, :].unsqueeze(1).broadcast_to([P, MH, ROPE]))
                dve.wait_ge(rms_done, t + 1)
                step(nc.vector.reciprocal(ms[:, MH:], ms[:, MH:]))
                step(nc.vector.tensor_tensor(f, f, ms[:, MH:].unsqueeze(2).broadcast_to([P, MH, NOPE]), ALU.mult))
                nc.vector.tensor_tensor(f, f, gain.unsqueeze(1).broadcast_to([P, MH, NOPE]), ALU.mult
                                        ).then_inc(kn_done, 1)

            tiles(dve, ((2, evac_keys), (0, norm), (1, evac_cached)), step, 3)

            dve.wait_ge(z_done, PTILES + 1)

            def weights(a):
                if a < 2:
                    dve.wait_ge(s_done, 2 * a + 1)
                    back = stick[:, a, 0:SKEYS][:, ::-1]
                    step(nc.vector.tensor_tensor_scan(back, back, back, 1.0, ALU.mult, ALU.bypass))
                    dve.wait_ge(s_done, 2 * a + 2)
                    nc.vector.tensor_tensor(z[:, a, :], z[:, a, :], stick[:, a, 1:], ALU.mult).then_inc(prob, 1)
                else:
                    step(nc.vector.tensor_reduce(sm[:, 6:7], z[:, a, :], AX.X, ALU.max))
                    nc.vector.tensor_scalar(sm[:, a:a + 1], sm[:, 6:7], -MLA_SCALE, None, ALU.mult
                                            ).then_inc(mx_done, 1)
                    dve.wait_ge(mx_done, a - 1)

            dve.wait_ge(pool_step, 1)
            dve.wait_ge(masked, ROWG)
            weights(0)
            for n, a in enumerate(GROUPS):
                for i in (0, 2, 4):
                    t0, cnt = BATCHES[i]
                    dve.wait_ge(tr, 5 * n + i + 1)
                    if n:
                        dve.wait_ge(pv, n)
                    k = keys_of(t0)
                    nc.vector.tensor_copy(wT[0:k, t0:t0 + cnt, :],
                                          A[0:k, 0:cnt * P].rearrange("p (j t) -> p j t", t=P)).then_inc(evA, 1)
                if a + 1 < 4:
                    weights(a + 1)
                dve.wait_ge(pv, n + 1)
                if a < 2:
                    for j in range(ROWG):
                        h = a * ROWG + j
                        end = nc.vector.tensor_copy(o_s[:, h * SBD:(h + 1) * SBD],
                                                    C[j * DEC:(j + 1) * DEC, j * SBD:(j + 1) * SBD])
                    end.then_inc(o_done, 1)
                else:
                    step(nc.vector.reciprocal(sm[:, 2 + a:3 + a], sm[:, 2 + a:3 + a]))
                    nc.vector.tensor_scalar(pcn[:], C[:, 0:256], sm[:, 2 + a:3 + a], None, ALU.mult
                                            ).then_inc(pcn_done, 1)
                    dve.wait_ge(om, a - 1)
                    nc.vector.tensor_copy(o_s[:, SBW + (a - 2) * 256:SBW + (a - 1) * 256], F[0:DEC, 0:256]
                                          ).then_inc(o_done, 1)


def phase_e(nc, io, g):
    with ExitStack() as stack:
        m = Memory(nc, stack)
        UNITS = 2 * PT
        PAIRS = SBH // 2
        TR, PV, WBUFS = 2, 3, 4
        q_s = m.sb("e_q_s", [P, 2, SEQ])
        q_m = m.sb("e_q_m", [MK, 2, SEQ])
        keys = m.sb("e_keys", [P, PAIRS, SEQ])
        stick = m.sb("e_stick", [P, 2, SEQ + 1])
        w = m.sb("e_w", [P, WBUFS, SEQ])
        wT = m.sb("e_wT", [P, 2, PT, P])
        o = m.sb("e_o", [P, 2, PT, SBD])
        sm = m.sb("e_sm", [P, WBUFS, 4])
        Z = [m.ps(f"e_Z{b}", [P, SEQ]) for b in range(2)]
        TA, TB = (m.ps(x, [P, 512]) for x in ("e_TA", "e_TB"))
        O = [m.ps(f"e_O{b}", [P, 512]) for b in range(2)]
        (zero, keys_in, keys_in2, z_mm, z_read, s_done, w_done, tr_a, tr_b, evA, evB, pv, o_done,
         mx_done, dve_step) = m.sems(
            "e_zero e_keys_in e_keys_in2 e_z_mm e_z_read e_s_done e_w_done e_tr_a e_tr_b e_evA e_evB e_pv e_o_done "
            "e_mx_done e_dve_step")
        q_in = (m.sems("e_qs_in0 e_qs_in1"), m.sems("e_qm_in0 e_qm_in1"))
        st_o = m.sems("e_st_o0 e_st_o1")
        block = stack.enter_context(nc.Block())
        BIG = [t >= 4 for t in range(PT)] * 2

        def big(latent, p, u):
            return (latent * PAIRS + p) * sum(BIG) + sum(BIG[:u])

        def unit(latent, p, u):
            return (latent * PAIRS + p) * UNITS + u, u % PT, u // PT

        def first(latent, p, u, n=1):
            return not latent and isinstance(p, int) and p == 0 and u < n

        def units(engine, body, behind, steps=None, per=(0, 0)):
            def turn(latent, p, u):
                body(latent, p, u)
                for lag, part in behind:
                    if u >= lag:
                        part(latent, p, u - lag)
                    elif not (isinstance(p, int) and p == 0):
                        part(latent, p - 1, u - lag + UNITS)
                    elif latent:
                        part(0, PAIRS - 1, u - lag + UNITS)

            for latent in range(2):
                for u in range(UNITS):
                    turn(latent, 0, u)
                if steps:
                    steps.straight()
                with engine.Fori(1, PAIRS) as p:
                    if steps:
                        steps.enter(p - 1, per[latent])
                    for u in range(UNITS):
                        turn(latent, p, u)
                if steps:
                    steps.leave(PAIRS - 1)
            for u in range(UNITS, UNITS + PV):
                for lag, part in behind:
                    if u - lag < UNITS:
                        part(1, PAIRS - 1, u - lag)

        @block.sync
        def _(sp):
            def load_q(latent, p, hh):
                if latent:
                    sp.dma_start(q_m[:, hh, :], g.qm_dram[2 * p + hh, :, 0:SEQ]).then_inc(q_in[1][hh], 16)
                else:
                    r = slice(hh * SBD, (hh + 1) * SBD)
                    sp.dma_start(q_s[r, hh, :], g.qs_dram[p, r, 0:SEQ]).then_inc(q_in[0][hh], 16)

            sp.dma_start(keys[:, 0, :], g.ks_dram[0, :, 0:SEQ]).then_inc(keys_in, 16)
            for hh in range(2):
                load_q(0, 0, hh)
            sp.dma_start(keys[:, 1:, :], g.ks_dram[1:, :, 0:SEQ].rearrange("a p t -> p a t")).then_inc(keys_in2, 16)
            for hh in range(2):
                load_q(1, 0, hh)

            def store(latent, p, hh):
                sp.wait_ge(o_done, (latent * PAIRS + p) * UNITS + (hh + 1) * PT)
                col = bass.ds((SBW if latent else 0) + (2 * p + hh) * SBD, SBD)
                sp.dma_start(g.o_dram[0:SEQ, col].rearrange("(t p) c -> p t c", p=P), o[:, hh]
                             ).then_inc(st_o[hh], 16)

            for latent in range(2):
                with sp.Fori(0, PAIRS - 1) as p:
                    for hh in range(2):
                        sp.wait_ge(z_mm, (latent * PAIRS + p) * UNITS + (hh + 1) * PT)
                        load_q(latent, p + 1, hh)
                        store(latent, p, hh)
                for hh in range(2):
                    store(latent, PAIRS - 1, hh)
            for hh in range(2):
                sp.wait_ge(st_o[hh], 16 * 2 * PAIRS)

        @block.gpsimd
        def _(pool):
            nc.gpsimd.memset(q_s[SBD:P, 0, :], 0.0).then_inc(zero, 1)
            pool.wait_ge(zero, 1)
            nc.gpsimd.memset(q_s[0:SBD, 1, :], 0.0).then_inc(zero, 1)
            pool.wait_ge(zero, 2)
            nc.gpsimd.memset(stick[:, :, SEQ:], 1.0).then_inc(zero, 1)

        @block.tensor
        def _(pe):
            def transpose(latent, p, u):
                n, t, hh = unit(latent, p, u)
                pe.wait_ge(w_done, n + 1)
                if not first(latent, p, u):
                    pe.wait_ge(evA, n)
                for j in range(min(4, t + 1)):
                    src = w[:, u % WBUFS, SEQ - (t + 1 - j) * P:SEQ - (t - j) * P]
                    end = nc.tensor.transpose(TA[:, j * P:(j + 1) * P], src, g.ident[:])
                end.then_inc(tr_a, 1)
                if BIG[u]:
                    nb = big(latent, p, u)
                    if not (isinstance(nb, int) and nb == 0):
                        pe.wait_ge(evB, nb)
                    for j in range(4, t + 1):
                        src = w[:, u % WBUFS, SEQ - (t + 1 - j) * P:SEQ - (t - j) * P]
                        end = nc.tensor.transpose(TB[:, (j - 4) * P:(j - 3) * P], src, g.ident[:])
                    end.then_inc(tr_b, 1)

            def product(latent, p, u):
                n, t, hh = unit(latent, p, u)
                b = u % 2
                values = g.v_m if latent else g.v_sb
                pe.wait_ge(evA, n + 1)
                if not first(latent, p, u, 2):
                    pe.wait_ge(o_done, n - 1)
                col = (2 * p + hh) * SBD
                for j in range(t + 1):
                    if j == 4:
                        pe.wait_ge(evB, big(latent, p, u) + 1)
                    end = nc.tensor.matmul(O[b][:, 0:SBD], lhsT=wT[:, b, j, :], rhs=values[:, j, bass.ds(col, SBD)],
                                           start=j == 0, stop=j == t)
                end.then_inc(pv, 1)

            def body(latent, p, u):
                n, t, hh = unit(latent, p, u)
                if u % PT == 0:
                    pe.wait_ge(q_in[latent][hh], 16 * p + 16)
                if u == 0 and not latent and not isinstance(p, int):
                    pe.wait_ge(keys_in2, 16)
                if not first(latent, p, u, 2):
                    pe.wait_ge(w_done, n - 1)
                q, mask = (q_m, g.mask_mla) if latent else (q_s, g.mask_sb)
                for c in range(0, (t + 1) * P, 512):
                    c1 = min(c + 512, (t + 1) * P)
                    rhs = g.kT_m[:, 2 * p + hh, c:c1] if latent else keys[:, p, c:c1]
                    nc.tensor.matmul(Z[u % 2][:, c:c1], lhsT=q[:, hh, t * P:(t + 1) * P], rhs=rhs, start=True,
                                     stop=c1 < (t + 1) * P)
                nc.tensor.matmul(Z[u % 2][:, t * P:(t + 1) * P], lhsT=g.identb[:], rhs=mask[:], start=False,
                                 stop=True).then_inc(z_mm, 1)

            pe.wait_ge(keys_in, 16)
            pe.wait_ge(zero, 3)
            units(pe, body, ((TR, transpose), (PV, product)))

        @block.scalar
        def _(act):
            def out_a(latent, p, u):
                n, t, hh = unit(latent, p, u)
                act.wait_ge(tr_a, n + 1)
                if not first(latent, p, u, 2):
                    act.wait_ge(pv, n - 1)
                cnt = min(4, t + 1)
                nc.scalar.activation(wT[:, u % 2, 0:cnt, :], TA[:, 0:cnt * P].rearrange("p (j t) -> p j t", t=P),
                                     ACT.Copy).then_inc(evA, 1)

            def body(latent, p, u):
                n, t, hh = unit(latent, p, u)
                b, bw, W = u % 2, u % WBUFS, (t + 1) * P
                act.wait_ge(z_mm, n + 1)
                if latent:
                    act.wait_ge(mx_done, n - PAIRS * UNITS + 1)
                    act.wait_ge(pv, n - (WBUFS - 1))
                    act.wait_ge(o_done, n - (WBUFS - 1))
                    nc.scalar.activation(w[:, bw, SEQ - W:], Z[b][:, 0:W], ACT.Exp, bias=sm[:, bw, 1:2],
                                         scale=MLA_SCALE, accum_out=sm[:, bw, 2:3]).then_inc(w_done, 1)
                else:
                    if not first(latent, p, u, 2):
                        act.wait_ge(w_done, n - 1)
                    nc.scalar.activation(stick[:, b, SEQ - W:SEQ], Z[b][:, 0:W], ACT.Sigmoid, scale=-SB_SCALE
                                         ).then_inc(s_done, 1)
                    if not first(latent, p, u, WBUFS):
                        act.wait_ge(pv, n - (WBUFS - 1))
                    nc.scalar.activation(w[:, bw, SEQ - W:], Z[b][:, 0:W], ACT.Sigmoid, scale=SB_SCALE
                                         ).then_inc(z_read, 1)

            units(act, body, ((TR, out_a),))

        @block.vector
        def _(dve):
            step = Steps(dve, dve_step)

            def evac_b(latent, p, u):
                n, t, hh = unit(latent, p, u)
                if BIG[u]:
                    dve.wait_ge(tr_b, big(latent, p, u) + 1)
                    if not first(latent, p, u, 2):
                        dve.wait_ge(pv, n - 1)
                    nc.vector.tensor_copy(wT[:, u % 2, 4:t + 1, :],
                                          TB[:, 0:(t - 3) * P].rearrange("p (j t) -> p j t", t=P)).then_inc(evB, 1)

            def out(latent, p, u):
                n, t, hh = unit(latent, p, u)
                b, bw = u % 2, u % WBUFS
                dve.wait_ge(pv, n + 1)
                if u % PT == 0 and (latent or not (isinstance(p, int) and p == 0)):
                    dve.wait_ge(st_o[hh], 16 * (latent * PAIRS + p))
                if latent:
                    step(nc.vector.reciprocal(sm[:, bw, 3:4], sm[:, bw, 2:3]))
                    nc.vector.tensor_scalar(o[:, hh, t, :], O[b][:, 0:SBD], sm[:, bw, 3:4], None, ALU.mult
                                            ).then_inc(o_done, 1)
                else:
                    nc.vector.tensor_copy(o[:, hh, t, :], O[b][:, 0:SBD]).then_inc(o_done, 1)

            def body(latent, p, u):
                n, t, hh = unit(latent, p, u)
                b, bw, W = u % 2, u % WBUFS, (t + 1) * P
                if latent:
                    dve.wait_ge(z_mm, n + 1)
                    step(nc.vector.tensor_reduce(sm[:, bw, 0:1], Z[b][:, 0:W], AX.X, ALU.max))
                    dve.wait_ge(w_done, n - (WBUFS - 1))
                    nc.vector.tensor_scalar(sm[:, bw, 1:2], sm[:, bw, 0:1], -MLA_SCALE, None, ALU.mult
                                            ).then_inc(mx_done, 1)
                else:
                    dve.wait_ge(s_done, n + 1)
                    back = stick[:, b, SEQ - W:SEQ][:, ::-1]
                    step(nc.vector.tensor_tensor_scan(back, back, back, 1.0, ALU.mult, ALU.bypass))
                    dve.wait_ge(z_read, n + 1)
                    nc.vector.tensor_tensor(w[:, bw, SEQ - W:], w[:, bw, SEQ - W:], stick[:, b, SEQ - W + 1:],
                                            ALU.mult).then_inc(w_done, 1)

            dve.wait_ge(zero, 3)
            units(dve, body, ((TR, evac_b), (PV, out)), step, (UNITS, 2 * UNITS))


def phase_f(nc, io, g):
    with ExitStack() as stack:
        m = Memory(nc, stack)
        wo = m.sb("f_wo", [P, KD, D])
        wr = m.sb("f_wr", [P, KD, NG + NE])
        rows = m.sb("f_rows", [P, 3, 2, D])
        o = m.sb("f_o", [P, D])
        oT = m.sb("f_oT", [P, KD, P])
        xr = m.sb("f_xr", [P, D])
        h2 = m.sb("f_h2", [P, D])
        h2T = m.sb("f_h2T", [P, 2, KD, P])
        sq = m.sb("f_sq", [P, D])
        st = m.sb("f_st", [P, 3])
        zero = m.sb("f_zero", [1, D])
        LROWS = NE * REGION // P
        rown = m.sb("f_rown", [P, LROWS], I32)
        padt = m.sb("f_padt", [P, LROWS], I32)
        rowf = m.sb("f_rowf", [P, LROWS])
        pad = m.sb("f_pad", [P, LROWS, 2], U32)
        A = m.ps("f_A", [P, D])
        B = m.ps("f_B", [P, D])
        C = m.ps("f_C", [P, D])
        R = m.ps("f_R", [P, 512])
        w_in = m.sems("f_w_in0 f_w_in1")
        (r_in, o_in, x_in, z0, z_out, row_mm, row_done, oT_mm, oT_done, pr_mm, x2_done, ssq, rms, h2_done,
         h2T_mm, h2T_done, rt_mm, rt_done, st_h2, dve_step, pool_step, pad_done) = m.sems(
            "f_r_in f_o_in f_x_in f_z0 f_z_out f_row_mm f_row_done f_oT_mm f_oT_done f_pr_mm f_x2_done "
            "f_ssq f_rms f_h2_done f_h2T_mm f_h2T_done f_rt_mm f_rt_done f_st_h2 f_dve_step f_pool_step f_pad_done")
        block = stack.enter_context(nc.Block())
        bias = g.rows[:, ROWS["b_rg"][0]:ROWS["b_re"][1]]

        def last(i):
            return isinstance(i, int) and i == PT

        def width(i):
            return DEC if last(i) else P

        FIRST = 4

        def tiles(engine, parts, steps=None, per=0):
            def step(i, odd):
                for lag, part in parts:
                    if not isinstance(i, int) or 0 <= i - lag <= PT:
                        part(i - lag, (odd + lag) % 2)

            for i in range(FIRST):
                step(i, i % 2)
            if steps:
                steps.straight()
            with engine.Fori(FIRST // 2, PT // 2) as j:
                if steps:
                    steps.enter(j - FIRST // 2, 2 * per)
                for odd in range(2):
                    step(j * 2 + odd, odd)
            if steps:
                steps.leave((PT - FIRST) // 2)
            for i in range(PT, PT + 1 + max(lag for lag, _ in parts)):
                step(i, i % 2)

        def later(i):
            return not (isinstance(i, int) and i == 0)

        SPREADS = [(rows[:, 0, b, :], g.modT[:, 16:24, b]) for b in range(2)] + \
                  [(rows[:, 1, b, :], g.scale_m[:, :, b]) for b in range(2)] + \
                  [(rows[:, 2, b, :], g.modT[:, 24:32, b]) for b in range(2)] + \
                  [(g.gate_m[:, b, :], g.modT[:, 40:48, b]) for b in range(2)]

        @block.sync
        def _(sp):
            w_out = io["w_out"].rearrange("(k p) n -> p k n", p=P)

            def the_rest():
                sp.dma_start(wr[:, :, 0:NG], io["w_rg"].rearrange("(k p) n -> p k n", p=P)).then_inc(r_in, 16)
                sp.dma_start(wr[:, :, NG:], io["w_re"].rearrange("(k p) n -> p k n", p=P)).then_inc(r_in, 16)
                sp.wait_ge(z0, 1)
                sp.wait_ge(pad_done, 1)
                sp.dma_start(g.h2_dram[PAD:PAD + 1, :], zero[:]).then_inc(z_out, 16)
                sp.dma_start(g.list_dram.rearrange("(p n) o -> p n o", p=P), pad[:]).then_inc(z_out, 16)

            def halves():
                for c in range(2):
                    sp.dma_start(wo[:, :, c * 512:(c + 1) * 512], w_out[:, :, c * 512:(c + 1) * 512]
                                 ).then_inc(w_in[c], 16)

            def store(i):
                sp.wait_ge(h2_done, i + 1)
                sp.dma_start(g.h2_dram[bass.ds(i * P, width(i)), :], h2[0:width(i), :]).then_inc(st_h2, 16)

            def body(i, odd):
                T = width(i)
                if later(i):
                    sp.wait_ge(oT_mm, i)
                sp.dma_start(o[0:T, :], g.o_dram[bass.ds(i * P, T), :]).then_inc(o_in, 16)
                if later(i):
                    sp.wait_ge(x2_done, i)
                x = io["x_sample"] if last(i) else io["x_prompt"][bass.ds(i * P, P), :]
                sp.dma_start(xr[0:T, :], x).then_inc(x_in, 16)
                if later(i):
                    store(i - 1)
                else:
                    halves()
                    the_rest()

            tiles(sp, ((0, body),))
            store(PT)
            sp.wait_ge(st_h2, 16 * NT)
            sp.wait_ge(z_out, 32)

        @block.gpsimd
        def _(pool):
            nc.gpsimd.iota(rown[:], pattern=[[1, LROWS]], base=0, channel_multiplier=LROWS).then_inc(pool_step, 1)
            pool.wait_ge(pool_step, 1)
            nc.gpsimd.iota(padt[:], pattern=[[0, LROWS]], base=PAD, channel_multiplier=0).then_inc(pool_step, 1)
            pool.wait_ge(pool_step, 2)
            nc.gpsimd.memset(zero[:], 0.0).then_inc(z0, 1)

        @block.tensor
        def _(pe):
            for n, (_, col) in enumerate(SPREADS):
                dst = (A, B, C)[n % 3]
                if n >= 3:
                    pe.wait_ge(row_done, n - 2)
                for k in range(KD):
                    end = nc.tensor.transpose(dst[:, k * P:(k + 1) * P], col[:, k:k + 1].broadcast_to([P, P]),
                                              g.ident[:])
                end.then_inc(row_mm, 1)
            pe.wait_ge(row_done, len(SPREADS))

            def turned(i, odd):
                T = width(i)
                pe.wait_ge(o_in, 16 * i + 16)
                if later(i):
                    pe.wait_ge(oT_done, i)
                for k in range(KD):
                    end = nc.tensor.transpose(A[:, k * P:k * P + T], o[0:T, k * P:(k + 1) * P], g.ident[0:T, 0:T])
                end.then_inc(oT_mm, 1)

            def projected(i, odd):
                T = width(i)
                if later(i):
                    pe.wait_ge(x2_done, i)
                pe.wait_ge(oT_done, i + 1)
                for c in range(2):
                    if not later(i):
                        pe.wait_ge(w_in[c], 16)
                    for k in range(KD):
                        end = nc.tensor.matmul(C[0:T, c * 512:(c + 1) * 512], lhsT=oT[:, k, 0:T],
                                               rhs=wo[:, k, c * 512:(c + 1) * 512], start=k == 0, stop=k == KD - 1)
                end.then_inc(pr_mm, 1)

            def normed_turned(i, odd):
                T = width(i)
                pe.wait_ge(h2_done, i + 1)
                if later(i):
                    pe.wait_ge(h2T_done, i)
                for k in range(KD):
                    end = nc.tensor.transpose(B[:, k * P:k * P + T], h2[0:T, k * P:(k + 1) * P],
                                              g.ident[0:T, 0:T])
                end.then_inc(h2T_mm, 1)

            def routed(i, odd):
                T = width(i)
                pe.wait_ge(h2T_done, i + 1)
                if later(i):
                    pe.wait_ge(rt_done, i)
                else:
                    pe.wait_ge(r_in, 32)
                for k in range(KD):
                    end = nc.tensor.matmul(R[0:T, 0:NG + NE], lhsT=h2T[:, odd, k, 0:T], rhs=wr[:, k, :],
                                           start=k == 0, stop=k == KD - 1)
                end.then_inc(rt_mm, 1)

            tiles(pe, ((0, turned), (2, normed_turned), (3, routed), (0, projected)))

        @block.scalar
        def _(act):
            for n, (dst, _) in enumerate(SPREADS):
                act.wait_ge(row_mm, n + 1)
                nc.scalar.activation(dst, (A, B, C)[n % 3][:], ACT.Copy).then_inc(row_done, 1)

            def o_out(i, odd):
                T = width(i)
                act.wait_ge(oT_mm, i + 1)
                if later(i):
                    act.wait_ge(pr_mm, i)
                nc.scalar.activation(oT[:, :, 0:T], A[:].rearrange("p (k t) -> p k t", t=P)[:, :, 0:T], ACT.Copy
                                     ).then_inc(oT_done, 1)

            def h2_out(i, odd):
                T = width(i)
                act.wait_ge(h2T_mm, i + 1)
                if not isinstance(i, int) or i > 1:
                    act.wait_ge(rt_mm, i - 1)
                nc.scalar.activation(h2T[:, odd, :, 0:T],
                                     B[:].rearrange("p (k t) -> p k t", t=P)[:, :, 0:T], ACT.Copy
                                     ).then_inc(h2T_done, 1)

            def norm(i, odd):
                T = width(i)
                act.wait_ge(x2_done, i + 1)
                nc.scalar.activation(sq[0:T], g.x2[0:T, i, :], ACT.Square, scale=D ** -0.5,
                                     accum_out=st[0:T, 0:1]).then_inc(ssq, 1)
                act.wait_ge(ssq, i + 1)
                nc.scalar.activation(st[0:T, 1:2], st[0:T, 0:1], ACT.Sqrt, bias=g.eps[0:T]).then_inc(rms, 1)

            tiles(act, ((0, o_out), (2, h2_out), (1, norm)))

        @block.vector
        def _(dve):
            step = Steps(dve, dve_step)
            step(nc.vector.memset(g.logits[:], 0.0))
            dve.wait_ge(pool_step, 2)
            step(nc.vector.tensor_scalar(rown[:], rown[:], P - 1, None, ALU.bitwise_and))
            step(nc.vector.tensor_scalar(rowf[:], rown[:], float(2 * TOK), None, ALU.add))
            step(nc.vector.tensor_copy(pad[:, :, 0], padt[:]))
            nc.vector.tensor_copy(pad[:, :, 1], rowf[:]).then_inc(pad_done, 1)
            dve.wait_ge(row_done, len(SPREADS))

            def logits(i, odd):
                T = width(i)
                dve.wait_ge(rt_mm, i + 1)
                nc.vector.tensor_tensor(g.logits[0:T, i, :], R[0:T, 0:NG + NE], bias[0:T], ALU.add
                                        ).then_inc(rt_done, 1)

            def body(i, odd):
                T, b = width(i), 1 if last(i) else 0
                dve.wait_ge(pr_mm, i + 1)
                step(nc.vector.tensor_tensor(g.x2[0:T, i, :], C[0:T], rows[0:T, 0, b, :], ALU.mult))
                dve.wait_ge(x_in, 16 * i + 16)
                nc.vector.tensor_tensor(g.x2[0:T, i, :], g.x2[0:T, i, :], xr[0:T], ALU.add).then_inc(x2_done, 1)
                dve.wait_ge(rms, i + 1)
                step(nc.vector.reciprocal(st[0:T, 2:3], st[0:T, 1:2]))
                if later(i):
                    dve.wait_ge(h2T_mm, i)
                    dve.wait_ge(st_h2, 16 * i)
                step(nc.vector.scalar_tensor_tensor(h2[0:T], g.x2[0:T, i, :], st[0:T, 2:3], rows[0:T, 1, b, :],
                                                    ALU.mult, ALU.mult))
                nc.vector.tensor_tensor(h2[0:T], h2[0:T], rows[0:T, 2, b, :], ALU.add).then_inc(h2_done, 1)

            tiles(dve, ((3, logits), (0, body)), step, 3)


def phase_r(nc, io, g):
    with ExitStack() as stack:
        m = Memory(nc, stack)
        gm = m.sb("r_gm", [P, NT])
        ex = m.sb("r_ex", [P, NT, NG])
        den = m.sb("r_den", [P, NT])
        pg = m.sb("r_pg", [P, NT])
        eq = m.sb("r_eq", [P, NT, EPG])
        sc = m.sb("r_sc", [P, NT])
        og = m.sb("r_og", [P, NT, NG])
        oe = [m.sb(f"r_oe{k}", [P, NT, EPG]) for k in range(2)]
        full = m.sb("r_full", [P, NT, NG, EPG])
        e_in = m.sb("r_e_in", [P, NT, EPG])
        v = [m.sb(f"r_v{k}", [P, NT]) for k in range(2)]
        pick = [m.sb(f"r_pick{k}", [P, NT, NE]) for k in range(2)]
        both = m.sb("r_both", [P, NT, NE])
        cum = m.sb("r_cum", [P, NT + 1, NE])
        rank = m.sb("r_rank", [P, NT, NE])
        tmp = m.sb("r_tmp", [P, NT, NE])
        rk = m.sb("r_rk", [P, NT])
        ei = m.sb("r_ei", [P, NT])
        dd = m.sb("r_dd", [P, NT])
        valid = m.sb("r_valid", [P, NT])
        count = m.sb("r_count", [P, NE])
        cmax = m.sb("r_cmax", [P, 1])
        i32 = m.sb("r_i32", [P, NE], I32)
        dest = m.sb("r_dest", [P, 2, NT], U32)
        idx = m.sb("r_idx", [P, NE])
        rev = m.sb("r_rev", [P, EPG])
        pair = m.sb("r_pair", [P, 2, NT, 2], U32)
        ranks = m.ps("r_ranks", [P, 512])
        counts = m.ps("r_counts", [P, 512])
        dve_step, pool_step, diff, expd, picked, ranked, placed, listed = m.sems(
            "r_dve_step r_pool_step r_diff r_expd r_picked r_ranked r_placed r_listed")
        block = stack.enter_context(nc.Block())

        @block.sync
        def _(sp):
            for e in range(2):
                load_gate_up(nc, io, g, sp, e, e, g.wgu_in[e])
                load_down(nc, io, g, sp, e, e, g.wd_in[e])

        def over(ap, n):
            return ap.unsqueeze(2).broadcast_to([P, NT, n])

        @block.gpsimd
        def _(pool):
            step = Steps(pool, pool_step)
            step(nc.gpsimd.iota(i32[:], pattern=[[1, NE]], base=0, channel_multiplier=0))
            for k in range(2):
                step(nc.gpsimd.iota(pair[:, k, :, 0], pattern=[[P, NT]], base=0, channel_multiplier=1))
                step(nc.gpsimd.iota(pair[:, k, :, 1], pattern=[[P, NT]], base=k * TOK, channel_multiplier=1))
            step(nc.gpsimd.memset(valid[:], 1.0))
            step(nc.gpsimd.memset(valid[:, PT:], 0.0))
            step(nc.gpsimd.memset(valid[0:DEC, PT:], 1.0))
            for k in range(2):
                pool.wait_ge(placed, k + 1)
                for i in range(NT):
                    T = P if i < PT else DEC
                    nc.gpsimd.indirect_dma_start(out=g.list_dram[:, :],
                                                 out_offset=bass.IndirectOffsetOnAxis(ap=dest[0:T, k, i:i + 1],
                                                                                      axis=0),
                                                 in_=pair[0:T, k, i, :], in_offset=None).then_inc(listed, 16)
            pool.wait_ge(listed, 2 * 16 * NT)

        @block.tensor
        def _(pe):
            pe.wait_ge(picked, 1)
            flat = lambda ap: ap.rearrange("p i e -> p (i e)")
            nc.tensor.matmul(ranks[:, 0:NT * NE], lhsT=g.tri[:], rhs=flat(both[:]), start=True, stop=False)
            nc.tensor.matmul(ranks[:, 0:NT * NE], lhsT=g.ones[:], rhs=flat(cum[:, 0:NT, :]), start=False, stop=True)
            nc.tensor.matmul(counts[:, 0:NE], lhsT=g.ones[:], rhs=cum[:, NT, :], start=True, stop=True
                             ).then_inc(ranked, 1)

        @block.scalar
        def _(act):
            act.wait_ge(diff, 1)
            nc.scalar.activation(ex[:], ex[:], ACT.Exp).then_inc(expd, 1)
            act.wait_ge(diff, 2)
            nc.scalar.activation(v[1][:], v[1][:], ACT.Exp).then_inc(expd, 1)

        @block.vector
        def _(dve):
            step = Steps(dve, dve_step)
            V = nc.vector
            dve.wait_ge(pool_step, 8)
            step(V.tensor_copy(idx[:], i32[:]))
            step(V.tensor_scalar(rev[:], idx[:, 0:EPG], -1.0, float(EPG), ALU.mult, ALU.add))
            lg = g.logits[:, :, 0:NG]
            le = g.logits[:, :, NG:].rearrange("p i (a e) -> p i a e", e=EPG)

            def first_max(out, values, top, n):
                r = rev[:, 0:n].unsqueeze(1).broadcast_to([P, NT, n])
                step(V.tensor_reduce(top, values, AX.X, ALU.max))
                step(V.tensor_tensor(eq[:, :, 0:n], values, over(top, n), ALU.is_equal))
                step(V.tensor_tensor(eq[:, :, 0:n], eq[:, :, 0:n], r, ALU.mult))
                step(V.tensor_reduce(sc[:], eq[:, :, 0:n], AX.X, ALU.max))
                step(V.tensor_tensor(out, eq[:, :, 0:n], over(sc[:], n), ALU.is_equal))

            first_max(og[:], lg, gm[:], NG)
            V.tensor_tensor(ex[:], lg, over(gm[:], NG), ALU.subtract).then_inc(diff, 1)
            step(V.tensor_tensor(full[:], le, og[:].unsqueeze(3).broadcast_to([P, NT, NG, EPG]), ALU.mult))
            step(V.tensor_reduce(e_in[:], full[:].rearrange("p i a e -> p i e a"), AX.X, ALU.add))
            first_max(oe[0][:], e_in[:], v[0][:], EPG)
            step(V.scalar_tensor_tensor(e_in[:].rearrange("p i e -> p (i e)"),
                                        oe[0][:].rearrange("p i e -> p (i e)"), 3.0 * NEG,
                                        e_in[:].rearrange("p i e -> p (i e)"), ALU.mult, ALU.add))
            first_max(oe[1][:], e_in[:], v[1][:], EPG)
            V.tensor_tensor(v[1][:], v[1][:], v[0][:], ALU.subtract).then_inc(diff, 1)
            dve.wait_ge(expd, 2)
            step(V.tensor_reduce(den[:], ex[:], AX.X, ALU.add))
            step(V.tensor_scalar(pg[:], v[1][:], 1.0, None, ALU.add))
            step(V.tensor_tensor(den[:], den[:], pg[:], ALU.mult))
            step(V.reciprocal(g.weight[:, 0, :], den[:]))
            step(V.tensor_tensor(g.weight[:, 1, :], g.weight[:, 0, :], v[1][:], ALU.mult))
            for k in range(2):
                p4 = pick[k][:].rearrange("p i (a e) -> p i a e", e=EPG)
                step(V.tensor_tensor(oe[k][:], oe[k][:], over(valid[:], EPG), ALU.mult))
                step(V.tensor_tensor(p4, og[:].unsqueeze(3).broadcast_to([P, NT, NG, EPG]),
                                     oe[k][:].unsqueeze(2).broadcast_to([P, NT, NG, EPG]), ALU.mult))
            step(V.memset(cum[:, 0, :], 0.0))
            step(V.tensor_tensor(both[:], pick[0][:], pick[1][:], ALU.add))
            for i in range(NT):
                end = V.tensor_tensor(cum[:, i + 1, :], cum[:, i, :], both[:, i, :], ALU.add)
                if i < NT - 1:
                    step(end)
            end.then_inc(picked, 1)
            dve.wait_ge(ranked, 1)
            step(V.tensor_copy(rank[:], ranks[:, 0:NT * NE].rearrange("p (i e) -> p i e", e=NE)))
            step(V.tensor_copy(count[:], counts[:, 0:NE]))
            step(V.tensor_copy(g.count[:], count[:]))
            step(V.tensor_reduce(cmax[:], count[:], AX.X, ALU.max))
            step(V.tensor_copy(g.longest[:], cmax[:]))
            for k in range(2):
                step(V.tensor_tensor(tmp[:], pick[k][:], rank[:], ALU.mult))
                step(V.tensor_reduce(rk[:], tmp[:], AX.X, ALU.add))
                step(V.tensor_tensor(tmp[:], pick[k][:], idx[:].unsqueeze(1).broadcast_to([P, NT, NE]), ALU.mult))
                step(V.tensor_reduce(ei[:], tmp[:], AX.X, ALU.add))
                step(V.scalar_tensor_tensor(dd[:], ei[:], float(REGION), rk[:], ALU.mult, ALU.add))
                V.tensor_copy(dest[:, k, :], dd[:]).then_inc(placed, 1)
                dve.wait_ge(placed, k + 1)


def load_gate_up(nc, io, g, engine, e, b, sem):
    engine.dma_start(g.w_gate[:, b], io["w_gate"][e].rearrange("(k p) n -> p k n", p=P)).then_inc(sem, 16)
    engine.dma_start(g.w_up[:, b], io["w_up"][e].rearrange("(k p) n -> p k n", p=P)).then_inc(sem, 16)


def load_down(nc, io, g, engine, e, b, sem):
    engine.dma_start(g.w_down[:, b], io["w_down"][e].rearrange("(k p) n -> p k n", p=P)).then_inc(sem, 16)


def phase_g(nc, io, g):
    with ExitStack() as stack:
        m = Memory(nc, stack)
        FT = DE // P
        TURN = 4
        wg, wu, wd = g.w_gate, g.w_up, g.w_down
        ix = [m.sb(f"g_ix{r}", [P, 2], U32) for r in range(TURN)]
        sl = [m.sb(f"g_sl{b}", [P, 2], U32) for b in range(2)]
        xg = m.sb("g_xg", [P, TURN, D])
        xT = m.sb("g_xT", [P, KD, P])
        sig = m.sb("g_sig", [P, FT, P])
        hid = m.sb("g_hid", [P, 2, FT, P])
        y = m.sb("g_y", [P, 2, D])
        X = m.ps("g_X", [P, D])
        GU = [m.ps(f"g_GU{b}", [P, 2 * FT, P]) for b in range(2)]
        Y = [m.ps(f"g_Y{b}", [P, D]) for b in range(2)]
        xT_mm, xT_done, gu_mm, sig_done, hid_done, dn_mm, y_done, st_y, dve_step, started = m.sems(
            "g_xT_mm g_xT_done g_gu_mm g_sig_done g_hid_done g_dn_mm g_y_done g_st_y g_dve_step g_started")
        sl_in = m.sems("g_sl0 g_sl1")
        wgu_in, wd_in = g.wgu_in, g.wd_in
        ix_in = m.sems("g_ix_in0 g_ix_in1 g_ix_in2 g_ix_in3")
        xg_in = m.sems("g_xg_in0 g_xg_in1 g_xg_in2 g_xg_in3")
        (l_free, l_w, l_ix, l_xg, l_xT_mm, l_xT, l_gu, l_sig, l_hid, l_dn, l_y, l_st, l_step) = m.sems(
            "l_free l_w l_ix l_xg l_xT_mm l_xT l_gu l_sig l_hid l_dn l_y l_st l_step")
        block = stack.enter_context(nc.Block())

        def experts(engine, parts, steps=None, per=0):
            def step(j, r):
                for lag, part in parts:
                    if r >= lag:
                        part(j * TURN + (r - lag), j, r - lag)
                    elif not (isinstance(j, int) and j == 0):
                        part(j * TURN + (r - lag), j - 1, r - lag + TURN)

            for r in range(TURN):
                step(0, r)
            if steps:
                steps.straight()
            with engine.Fori(1, NE // TURN) as j:
                if steps:
                    steps.enter(j - 1, per)
                for r in range(TURN):
                    step(j, r)
            if steps:
                steps.leave(NE // TURN - 1)
            for e in range(NE, NE + max(lag for lag, _ in parts)):
                for lag, part in parts:
                    if e - lag < NE:
                        part(e - lag, (e - lag) // TURN, (e - lag) % TURN)

        def later(e, than=0):
            return not isinstance(e, int) or e > than

        def use(j, r):
            return j * (TURN // 2) + r // 2

        def long_lists(engine, body):
            longest = engine.value_load(g.longest[0:1, 0:1], min_val=0, max_val=TOK)
            done = engine.alloc_register("done")
            engine.reg_mov(done, 0)
            with engine.If(longest > P):
                with engine.Fori(0, NE) as e:
                    count = engine.value_load(g.count[0:1, bass.ds(e, 1)], min_val=0, max_val=TOK)
                    with engine.Fori(1, REGION // P) as r:
                        with engine.If(count > r * P):
                            body(e, r * P, engine.snap(done))
                            engine.reg_add(done, done, 1)

        def scatter(pool, b, sem):
            nc.gpsimd.indirect_dma_start(out=g.y_dram[:, :], in_=y[:, b, :], in_offset=None,
                                         out_offset=bass.IndirectOffsetOnAxis(ap=sl[b][:, 1:2], axis=0)
                                         ).then_inc(sem, 16)

        def gather(pool, r, sem):
            nc.gpsimd.indirect_dma_start(out=xg[:, r, :], out_offset=None, in_=g.h2_dram[:, :],
                                         in_offset=bass.IndirectOffsetOnAxis(ap=ix[r][:, 0:1], axis=0)
                                         ).then_inc(sem, 16)

        def transposes(r):
            for k in range(KD):
                end = nc.tensor.transpose(X[:, k * P:(k + 1) * P], xg[:, r, k * P:(k + 1) * P], g.ident[:])
            return end

        def gate_up(b):
            for f in range(2 * FT):
                w = (wg, wu)[f // FT]
                for k in range(KD):
                    end = nc.tensor.matmul(GU[b][:, f, :], lhsT=w[:, b, k, (f % FT) * P:(f % FT + 1) * P],
                                           rhs=xT[:, k, :], start=k == 0, stop=k == KD - 1)
            return end

        def down(b):
            for c in range(2):
                for k in range(FT):
                    end = nc.tensor.matmul(Y[b][:, c * 512:(c + 1) * 512], lhsT=hid[:, b, k, :],
                                           rhs=wd[:, b, k, c * 512:(c + 1) * 512], start=k == 0, stop=k == FT - 1)
            return end

        @block.sync
        def _(sp):
            def list_in(e, j, r):
                if later(e, TURN - 1):
                    sp.wait_ge(xg_in[r], j * 16)
                sp.dma_start(ix[r][:], g.list_dram[bass.ds(e * REGION, P), :]).then_inc(ix_in[r], 16)

            def weights(e, j, r):
                if not later(e, 1):
                    return
                sp.wait_ge(gu_mm, e - 1)
                load_gate_up(nc, io, g, sp, e, r % 2, wgu_in[r % 2])
                sp.wait_ge(dn_mm, e - 1)
                load_down(nc, io, g, sp, e, r % 2, wd_in[r % 2])

            experts(sp, ((0, list_in), (2, weights)))
            sp.wait_ge(st_y, 16 * NE)
            sp.sem_inc(l_free, 1)

            def long_body(e, row, n):
                sp.wait_ge(l_free, n + 1)
                load_gate_up(nc, io, g, sp, e, 0, l_w)
                load_down(nc, io, g, sp, e, 0, l_w)
                sp.wait_ge(l_st, n * 16 + 16)
                sp.sem_inc(l_free, 1)

            long_lists(sp, long_body)

        @block.gpsimd
        def _(pool):
            def rows_in(e, j, r):
                pool.wait_ge(ix_in[r], j * 16 + 16)
                if later(e, TURN - 1):
                    pool.wait_ge(xT_mm, e - (TURN - 1))
                pool.sem_inc(started, 1)
                gather(pool, r, xg_in[r])

            def results_out(e, j, r):
                pool.wait_ge(sl_in[r % 2], use(j, r) * 16 + 16)
                pool.wait_ge(y_done, e + 1)
                if later(e):
                    pool.wait_ge(st_y, e * 16)
                pool.sem_inc(started, 1)
                scatter(pool, r % 2, st_y)

            experts(pool, ((0, rows_in), (3, results_out)))

            def long_body(e, row, n):
                pool.wait_ge(l_free, n + 1)
                pool.sem_inc(started, 1)
                nc.gpsimd.dma_start(ix[0][:], g.list_dram[bass.ds(e * REGION + row, P), :]).then_inc(l_ix, 16)
                nc.gpsimd.dma_start(sl[0][:], g.list_dram[bass.ds(e * REGION + row, P), :]).then_inc(l_ix, 16)
                pool.wait_ge(l_ix, n * 32 + 32)
                pool.sem_inc(started, 1)
                gather(pool, 0, l_xg)
                pool.wait_ge(l_y, n + 1)
                pool.sem_inc(started, 1)
                scatter(pool, 0, l_st)

            long_lists(pool, long_body)

        @block.tensor
        def _(pe):
            def rows_turned(e, j, r):
                pe.wait_ge(xg_in[r], j * 16 + 16)
                if later(e):
                    pe.wait_ge(xT_done, e)
                transposes(r).then_inc(xT_mm, 1)

            def first_products(e, j, r):
                pe.wait_ge(wgu_in[r % 2], use(j, r) * 32 + 32)
                pe.wait_ge(xT_done, e + 1)
                if later(e, 1):
                    pe.wait_ge(hid_done, e - 1)
                gate_up(r % 2).then_inc(gu_mm, 1)

            def second_products(e, j, r):
                pe.wait_ge(wd_in[r % 2], use(j, r) * 16 + 16)
                pe.wait_ge(hid_done, e + 1)
                if later(e, 1):
                    pe.wait_ge(y_done, e - 1)
                down(r % 2).then_inc(dn_mm, 1)

            experts(pe, ((1, first_products), (0, rows_turned), (2, second_products)))

            def long_body(e, row, n):
                pe.wait_ge(l_xg, n * 16 + 16)
                transposes(0).then_inc(l_xT_mm, 1)
                pe.wait_ge(l_xT, n + 1)
                pe.wait_ge(l_w, n * 48 + 48)
                gate_up(0).then_inc(l_gu, 1)
                pe.wait_ge(l_hid, n + 1)
                down(0).then_inc(l_dn, 1)

            long_lists(pe, long_body)

        @block.scalar
        def _(act):
            def squash(b):
                return nc.scalar.activation(sig[:], GU[b][:, 0:FT, :], ACT.Sigmoid)

            def out(b):
                return nc.scalar.activation(y[:, b, :], Y[b][:], ACT.Copy)

            def sigmoids(e, j, r):
                act.wait_ge(gu_mm, e + 1)
                if later(e):
                    act.wait_ge(hid_done, e)
                squash(r % 2).then_inc(sig_done, 1)

            def results(e, j, r):
                if later(e, 1):
                    act.wait_ge(st_y, (e - 1) * 16)
                act.dma_start(sl[r % 2][:], g.list_dram[bass.ds(e * REGION, P), :]).then_inc(sl_in[r % 2], 16)
                act.wait_ge(dn_mm, e + 1)
                out(r % 2).then_inc(y_done, 1)

            experts(act, ((0, sigmoids), (1, results)))

            def long_body(e, row, n):
                act.wait_ge(l_gu, n + 1)
                squash(0).then_inc(l_sig, 1)
                act.wait_ge(l_dn, n + 1)
                out(0).then_inc(l_y, 1)

            long_lists(act, long_body)

        @block.vector
        def _(dve):
            step = Steps(dve, dve_step)

            def rows_out():
                return nc.vector.tensor_copy(xT[:], X[:].rearrange("p (k t) -> p k t", t=P))

            def gated(b, mark):
                mark(nc.vector.tensor_tensor(sig[:], GU[b][:, 0:FT, :], sig[:], ALU.mult))
                return nc.vector.tensor_tensor(hid[:, b], GU[b][:, FT:, :], sig[:], ALU.mult)

            def rows_turned(e, j, r):
                dve.wait_ge(xT_mm, e + 1)
                if later(e):
                    dve.wait_ge(gu_mm, e)
                rows_out().then_inc(xT_done, 1)

            def products(e, j, r):
                dve.wait_ge(sig_done, e + 1)
                if later(e, 1):
                    dve.wait_ge(dn_mm, e - 1)
                gated(r % 2, step).then_inc(hid_done, 1)

            experts(dve, ((0, rows_turned), (1, products)), step, TURN)

            def long_body(e, row, n):
                dve.wait_ge(l_xT_mm, n + 1)
                rows_out().then_inc(l_xT, 1)
                dve.wait_ge(l_sig, n + 1)

                def mark(ins):
                    ins.then_inc(l_step, 1)
                    dve.wait_ge(l_step, n + 1)

                gated(0, mark).then_inc(l_hid, 1)

            long_lists(dve, long_body)


def phase_h(nc, io, g):
    with ExitStack() as stack:
        m = Memory(nc, stack)
        BUFS = 4
        y = [[m.sb(f"h_y{k}{b}", [P, D]) for b in range(BUFS)] for k in range(2)]
        out = m.sb("h_out", [P, BUFS, D])
        y_in = [m.sems(" ".join(f"h_y_in{k}{b}" for b in range(BUFS))) for k in range(2)]
        st = m.sems(" ".join(f"h_st{b}" for b in range(BUFS)))
        summed, first_done, dve_step = m.sems("h_summed h_first_done h_dve_step")
        block = stack.enter_context(nc.Block())
        TILES = [(i, i % BUFS, i // BUFS, P if i < PT else DEC) for i in range(NT)]

        @block.sync
        def _(sp):
            def load(i, b, n, T):
                if n:
                    sp.wait_ge(summed, i - BUFS + 1)
                for k in range(2):
                    sp.dma_start(y[k][b][0:T, :], g.y_dram[i * P + k * TOK:i * P + k * TOK + T, :]
                                 ).then_inc(y_in[k][b], 16)

            for tile in TILES:
                load(*tile)

        @block.scalar
        def _(act):
            def store(i, b, n, T):
                act.wait_ge(summed, i + 1)
                act.dma_start(io["y_p"][i * P:(i + 1) * P, :] if i < PT else io["y_s"], out[0:T, b]
                              ).then_inc(st[b], 16)

            for i, b, n, T in TILES:
                act.wait_ge(y_in[0][b], 16 * n + 16)
                if n:
                    act.wait_ge(st[b], 16 * n)
                nc.scalar.activation(out[0:T, b], y[0][b][0:T], ACT.Copy, scale=g.weight[0:T, 0, i:i + 1]
                                     ).then_inc(first_done, 1)
                if i >= 2:
                    store(*TILES[i - 2])
            store(*TILES[NT - 2])
            store(*TILES[NT - 1])
            for b in range(BUFS):
                act.wait_ge(st[b], 16 * len(range(b, NT, BUFS)))

        @block.vector
        def _(dve):
            step = Steps(dve, dve_step)
            for i, b, n, T in TILES:
                dve.wait_ge(first_done, i + 1)
                dve.wait_ge(y_in[1][b], 16 * n + 16)
                step(nc.vector.scalar_tensor_tensor(out[0:T, b], y[1][b][0:T], g.weight[0:T, 1, i:i + 1],
                                                    out[0:T, b], ALU.mult, ALU.add))
                step(nc.vector.tensor_tensor(out[0:T, b], out[0:T, b], g.gate_m[0:T, int(i == PT), :], ALU.mult))
                nc.vector.tensor_tensor(out[0:T, b], out[0:T, b], g.x2[0:T, i, :], ALU.add).then_inc(summed, 1)


class Shared:
    pass


INPUTS = ("x_prompt", "x_sample", "cache_sb_k", "cache_sb_v", "cache_mla_ckv", "cache_mla_kpe", "c_prompt",
          "c_sample", "w_ada", "b_ada", "g_mix", "w_in", "g_sb_q", "g_sb_k", "g_qa", "w_qb", "g_kva", "w_kvb",
          "g_mq_nope", "g_mk_nope", "g_mq_pe", "g_mk_pe", "w_out", "g_ffn", "w_rg", "b_rg", "w_re", "b_re",
          "w_gate", "w_up", "w_down")


def program(nc, io):
    USED.clear()
    g = Shared()
    with ExitStack() as stack:
        m = Memory(nc, stack)
        g.qs_dram = nc.dram_tensor("qs_dram", [SBH // 2, P, TOK], F32, kind="Internal").ap()
        g.ks_dram = nc.dram_tensor("ks_dram", [SBH // 2, P, TOK], F32, kind="Internal").ap()
        g.o_dram = nc.dram_tensor("o_dram", [TOK, D], F32, kind="Internal").ap()
        g.h2_dram = nc.dram_tensor("h2_dram", [TOK + 1, D], F32, kind="Internal").ap()
        g.list_dram = nc.dram_tensor("list_dram", [NE * REGION, 2], U32, kind="Internal").ap()
        g.y_dram = nc.dram_tensor("y_dram", [2 * TOK + P, D], F32, kind="Internal").ap()
        g.qm_dram = nc.dram_tensor("qm_dram", [MH, MK, TOK], F32, kind="Internal").ap()
        g.ident = m.sb("ident", [P, P])
        g.identb = m.sb("identb", [P, P], BF16)
        g.mask_sb = m.sb("mask_sb", [P, P], BF16)
        g.mask_mla = m.sb("mask_mla", [P, P], BF16)
        g.tri = m.sb("tri", [P, P])
        g.ones = m.sb("ones", [P, P])
        g.eps = m.sb("eps", [P, 1])
        g.rows = m.sb("rows", [P, ROWW])
        g.modT = m.sb("modT", [P, 48, 2])
        g.scale_a = m.sb("scale_a", [P, KD, 2])
        g.scale_m = m.sb("scale_m", [P, KD, 2])
        g.ckv_new = m.sb("ckv_new", [P, KR])
        g.w_in_loaded, g.w_small_loaded = m.sems("w_in_loaded w_small_loaded")
        with ExitStack() as keys:
            m = Memory(nc, keys)
            g.kT_m = m.sb("kT_m", [MK, MH, TOK])
            g.values = m.sb("values", [P, 2 * NT * SBW])
            g.v_sb = g.values[:, 0:NT * SBW].rearrange("p (i n) -> p i n", n=SBW)
            g.v_m = g.values[:, NT * SBW:].rearrange("p (i n) -> p i n", n=MH * MV)
            g.w_kvb = m.sb("w_kvb_sb", [P, KR // P, MH * (NOPE + MV)])
            with ExitStack() as weights:
                m = Memory(nc, weights)
                g.w_in = m.sb("w_in_sb", [P, KD, INC])
                g.w_qb = m.sb("w_qb_sb", [P, QR // P, MH * MK])
                g.rope = m.sb("rope_sb", [P, NT, 2 * ROPE])
                g.x = m.sb("x_sb", [P, D])
                g.x_in, = m.sems("x_in")
                phase_a(nc, io, g)
                phase_b(nc, io, g)
            phase_cd(nc, io, g)
            phase_e(nc, io, g)
        retire_semaphores(nc)
        m = Memory(nc, stack)
        g.x2 = m.sb("x2", [P, NT, D])
        g.gate_m = m.sb("gate_m", [P, 2, D])
        g.logits = m.sb("logits", [P, NT, NG + NE])
        g.weight = m.sb("weight", [P, 2, NT])
        g.count = m.sb("count", [P, NE], I32)
        g.longest = m.sb("longest", [P, 1], I32)
        phase_f(nc, io, g)
        g.w_gate = m.sb("w_gate_sb", [P, 2, KD, DE])
        g.w_up = m.sb("w_up_sb", [P, 2, KD, DE])
        g.w_down = m.sb("w_down_sb", [P, 2, DE // P, D])
        g.wgu_in = m.sems("wgu_in0 wgu_in1")
        g.wd_in = m.sems("wd_in0 wd_in1")
        phase_r(nc, io, g)
        phase_g(nc, io, g)
        phase_h(nc, io, g)


def rope_table():
    inv = np.float32(10000.0) ** (-np.arange(0, ROPE, 2, dtype=np.float32) / np.float32(ROPE))
    pos = np.zeros(NT * P, np.float32)
    pos[:SEQ] = np.arange(SEQ)
    pos[SEQ:TOK] = PAST + np.arange(DEC)
    ang = pos[:, None] * inv[None, :].astype(np.float32)
    c, s = np.cos(ang), np.sin(ang)
    t = np.concatenate([c, c, -s, s], axis=1).astype(np.float32)
    return np.ascontiguousarray(t.reshape(NT, P, 2 * ROPE).transpose(1, 0, 2))


def kernel(**inputs):
    import concourse.bacc as bacc
    from concourse.bass_utils import run_bass_kernel_spmd

    nc = bacc.Bacc("TRN2", target_bir_lowering=False, num_devices=1)
    shapes = {
        "x_prompt": (SEQ, D), "x_sample": (DEC, D), "cache_sb_k": (PAST, SBW), "cache_sb_v": (PAST, SBW),
        "cache_mla_ckv": (PAST, KR), "cache_mla_kpe": (PAST, ROPE), "c_prompt": (D,), "c_sample": (D,),
    }
    arrays, io = {}, {}
    for name in INPUTS:
        a = np.asarray(inputs[name])
        a = np.ascontiguousarray(a.reshape(shapes.get(name, a.shape[1:])))
        arrays[name] = a
        io[name] = nc.dram_tensor(name, a.shape, mybir.dt.from_np(a.dtype), kind="ExternalInput").ap()
    arrays["rope"] = rope_table()
    io["rope"] = nc.dram_tensor("rope", arrays["rope"].shape, F32, kind="ExternalInput").ap()
    outs = (("y_p", (SEQ, D), (1, SEQ, D)), ("y_s", (DEC, D), (1, DEC, D)),
            ("o_k_p", (SEQ, SBW), (1, 1, SEQ, SBH, SBD)), ("o_v_p", (SEQ, SBW), (1, 1, SEQ, SBH, SBD)),
            ("o_ckv_p", (SEQ, KR), (1, 1, SEQ, KR)), ("o_kpe_p", (SEQ, ROPE), (1, 1, SEQ, ROPE)),
            ("o_k_s", (DEC, SBW), (1, 1, DEC, SBH, SBD)), ("o_v_s", (DEC, SBW), (1, 1, DEC, SBH, SBD)),
            ("o_ckv_s", (DEC, KR), (1, 1, DEC, KR)), ("o_kpe_s", (DEC, ROPE), (1, 1, DEC, ROPE)))
    for name, shape, _ in outs:
        io[name] = nc.dram_tensor(name, shape, F32, kind="ExternalOutput").ap()
    program(nc, io)
    r = run_bass_kernel_spmd(nc, [arrays], core_ids=[0])
    return tuple(np.asarray(r.results[0][name]).reshape(shape) for name, _, shape in outs)
```
